# Optimizing a Trainium2 kernel written in Bass

```python
import math
import jax, jax.numpy as jnp
from jax import lax
import numpy as np

D_MODEL = 1024
BATCH = 1
SEQ = 512
DEPTH = 4

N_MIXERS = 3
EPS = 1e-6
N_POOL_LAYERS = (DEPTH + 2) // 3
N_GDN_LAYERS = (DEPTH + 1) // 3
N_MLA_LAYERS = DEPTH // 3

POOL_WIDTH = 2 * D_MODEL
POOL_WINDOWS = (2, 4, 8, 16)
POOL_GROUP = POOL_WIDTH // len(POOL_WINDOWS)

GDN_HEADS = 8
GDN_DK = 128
GDN_DV = 256
GDN_CONV = 4
GDN_CHUNK = 64
GDN_QK = GDN_HEADS * GDN_DK
GDN_V = GDN_HEADS * GDN_DV
GDN_CONV_CH = 2 * GDN_QK + GDN_V
GDN_IN = 2 * GDN_QK + 2 * GDN_V + 2 * GDN_HEADS

MLA_HEADS = 16
MLA_NOPE = 128
MLA_ROPE = 64
MLA_V = 128
MLA_Q_LORA = 768
MLA_KV_LORA = 512
MLA_QK = MLA_NOPE + MLA_ROPE
MLA_WIDTH = MLA_HEADS * MLA_V
MLA_IN = MLA_Q_LORA + MLA_KV_LORA + MLA_ROPE + MLA_WIDTH
ROPE_THETA = 10000.0
Q_BLOCK = 128


def rmsnorm(x, g):
    xf = x.astype(jnp.float32)
    y = xf * lax.rsqrt(jnp.mean(xf * xf, axis=-1, keepdims=True) + EPS)
    return (y * g.astype(jnp.float32)).astype(x.dtype)

def l2norm(x):
    return x * lax.rsqrt(jnp.sum(x * x, axis=-1, keepdims=True) + EPS)

def pool_mixer(h, w_in, w_grp, scale, w_out):
    B, S, _ = h.shape
    u, gate = jnp.split(h @ w_in, 2, axis=-1)
    c = jnp.pad(jnp.cumsum(u.astype(jnp.float32), axis=1), ((0, 0), (1, 0), (0, 0)))
    t = jnp.arange(S)
    groups = []
    for gi, w in enumerate(POOL_WINDOWS):
        sl = slice(gi * POOL_GROUP, (gi + 1) * POOL_GROUP)
        cg = c[:, :, sl]
        lo = jnp.pad(cg[:, :S - w + 1], ((0, 0), (w - 1, 0), (0, 0)))
        cnt = jnp.minimum(t + 1, w).astype(jnp.float32)[None, :, None]
        mean = (cg[:, 1:] - lo) / cnt
        groups.append(mean.astype(u.dtype) - u[..., sl])
    p = jnp.stack(groups, axis=2)
    p = jnp.einsum('bsgi,gio->bsgo', p, w_grp).reshape(B, S, POOL_WIDTH)
    y = p * scale * jax.nn.silu(gate)
    return y @ w_out

def causal_depthwise_conv(u, w):
    K, C = w.shape
    return lax.conv_general_dilated(u, w[:, None, :], window_strides=(1,),
                                    padding=[(K - 1, 0)],
                                    dimension_numbers=('NWC', 'WIO', 'NWC'),
                                    feature_group_count=C)

def chunk_gated_delta_rule(q, k, v, g, beta):
    B, S, H, dk = q.shape
    dv = v.shape[-1]
    C = GDN_CHUNK
    N = S // C

    def to_chunks(a):
        return a.reshape(B, N, C, H, -1).transpose(0, 3, 1, 2, 4)

    q, k, v = to_chunks(q), to_chunks(k), to_chunks(v)
    beta = beta.reshape(B, N, C, H).transpose(0, 3, 1, 2)
    g = jnp.cumsum(g.reshape(B, N, C, H).transpose(0, 3, 1, 2), axis=-1)
    k_beta = k * beta[..., None]
    v_beta = v * beta[..., None]
    causal = jnp.tril(jnp.ones((C, C), dtype=bool))
    strict = jnp.tril(jnp.ones((C, C), dtype=bool), -1)
    diff = g[..., :, None] - g[..., None, :]
    decay = jnp.exp(jnp.where(causal, diff, -jnp.inf))
    L = jnp.where(strict, jnp.einsum('bhnid,bhnjd->bhnij', k_beta, k) * decay, 0.0)
    A = jnp.eye(C, dtype=L.dtype) + L
    rhs = jnp.concatenate([v_beta, k_beta * jnp.exp(g)[..., None]], axis=-1)
    sol = lax.linalg.triangular_solve(A, rhs, left_side=True, lower=True)
    u_ps = sol[..., :dv]
    w_cd = sol[..., dv:]
    attn = jnp.where(causal, jnp.einsum('bhnid,bhnjd->bhnij', q, k) * decay, 0.0)

    def step(state, xs):
        q_c, k_c, u_c, w_c, g_c, a_c = xs
        v_new = u_c - jnp.einsum('bhck,bhkv->bhcv', w_c, state)
        o = (jnp.einsum('bhck,bhkv->bhcv', q_c * jnp.exp(g_c)[..., None], state)
             + jnp.einsum('bhij,bhjv->bhiv', a_c, v_new))
        g_last = g_c[..., -1]
        k_dec = k_c * jnp.exp(g_last[..., None] - g_c)[..., None]
        state = state * jnp.exp(g_last)[..., None, None] + jnp.einsum('bhck,bhcv->bhkv', k_dec, v_new)
        return state, o

    mv = lambda a: jnp.moveaxis(a, 2, 0)
    xs = (mv(q), mv(k), mv(u_ps), mv(w_cd), mv(g), mv(attn))
    state0 = jnp.zeros((B, H, dk, dv), jnp.float32)
    _, o = lax.scan(step, state0, xs)
    return o.transpose(1, 0, 3, 2, 4).reshape(B, S, H, dv)

def gdn_mixer(h, w_in, conv_w, a_log, dt_bias, norm_g, w_out):
    B, S, _ = h.shape
    f32 = jnp.float32
    proj = h @ w_in
    qkv, gate, b_raw, a_raw = jnp.split(
        proj, [GDN_CONV_CH, GDN_CONV_CH + GDN_V, GDN_CONV_CH + GDN_V + GDN_HEADS], axis=-1)
    qkv = jax.nn.silu(causal_depthwise_conv(qkv, conv_w))
    q, k, v = jnp.split(qkv, [GDN_QK, 2 * GDN_QK], axis=-1)
    q = l2norm(q.reshape(B, S, GDN_HEADS, GDN_DK).astype(f32)) * (GDN_DK ** -0.5)
    k = l2norm(k.reshape(B, S, GDN_HEADS, GDN_DK).astype(f32))
    v = v.reshape(B, S, GDN_HEADS, GDN_DV).astype(f32)
    beta = jax.nn.sigmoid(b_raw.astype(f32))
    g = -jnp.exp(a_log.astype(f32)) * jax.nn.softplus(a_raw.astype(f32) + dt_bias.astype(f32))
    o = chunk_gated_delta_rule(q, k, v, g, beta)
    o = rmsnorm(o, norm_g) * jax.nn.silu(gate.reshape(B, S, GDN_HEADS, GDN_DV).astype(f32))
    return o.reshape(B, S, GDN_V).astype(h.dtype) @ w_out

def rope(x, pos):
    half = x.shape[-1] // 2
    inv = ROPE_THETA ** (-jnp.arange(half, dtype=jnp.float32) / half)
    ang = pos.astype(jnp.float32)[..., None, None] * inv
    cos, sin = jnp.cos(ang), jnp.sin(ang)
    x1, x2 = x[..., :half], x[..., half:]
    return jnp.concatenate([x1 * cos - x2 * sin, x1 * sin + x2 * cos], axis=-1).astype(x.dtype)

def causal_block_attention(q, k, v):
    B, S, H, Dq = q.shape
    nb = S // Q_BLOCK
    scale = Dq ** -0.5
    qb = q.reshape(B, nb, Q_BLOCK, H, Dq).transpose(1, 0, 2, 3, 4)
    kpos = jnp.arange(S)

    def block(args):
        i, q_blk = args
        s = jnp.einsum('bqhd,bkhd->bhqk', q_blk, k).astype(jnp.float32) * scale
        qpos = i * Q_BLOCK + jnp.arange(Q_BLOCK)
        s = jnp.where(kpos[None, :] <= qpos[:, None], s, -jnp.inf)
        p = jax.nn.softmax(s, axis=-1)
        return jnp.einsum('bhqk,bkhd->bqhd', p.astype(v.dtype), v)

    o = lax.map(block, (jnp.arange(nb), qb))
    return o.transpose(1, 0, 2, 3, 4).reshape(B, S, H, v.shape[-1])

def mla_mixer(h, pos, w_in, q_norm_g, w_uq, kv_norm_g, w_ukv, w_out):
    B, S, _ = h.shape
    proj = h @ w_in
    cq, ckv, k_rope, gate = jnp.split(
        proj, [MLA_Q_LORA, MLA_Q_LORA + MLA_KV_LORA, MLA_Q_LORA + MLA_KV_LORA + MLA_ROPE], axis=-1)
    q = (rmsnorm(cq, q_norm_g) @ w_uq).reshape(B, S, MLA_HEADS, MLA_QK)
    kv = (rmsnorm(ckv, kv_norm_g) @ w_ukv).reshape(B, S, MLA_HEADS, MLA_NOPE + MLA_V)
    q_nope, q_rope = q[..., :MLA_NOPE], q[..., MLA_NOPE:]
    k_nope, v = kv[..., :MLA_NOPE], kv[..., MLA_NOPE:]
    q_rope = rope(q_rope, pos)
    k_rope = rope(k_rope[:, :, None, :], pos)
    q = jnp.concatenate([q_nope, q_rope], axis=-1)
    k = jnp.concatenate([k_nope, jnp.broadcast_to(k_rope, (B, S, MLA_HEADS, MLA_ROPE))], axis=-1)
    o = causal_block_attention(q, k, v).reshape(B, S, MLA_WIDTH)
    return (o * jax.nn.silu(gate)) @ w_out

def first_inputs(seed: int = 0) -> dict:
    key = jax.random.key(seed)
    ks = jax.random.split(key, 24)
    nrm = lambda k, shape, fan: jax.random.normal(k, shape, jnp.float32) * (fan ** -0.5)
    gain = lambda k, shape: 1.0 + 0.02 * jax.random.normal(k, shape, jnp.float32)
    nA, nB, nC = N_POOL_LAYERS, N_GDN_LAYERS, N_MLA_LAYERS
    x = jax.random.normal(ks[0], (BATCH, SEQ, D_MODEL), jnp.float32)
    positions = jnp.broadcast_to(jnp.arange(SEQ, dtype=jnp.int32)[None, :], (BATCH, SEQ))
    dt = jnp.exp(jax.random.uniform(ks[10], (nB, GDN_HEADS), jnp.float32,
                                    math.log(1e-3), math.log(1e-1)))
    return {
        "x": x,
        "positions": positions,
        "norm_g": gain(ks[1], (DEPTH, D_MODEL)),
        "pool_w_in": nrm(ks[2], (nA, D_MODEL, 2 * POOL_WIDTH), D_MODEL),
        "pool_w_grp": nrm(ks[3], (nA, len(POOL_WINDOWS), POOL_GROUP, POOL_GROUP), POOL_GROUP),
        "pool_scale": gain(ks[4], (nA, POOL_WIDTH)),
        "pool_w_out": nrm(ks[5], (nA, POOL_WIDTH, D_MODEL), POOL_WIDTH),
        "gdn_w_in": nrm(ks[6], (nB, D_MODEL, GDN_IN), D_MODEL),
        "gdn_conv": nrm(ks[7], (nB, GDN_CONV, GDN_CONV_CH), GDN_CONV),
        "gdn_a_log": jnp.log(jax.random.uniform(ks[8], (nB, GDN_HEADS), jnp.float32, 1.0, 16.0)),
        "gdn_dt_bias": dt + jnp.log(-jnp.expm1(-dt)),
        "gdn_norm_g": gain(ks[9], (nB, GDN_DV)),
        "gdn_w_out": nrm(ks[11], (nB, GDN_V, D_MODEL), GDN_V),
        "mla_w_in": nrm(ks[12], (nC, D_MODEL, MLA_IN), D_MODEL),
        "mla_q_norm_g": gain(ks[13], (nC, MLA_Q_LORA)),
        "mla_w_uq": nrm(ks[14], (nC, MLA_Q_LORA, MLA_HEADS * MLA_QK), MLA_Q_LORA),
        "mla_kv_norm_g": gain(ks[15], (nC, MLA_KV_LORA)),
        "mla_w_ukv": nrm(ks[16], (nC, MLA_KV_LORA, MLA_HEADS * (MLA_NOPE + MLA_V)), MLA_KV_LORA),
        "mla_w_out": nrm(ks[17], (nC, MLA_WIDTH, D_MODEL), MLA_WIDTH),
        "final_g": gain(ks[18], (D_MODEL,)),
    }

def first_block(x, positions, norm_g, pool_w_in, pool_w_grp, pool_scale, pool_w_out,
              gdn_w_in, gdn_conv, gdn_a_log, gdn_dt_bias, gdn_norm_g, gdn_w_out,
              mla_w_in, mla_q_norm_g, mla_w_uq, mla_kv_norm_g, mla_w_ukv, mla_w_out,
              final_g):
    for i in range(DEPTH):
        kind, j = i % N_MIXERS, i // N_MIXERS
        h = rmsnorm(x, norm_g[i])
        if kind == 0:
            y = pool_mixer(h, pool_w_in[j], pool_w_grp[j], pool_scale[j], pool_w_out[j])
        elif kind == 1:
            y = gdn_mixer(h, gdn_w_in[j], gdn_conv[j], gdn_a_log[j], gdn_dt_bias[j],
                          gdn_norm_g[j], gdn_w_out[j])
        else:
            y = mla_mixer(h, positions, mla_w_in[j], mla_q_norm_g[j], mla_w_uq[j],
                          mla_kv_norm_g[j], mla_w_ukv[j], mla_w_out[j])
        x = x + y.astype(x.dtype)
    return rmsnorm(x, final_g)


DEPTH_2 = 2

CHUNK = 64
QBLOCK = 128
MAX_STREAM_OFFSET = 4096

D_SSD = D_MODEL
SSD_HEADDIM = 64
SSD_HEADS = D_SSD // SSD_HEADDIM
SSD_GROUPS = 4
D_STATE = 128
SSD_CONV = 4
SSD_CHUNK = CHUNK

D_CONV = D_MODEL
CONF_KERNEL = 31

DIFF_HEADS = 8
DIFF_DK = 64
DIFF_DV = 2 * DIFF_DK
D_ATTN = DIFF_HEADS * DIFF_DV
ROT_DIM = DIFF_DK // 4
ROPE_THETA_2 = 500000.0

LN_EPS = 1e-5

N_EVEN = (DEPTH_2 + 1) // 2
N_ODD = DEPTH_2 // 2

XBC_DIM = D_SSD + 2 * SSD_GROUPS * D_STATE
EVEN_SPLITS = [D_SSD, XBC_DIM, SSD_HEADS, D_CONV, D_CONV, D_CONV]
EVEN_IN = sum(EVEN_SPLITS)
EVEN_MIX = D_SSD + D_CONV
ODD_IN = 4 * D_ATTN


def rmsnorm_2(x, w, eps=EPS):
    xf = x.astype(jnp.float32)
    y = xf * lax.rsqrt(jnp.mean(xf * xf, axis=-1, keepdims=True) + eps)
    return (y * w.astype(jnp.float32)).astype(x.dtype)

def layernorm(x, w, b, eps=LN_EPS):
    xf = x.astype(jnp.float32)
    mu = jnp.mean(xf, axis=-1, keepdims=True)
    var = jnp.mean(jnp.square(xf - mu), axis=-1, keepdims=True)
    y = (xf - mu) * lax.rsqrt(var + eps)
    return (y * w.astype(jnp.float32) + b.astype(jnp.float32)).astype(x.dtype)

def causal_dwconv(x, w, b):
    k = w.shape[0]
    out = lax.conv_general_dilated(
        x, w[:, None, :].astype(x.dtype), window_strides=(1,), padding=[(k - 1, 0)],
        dimension_numbers=("NWC", "WIO", "NWC"), feature_group_count=x.shape[-1])
    return out + b.astype(x.dtype)

def ssd_chunked(x, dt, a, bm, cm, d_skip):
    bsz, s, h, p = x.shape
    g, n = bm.shape[2], bm.shape[3]
    e = h // g
    l = SSD_CHUNK
    nc = s // l
    xd = (x * dt[..., None]).reshape(bsz, nc, l, g, e, p)
    da = (dt * a).reshape(bsz, nc, l, g, e).transpose(0, 3, 4, 1, 2)
    cs = jnp.cumsum(da, axis=-1)
    bm = bm.reshape(bsz, nc, l, g, n)
    cm = cm.reshape(bsz, nc, l, g, n)
    tril = jnp.tril(jnp.ones((l, l), dtype=bool))
    seg = cs[..., :, None] - cs[..., None, :]
    decay = jnp.exp(jnp.where(tril, seg, -jnp.inf))
    cb = jnp.einsum("bclgn,bcsgn->bcgls", cm, bm)
    y_diag = jnp.einsum("bcgls,bgecls,bcsgep->bclgep", cb, decay, xd)
    decay_states = jnp.exp(cs[..., -1:] - cs)
    states = jnp.einsum("bclgn,bgecl,bclgep->bcgepn", bm, decay_states, xd)
    chunk_decay = jnp.exp(cs[..., -1])

    def step(hstate, inp):
        st, dec = inp
        return hstate * dec[..., None, None] + st, hstate

    h0 = jnp.zeros((bsz, g, e, p, n), jnp.float32)
    _, prev = lax.scan(step, h0, (jnp.moveaxis(states, 1, 0), jnp.moveaxis(chunk_decay, -1, 0)))
    prev = jnp.moveaxis(prev, 0, 1)
    y_off = jnp.einsum("bclgn,bcgepn,bgecl->bclgep", cm, prev, jnp.exp(cs))
    y = (y_diag + y_off).reshape(bsz, s, h, p)
    return y + x * d_skip[:, None]

def partial_rotary(t, pos):
    half = ROT_DIM // 2
    inv = ROPE_THETA_2 ** (-2.0 * jnp.arange(half, dtype=jnp.float32) / ROT_DIM)
    ang = pos.astype(jnp.float32)[..., None] * inv
    cos = jnp.cos(ang)[:, :, None, None, :]
    sin = jnp.sin(ang)[:, :, None, None, :]
    tf = t.astype(jnp.float32)
    t1, t2 = tf[..., :half], tf[..., half:ROT_DIM]
    out = jnp.concatenate([t1 * cos - t2 * sin, t2 * cos + t1 * sin, tf[..., ROT_DIM:]], axis=-1)
    return out.astype(t.dtype)

def diff_attention(q, k, v, lam):
    bsz, s, h, _, dk = q.shape
    nb = s // QBLOCK
    qb = q.reshape(bsz, nb, QBLOCK, h, 2, dk).swapaxes(0, 1)
    kf = k.astype(jnp.float32)
    key_chunk = jnp.arange(s) // CHUNK
    scale = dk ** -0.5

    def one_block(args):
        qblk, bi = args
        sc = jnp.einsum("bqhmd,bkhmd->bhmqk", qblk.astype(jnp.float32), kf) * scale
        q_chunk = (bi * QBLOCK + jnp.arange(QBLOCK)) // CHUNK
        allowed = key_chunk[None, :] <= q_chunk[:, None]
        sc = jnp.where(allowed, sc, -jnp.inf)
        pr = jax.nn.softmax(sc, axis=-1)
        wts = pr[:, :, 0] - lam * pr[:, :, 1]
        return jnp.einsum("bhqk,bkhe->bqhe", wts.astype(v.dtype), v)

    o = lax.map(one_block, (qb, jnp.arange(nb)))
    return o.swapaxes(0, 1).reshape(bsz, s, h, v.shape[-1])

def even_layer(x, norm_w, w_in, conv_w, conv_b, dt_bias, a_log, d_skip, ssd_norm_w,
               dw_w, dw_b, ln_w, ln_b, w_out):
    bsz, s, _ = x.shape
    hn = rmsnorm_2(x, norm_w)
    proj = hn @ w_in
    idx = list(np.cumsum(EVEN_SPLITS)[:-1])
    z_a, xbc, dt_raw, glu_v, glu_g, z_b = jnp.split(proj, idx, axis=-1)
    xbc = jax.nn.silu(causal_dwconv(xbc, conv_w, conv_b))
    xs, bs, cs = jnp.split(xbc, [D_SSD, D_SSD + SSD_GROUPS * D_STATE], axis=-1)
    xs = xs.reshape(bsz, s, SSD_HEADS, SSD_HEADDIM).astype(jnp.float32)
    bs = bs.reshape(bsz, s, SSD_GROUPS, D_STATE).astype(jnp.float32)
    cs = cs.reshape(bsz, s, SSD_GROUPS, D_STATE).astype(jnp.float32)
    dt = jax.nn.softplus(dt_raw.astype(jnp.float32) + dt_bias.astype(jnp.float32))
    a = -jnp.exp(a_log.astype(jnp.float32))
    y = ssd_chunked(xs, dt, a, bs, cs, d_skip.astype(jnp.float32)).reshape(bsz, s, D_SSD)
    y = y * jax.nn.silu(z_a.astype(jnp.float32))
    y_a = rmsnorm_2(y.reshape(bsz, s, SSD_GROUPS, D_SSD // SSD_GROUPS),
                  ssd_norm_w.reshape(SSD_GROUPS, D_SSD // SSD_GROUPS)).reshape(bsz, s, D_SSD)
    y_a = y_a.astype(x.dtype)
    u = glu_v * jax.nn.sigmoid(glu_g)
    u = causal_dwconv(u, dw_w, dw_b)
    u = jax.nn.silu(layernorm(u, ln_w, ln_b))
    y_b = (u * jax.nn.silu(z_b)).astype(x.dtype)
    return x + jnp.concatenate([y_a, y_b], axis=-1) @ w_out

def odd_layer(x, positions, layer_idx, norm_w, w_in, q_norm_w, k_norm_w,
              lq1, lk1, lq2, lk2, subln_w, w_out):
    bsz, s, _ = x.shape
    lam_init = 0.8 - 0.6 * math.exp(-0.3 * layer_idx)
    hn = rmsnorm_2(x, norm_w)
    proj = hn @ w_in
    q, k, v, gate = jnp.split(proj, 4, axis=-1)
    q = rmsnorm_2(q.reshape(bsz, s, DIFF_HEADS, 2, DIFF_DK), q_norm_w)
    k = rmsnorm_2(k.reshape(bsz, s, DIFF_HEADS, 2, DIFF_DK), k_norm_w)
    q = partial_rotary(q, positions)
    k = partial_rotary(k, positions)
    v = v.reshape(bsz, s, DIFF_HEADS, DIFF_DV)
    f32 = jnp.float32
    lam = (jnp.exp(jnp.sum(lq1.astype(f32) * lk1.astype(f32)))
           - jnp.exp(jnp.sum(lq2.astype(f32) * lk2.astype(f32))) + lam_init)
    o = diff_attention(q, k, v, lam)
    o = rmsnorm_2(o, subln_w) * (1.0 - lam_init)
    o = o.reshape(bsz, s, D_ATTN) * jax.nn.silu(gate)
    return x + o.astype(x.dtype) @ w_out

def second_inputs(seed: int = 0) -> dict:
    key = jax.random.key(seed)
    ks = iter(jax.random.split(key, 40))

    def nrm(shape, scale):
        return jax.random.normal(next(ks), shape, jnp.float32) * scale

    x = nrm((BATCH, SEQ, D_MODEL), 1.0)
    offset = jax.random.randint(next(ks), (BATCH, 1), 0, MAX_STREAM_OFFSET, dtype=jnp.int32)
    positions = (offset + jnp.arange(SEQ, dtype=jnp.int32)[None, :]).astype(jnp.int32)

    ne, no = N_EVEN, N_ODD
    u = jax.random.uniform(next(ks), (ne, SSD_HEADS), jnp.float32)
    dt0 = jnp.exp(u * (math.log(0.1) - math.log(0.001)) + math.log(0.001))
    a_dt_bias = dt0 + jnp.log(-jnp.expm1(-dt0))
    a_a_log = jnp.log(jax.random.uniform(next(ks), (ne, SSD_HEADS), jnp.float32, 1.0, 16.0))
    return {
        "x": x,
        "positions": positions,
        "a_norm_w": 1.0 + nrm((ne, D_MODEL), 0.05),
        "a_w_in": nrm((ne, D_MODEL, EVEN_IN), D_MODEL ** -0.5),
        "a_conv_w": nrm((ne, SSD_CONV, XBC_DIM), SSD_CONV ** -0.5),
        "a_conv_b": nrm((ne, XBC_DIM), 0.02),
        "a_dt_bias": a_dt_bias,
        "a_a_log": a_a_log,
        "a_d_skip": 1.0 + nrm((ne, SSD_HEADS), 0.05),
        "a_ssd_norm_w": 1.0 + nrm((ne, D_SSD), 0.05),
        "a_dw_w": nrm((ne, CONF_KERNEL, D_CONV), CONF_KERNEL ** -0.5),
        "a_dw_b": nrm((ne, D_CONV), 0.02),
        "a_ln_w": 1.0 + nrm((ne, D_CONV), 0.05),
        "a_ln_b": nrm((ne, D_CONV), 0.02),
        "a_w_out": nrm((ne, EVEN_MIX, D_MODEL), EVEN_MIX ** -0.5),
        "c_norm_w": 1.0 + nrm((no, D_MODEL), 0.05),
        "c_w_in": nrm((no, D_MODEL, ODD_IN), D_MODEL ** -0.5),
        "c_q_norm_w": 1.0 + nrm((no, DIFF_DK), 0.05),
        "c_k_norm_w": 1.0 + nrm((no, DIFF_DK), 0.05),
        "c_lq1": nrm((no, DIFF_DK), 0.1),
        "c_lk1": nrm((no, DIFF_DK), 0.1),
        "c_lq2": nrm((no, DIFF_DK), 0.1),
        "c_lk2": nrm((no, DIFF_DK), 0.1),
        "c_subln_w": 1.0 + nrm((no, DIFF_DV), 0.05),
        "c_w_out": nrm((no, D_ATTN, D_MODEL), D_ATTN ** -0.5),
    }

def second_block(x, positions, a_norm_w, a_w_in, a_conv_w, a_conv_b, a_dt_bias, a_a_log,
              a_d_skip, a_ssd_norm_w, a_dw_w, a_dw_b, a_ln_w, a_ln_b, a_w_out,
              c_norm_w, c_w_in, c_q_norm_w, c_k_norm_w, c_lq1, c_lk1, c_lq2, c_lk2,
              c_subln_w, c_w_out):
    for i in range(DEPTH_2):
        if i % 2 == 0:
            j = i // 2
            x = even_layer(x, a_norm_w[j], a_w_in[j], a_conv_w[j], a_conv_b[j], a_dt_bias[j],
                           a_a_log[j], a_d_skip[j], a_ssd_norm_w[j], a_dw_w[j], a_dw_b[j],
                           a_ln_w[j], a_ln_b[j], a_w_out[j])
        else:
            j = i // 2
            x = odd_layer(x, positions, i, c_norm_w[j], c_w_in[j], c_q_norm_w[j], c_k_norm_w[j],
                          c_lq1[j], c_lk1[j], c_lq2[j], c_lk2[j], c_subln_w[j], c_w_out[j])
    return x


def setup_inputs(seed=0):
    out = dict(first_inputs(seed))
    for name, value in second_inputs(seed + 1).items():
        if name != "x":
            out[name + "_2"] = value
    return out


def reference(
    x, positions, norm_g, pool_w_in, pool_w_grp, pool_scale, pool_w_out, gdn_w_in, gdn_conv,
    gdn_a_log, gdn_dt_bias, gdn_norm_g, gdn_w_out, mla_w_in, mla_q_norm_g, mla_w_uq,
    mla_kv_norm_g, mla_w_ukv, mla_w_out, final_g, positions_2, a_norm_w_2, a_w_in_2, a_conv_w_2,
    a_conv_b_2, a_dt_bias_2, a_a_log_2, a_d_skip_2, a_ssd_norm_w_2, a_dw_w_2, a_dw_b_2,
    a_ln_w_2, a_ln_b_2, a_w_out_2, c_norm_w_2, c_w_in_2, c_q_norm_w_2, c_k_norm_w_2, c_lq1_2,
    c_lk1_2, c_lq2_2, c_lk2_2, c_subln_w_2, c_w_out_2,
):
    x = first_block(
        x, positions, norm_g, pool_w_in, pool_w_grp, pool_scale, pool_w_out, gdn_w_in, gdn_conv,
        gdn_a_log, gdn_dt_bias, gdn_norm_g, gdn_w_out, mla_w_in, mla_q_norm_g, mla_w_uq,
        mla_kv_norm_g, mla_w_ukv, mla_w_out, final_g,
    )
    return second_block(
        x, positions_2, a_norm_w_2, a_w_in_2, a_conv_w_2, a_conv_b_2, a_dt_bias_2, a_a_log_2,
        a_d_skip_2, a_ssd_norm_w_2, a_dw_w_2, a_dw_b_2, a_ln_w_2, a_ln_b_2, a_w_out_2,
        c_norm_w_2, c_w_in_2, c_q_norm_w_2, c_k_norm_w_2, c_lq1_2, c_lk1_2, c_lq2_2, c_lk2_2,
        c_subln_w_2, c_w_out_2,
    )


_drawn_inputs = setup_inputs


def setup_inputs(seed=0):
    import zlib

    import numpy as np

    out = dict(_drawn_inputs(seed))
    spreads = {}
    factors = {'pool_scale': 3.197,
     'gdn_norm_g': 4.18,
     'mla_q_norm_g': 8.0,
     'mla_kv_norm_g': 8.0,
     'a_conv_b_2': 2.768,
     'a_d_skip_2': 2.899,
     'a_dw_b_2': 5.383,
     'a_ln_w_2': 4.267,
     'a_ln_b_2': 8.0,
     'c_q_norm_w_2': 5.064,
     'c_k_norm_w_2': 4.475,
     'c_lq1_2': 4.045,
     'c_lk1_2': 7.879,
     'c_lk2_2': 8.0,
     'c_subln_w_2': 3.91}
    for name, (base, spread) in spreads.items():
        noise = np.random.default_rng([zlib.crc32(name.encode()), seed]).standard_normal(out[name].shape)
        drawn = base * np.exp(spread * noise) if base else spread * noise
        out[name] = __import__('jax').numpy.asarray(drawn.astype(out[name].dtype))
    for name, factor in factors.items():
        out[name] = (out[name] * factor).astype(out[name].dtype)
    return out
```

```python
import math
from contextlib import ExitStack

import numpy as np

SEQ, D = 512, 1024
P = 128
KD = D // P
EPS = 1e-6
RING = 4
BANKS = 4
SLOT = 1024
WINDOWS = (2, 4, 8, 16)
PAD = max(WINDOWS)
NCH = SEQ // P
NEG = -3.0e37
ROUND = 1.5 * 2.0 ** 23
TWO_PI = (6.28125, 0.0019350051879882812, 3.0199159795074593e-07)
PI_BELOW = 3.1415925


def ring_positions(n):
    short = {1: [3], 2: [2, 3], 5: [0, 1, 2, 3, 1]}
    if n in short:
        return short[n]
    threes = (-n) % 4
    return (n - 3 * threes) // 4 * [0, 1, 2, 3] + threes * [0, 1, 2]


class Stream:

    def __init__(self, sections):
        self.sec = {}
        slots, banks, tiles, first = [0] * RING, [0] * BANKS, 0, 0
        for name, iters, items in sections:
            s = {"iters": iters, "items": items, "slots0": list(slots), "first": first,
                 "banks0": list(banks), "tiles0": tiles}
            first += iters * len(items)
            ds, db, dt = [0] * RING, [0] * BANKS, 0
            s["slot"], s["tile"] = [], []
            t = 0
            for j, (_, nm) in enumerate(items):
                pos = ring_positions(len(items))[j]
                s["slot"].append((pos, ds[pos]))
                ds[pos] += 1
                row = []
                for m in range(nm):
                    b = t % BANKS
                    last = m == nm - 1
                    row.append((b, db[b], None if last else dt + 1))
                    db[b] += 1
                    dt += not last
                    t += 1
                s["tile"].append(row)
            s["per"] = (ds, db, dt)
            for q in range(RING):
                slots[q] += iters * ds[q]
            for b in range(BANKS):
                banks[b] += iters * db[b]
            tiles += iters * dt
            self.sec[name] = s
        self.plan_ahead()

    def pos(self, sec, j):
        return self.sec[sec]["slot"][j][0]

    def uses(self, sec, i, j):
        s = self.sec[sec]
        pos, before = s["slot"][j]
        return s["slots0"][pos] + before + i * s["per"][0][pos]

    def bank(self, sec, j, m):
        return self.sec[sec]["tile"][j][m][0]

    def bank_uses(self, sec, i, j, m):
        s = self.sec[sec]
        b, before, _ = s["tile"][j][m]
        return s["banks0"][b] + before + i * s["per"][1][b]

    def tiles(self, sec, i, j, m):
        s = self.sec[sec]
        _, _, through = s["tile"][j][m]
        return None if through is None else s["tiles0"] + through + i * s["per"][2]

    def plan_ahead(self):
        flat = [(name, i, j) for name, s in self.sec.items() for i in range(s["iters"])
                for j in range(len(s["items"]))]
        held, latest = {}, None
        self.at_start, self.after = [], {x: [] for x in flat}
        for x in flat:
            q = self.pos(x[0], x[2])
            if q in held and (latest is None or flat.index(held[q]) > flat.index(latest)):
                latest = held[q]
            (self.at_start if latest is None else self.after[latest]).append(x)
            held[q] = x
        for name, s in self.sec.items():
            for i in range(1, s["iters"] - 1):
                for j in range(len(s["items"])):
                    a, b = self.after[name, 0, j], self.after[name, i, j]
                    assert [(x[0], x[1], x[2]) for x in a] == [(x[0], x[1] - i, x[2]) for x in b], (name, i, j)

    def ahead(self, sec, i, j, last):
        if last:
            return self.after[sec, self.sec[sec]["iters"] - 1, j]
        return [(s, i + di, jj) for s, di, jj in self.after[sec, 0, j]]


class Steps:

    def __init__(self, sem, counts):
        self.sem, self.counts, self.n = sem, counts, 0

    def turn(self):
        self.n = 0

    def done(self, name):
        self.n += 1
        assert self.counts.setdefault(name, self.n) == self.n, name
        self.counts["per turn"] = max(self.counts.get("per turn", 0), self.n)
        return self.sem, 1

    def at(self, name, i=0, ago=0):
        per = self.counts.get("per turn", 1)
        return self.sem, self.counts.get(name, 1) + (i - ago + 1) * per


def program(nc, T, out, counts, layers):
    from concourse import mybir
    import concourse.bass as bass

    F32, F32R, I32 = mybir.dt.float32, mybir.dt.float32r, mybir.dt.int32
    ALU = mybir.AluOpType
    ACT = mybir.ActivationFunctionType
    AX = mybir.AxisListType
    ds = bass.ds

    kinds = {"pool": 0, "gdn": 0, "mla": 0, "even": 0, "odd": 0}
    plan = []
    for kind in layers:
        plan.append((kind, kinds.get(kind, 0)))
        if kind in kinds:
            kinds[kind] += 1

    SECTIONS = []
    for n, (kind, _) in enumerate(plan):
        SECTIONS += [(f"{name}{n}", iters, items) for name, iters, items in SLOTS.get(kind, [])]
    W = Stream(SECTIONS)

    top = ExitStack()
    with top:
        area = [top]

        def sb(name, shape, dt=F32):
            return area[0].enter_context(nc.sbuf_tensor(name, shape, dt))

        def sem(name):
            return top.enter_context(nc.semaphore(name))

        def steps(section, *engines):
            return [Steps(sem(f"{section}_{e}"), counts.setdefault((section, e), {})) for e in engines]

        xT = sb("xT", [P, KD, SEQ])
        xh = sb("xh", [P, KD, SEQ], F32R)
        xl = sb("xl", [P, KD, SEQ], F32R)
        raw = sb("raw", [P, RING, SLOT])
        whi = sb("whi", [P, RING, SLOT], F32R)
        wlo = sb("wlo", [P, RING, SLOT], F32R)
        R = sb("R", [P, SEQ])
        Rt = sb("Rt", [P, SEQ])
        sq = sb("sq", [P, 2, SEQ])
        cst = sb("cst", [P, 2 * P])
        ident = cst[:, 0:P]
        ones = cst[:, P:2 * P]
        bias = sb("bias", [P, len(BIASES)])
        par = sb("par", [P, PARAMS["end"][1]])
        psum = top.enter_context(nc.psum_tensor("psum", [P, 8, SEQ], F32))

        def gbank(b):
            return psum[:, b, :]

        def wbank(b):
            return psum[:, BANKS + b, :]

        raw_landed = [sem(f"raw_landed{q}") for q in range(RING)]
        hi_ready = [sem(f"hi_ready{q}") for q in range(RING)]
        lo_ready = [sem(f"lo_ready{q}") for q in range(RING)]
        slot_used = [sem(f"slot_used{q}") for q in range(RING)]
        tile_ready = sem("tile_ready")
        bank_taken = [sem(f"bank_taken{b}") for b in range(BANKS)]
        consts_in = sem("consts_in")
        out_stored = sem("out_stored")

        def load_slot(sp, sec, i, j):
            q = W.pos(sec, j)
            nk, nm = W.sec[sec]["items"][j]
            n = nk * nm * P
            sp.wait_ge(lo_ready[q], W.uses(sec, i, j) + 1)
            s = W.sec[sec]
            src = T["weights"][s["first"] + j] if isinstance(i, int) and i == 0 and s["iters"] == 1 else \
                T["weights"][ds(i * len(s["items"]) + (s["first"] + j), 1)].rearrange("a p n -> p (a n)")
            sp.dma_start(raw[:, q, 0:n], src[:, 0:n]).then_inc(raw_landed[q], 16)

        def load_slots(sec):
            def sync(sp):
                s = W.sec[sec]
                if s["iters"] == 1:
                    for j in range(len(s["items"])):
                        load_slot(sp, sec, 0, j)
                else:
                    with sp.Fori(0, s["iters"]) as i:
                        for j in range(len(s["items"])):
                            load_slot(sp, sec, i, j)
            return sync

        def split_slots(sec):
            def gpsimd(pool):
                s = W.sec[sec]
                if s["iters"] == 1:
                    for j in range(len(s["items"])):
                        slot_lo(pool, sec, 0, j)
                else:
                    with pool.Fori(0, s["iters"]) as i:
                        for j in range(len(s["items"])):
                            slot_lo(pool, sec, i, j)
            return gpsimd

        def slot_hi(act, sec, i, j):
            q = W.pos(sec, j)
            nk, nm = W.sec[sec]["items"][j]
            act.wait_ge(raw_landed[q], W.uses(sec, i, j) * 16 + 16)
            act.wait_ge(slot_used[q], W.uses(sec, i, j) + 1)
            act.activation(whi[:, q, 0:nk * nm * P], raw[:, q, 0:nk * nm * P], ACT.Copy).then_inc(hi_ready[q], 1)

        def hi_after(act, sec, i, j, last):
            for nxt in W.ahead(sec, i, j, last):
                slot_hi(act, *nxt)

        def slot_lo(pool, sec, i, j):
            q = W.pos(sec, j)
            nk, nm = W.sec[sec]["items"][j]
            n = nk * nm * P
            pool.wait_ge(hi_ready[q], W.uses(sec, i, j) + 1)
            pool.tensor_tensor(wlo[:, q, 0:n], raw[:, q, 0:n], whi[:, q, 0:n].bitcast(F32),
                               ALU.subtract).then_inc(lo_ready[q], 1)

        def product(pe, sec, i, j, m, hi, lo, waits=None, k0=0, k1=None):
            q = W.pos(sec, j)
            nk, nm = W.sec[sec]["items"][j]
            b = W.bank(sec, j, m)
            k1 = nk if k1 is None else k1
            if m == k0 == 0:
                pe.wait_ge(lo_ready[q], W.uses(sec, i, j) + 2)
            if k0 == 0:
                pe.wait_ge(bank_taken[b], W.bank_uses(sec, i, j, m) + 1)
            for k in range(k0, k1):
                if waits and waits[k]:
                    pe.wait_ge(*waits[k])
                c = (k * nm + m) * P
                pe.matmul(gbank(b), whi[:, q, c:c + P], hi[:, k, :], start=k == 0, stop=False)
                pe.matmul(gbank(b), whi[:, q, c:c + P], lo[:, k, :], start=False, stop=False)
                done = pe.matmul(gbank(b), wlo[:, q, c:c + P], hi[:, k, :], start=False, stop=k == nk - 1)
            if k1 < nk:
                return
            if m == nm - 1:
                done.then_inc(slot_used[q], 1)
            else:
                done.then_inc(tile_ready, 1)

        def tile_done(sec, i, j, m):
            n = W.tiles(sec, i, j, m)
            if n is None:
                return slot_used[W.pos(sec, j)], W.uses(sec, i, j) + 2
            return tile_ready, n

        def tile_taken(sec, i, j, m):
            return bank_taken[W.bank(sec, j, m)], W.bank_uses(sec, i, j, m) + 2

        def taken(sec, j, m):
            return bank_taken[W.bank(sec, j, m)], 1

        def tile(sec, j, m):
            return gbank(W.bank(sec, j, m))

        def loop(eng, n, body):
            if n > 1:
                with eng.Fori(0, n - 1) as i:
                    body(i, False)
            body(n - 1, True)

        def param(name):
            c0, c1 = PARAMS[name]
            return par[:, c0:c1]

        x_ready = []

        def split(dve, st, hi, lo, src, name, wait=None):
            if wait:
                dve.wait_ge(*wait)
            dve.tensor_copy(hi, src).then_inc(*st.done(f"{name} hi"))
            return name

        def load_x(n, j):
            xin = sb("xin", [P, NCH, D])
            x_landed = sem("x_landed")
            te, ve = steps("load_x", "tensor", "vector")

            def sync(sp):
                sp.dma_start(xin[:, :, :], T["x"][0].rearrange("(t p) d -> p t d", p=P)).then_inc(x_landed, 16)

            def tensor(pe):
                pe.wait_ge(x_landed, 16)
                for k in range(KD):
                    if k >= BANKS:
                        pe.wait_ge(*ve.at(f"x {k - BANKS}"))
                    for t in range(NCH):
                        last = pe.transpose(wbank(k % BANKS)[:, t * P:(t + 1) * P],
                                            xin[:, t, k * P:(k + 1) * P], ident)
                    last.then_inc(*te.done(f"x {k}"))

            def vector(dve):
                for k in range(KD):
                    dve.wait_ge(*te.at(f"x {k}"))
                    dve.tensor_copy(xT[:, k, :], wbank(k % BANKS)).then_inc(*ve.done(f"x {k}"))

            x_ready.append(ve.at(f"x {KD - 1}"))
            return {"sync": sync, "tensor": tensor, "vector": vector, "steps": {"tensor": [te], "vector": [ve]}}

        def norm(n, gain, rewrite=False):
            ae, te, ve = steps(f"norm{n}", "scalar", "tensor", "vector")
            before = x_ready[-1]

            def scalar(act):
                act.wait_ge(*before)
                for k in range(KD):
                    if k >= 2:
                        act.wait_ge(*te.at(f"sum {k - 2}"))
                    act.activation(sq[:, k % 2, :], xT[:, k, :], ACT.Square).then_inc(*ae.done(f"square {k}"))
                act.wait_ge(*te.at(f"sum {KD - 1}"))
                act.activation(Rt[:, :], wbank(0), ACT.Ln, bias=bias[:, 0:1], scale=1.0 / D)\
                   .then_inc(*ae.done("ln"))
                act.wait_ge(*ae.at("ln"))
                act.activation(R[:, :], Rt[:, :], ACT.Exp, scale=-0.5).then_inc(*ae.done("R"))

            def tensor(pe):
                for k in range(KD):
                    pe.wait_ge(*ae.at(f"square {k}"))
                    pe.matmul(wbank(0), ones, sq[:, k % 2, :], start=k == 0, stop=k == KD - 1)\
                      .then_inc(*te.done(f"sum {k}"))

            def vector(dve):
                dve.wait_ge(*before)
                if not rewrite:
                    for k in range(KD):
                        dve.tensor_scalar(xh[:, k, :], xT[:, k, :], gain[:, k:k + 1], None, ALU.mult)\
                           .then_inc(*ve.done(f"hi {k}"))
                        dve.wait_ge(*ve.at(f"hi {k}"))
                        dve.scalar_tensor_tensor(out=xl[:, k, :], in0=xT[:, k, :], scalar=gain[:, k:k + 1],
                                                 in1=xh[:, k, :].bitcast(F32), op0=ALU.mult, op1=ALU.subtract)\
                           .then_inc(*ve.done(f"lo {k}"))
                dve.wait_ge(*ae.at("R"))
                if rewrite:
                    for k in range(KD):
                        dve.scalar_tensor_tensor(out=xT[:, k, :], in0=xT[:, k, :], scalar=gain[:, k:k + 1],
                                                 in1=R[:, :], op0=ALU.mult, op1=ALU.mult)\
                           .then_inc(*ve.done(f"x {k}"))

            if rewrite:
                x_ready.append(ve.at(f"x {KD - 1}"))
            return {"scalar": scalar, "tensor": tensor, "vector": vector,
                    "steps": {"scalar": [ae], "tensor": [te], "vector": [ve]}, "v": ve}

        def operand_waits(nv):
            return [nv["v"].at(f"lo {k}") for k in range(KD)]

        def add_to_x(dve, sec, i, j, tiles):
            for m, t in enumerate(tiles):
                dve.wait_ge(*tile_done(sec, i, j, m))
                dve.tensor_tensor(xT[:, t, :], tile(sec, j, m), xT[:, t, :], ALU.add).then_inc(*taken(sec, j, m))

        def merge(*parts):
            out = {"steps": {}}
            for e in ("sync", "gpsimd", "scalar", "vector", "tensor"):
                fs = [p[e] for p in parts if e in p]
                if fs:
                    out[e] = (lambda fs: lambda eng: [f(eng) for f in fs] and None)(fs)
                ss = [s for p in parts for s in p.get("steps", {}).get(e, [])]
                if ss:
                    out["steps"][e] = ss
            return out

        def pool_layer(n, l):
            nv = norm(n, param(f"norm_g{(0, 3)[l]}"))
            sec = f"pool{n}"
            G = D * 2 // 4 // P
            u = sb(f"pool_u{n}", [P, G, SEQ])
            cum = sb(f"pool_cum{n}", [P, 2, PAD + SEQ])
            d = sb(f"pool_d{n}", [P, 2, SEQ])
            ph = sb(f"pool_ph{n}", [P, G, SEQ], F32R)
            pl = sb(f"pool_pl{n}", [P, G, SEQ], F32R)
            yh = sb(f"pool_yh{n}", [P, G, SEQ], F32R)
            yl = sb(f"pool_yl{n}", [P, G, SEQ], F32R)
            g = sb(f"pool_g{n}", [P, G, SEQ])
            rcnt = sb(f"pool_rcnt{n}", [P, 4, SEQ])
            onesrow = sb(f"pool_onesrow{n}", [P, SEQ])
            scale = param(f"pool_scale{l}")
            tables_in = sem(f"pool_tables_in{n}")
            ae, te, ve = steps(sec, "scalar", "tensor", "vector")

            def tables(act):
                act.wait_ge(*x_ready_before)
                act.dma_start(rcnt[:, :, :], T["rcnt"].rearrange("p (w s) -> p w s", w=4)).then_inc(tables_in, 16)

            def sync(sp):
                load_slots(sec)(sp)

            def scalar(act):
                def turn(i, last):
                    ae.turn()
                    for j in range(8):
                        hi_after(act, sec, i, j, last)
                    for m in range(G):
                        act.wait_ge(*tile_taken(sec, i, 4 + m, 0))
                        act.activation(g[:, m, :], g[:, m, :], ACT.Silu).then_inc(*ae.done(f"silu {m}"))
                    for j in range(8, 14):
                        hi_after(act, sec, i, j, last)
                loop(act, 4, turn)

            def tensor(pe):
                def turn(i, last):
                    te.turn()
                    first = operand_waits(nv)
                    for j in range(8):
                        product(pe, sec, i, j, 0, xh, xl, first if j == 0 else None)
                    for m in range(G):
                        product(pe, sec, i, 8 + m // 2, m % 2, ph, pl, [ve.at(f"p lo {k}", i) for k in range(G)])
                    for m in range(KD):
                        product(pe, sec, i, 10 + m // 2, m % 2, yh, yl, [ve.at(f"y lo {k}", i) for k in range(G)])
                loop(pe, 4, turn)

            def vector(dve):
                dve.wait_ge(tables_in, 16)
                dve.memset(cum[:, :, 0:PAD], 0.0).then_inc(tables_in, 1)
                dve.memset(onesrow[:, :], 1.0).then_inc(tables_in, 1)
                dve.wait_ge(tables_in, 18)

                def turn(i, last):
                    ve.turn()
                    shift = WINDOWS[3] if last else None
                    for m in range(G):
                        dve.wait_ge(*tile_done(sec, i, m, 0))
                        dve.tensor_tensor(u[:, m, :], tile(sec, m, 0), R[:, :], ALU.mult)\
                           .then_inc(*taken(sec, m, 0))
                    for m in range(G):
                        b = m % 2
                        dve.wait_ge(*tile_taken(sec, i, m, 0))
                        dve.tensor_tensor_scan(cum[:, b, PAD:], onesrow[:, :], u[:, m, :], 0.0,
                                               ALU.mult, ALU.add).then_inc(*ve.done(f"cum {m}"))
                        dve.wait_ge(*ve.at(f"cum {m}", i))
                        back = cum[:, b, PAD - shift:PAD - shift + SEQ] if last else \
                            cum[:, b, ds(PAD - 2 - i * i - i, SEQ)]
                        dve.tensor_tensor(d[:, b, :], cum[:, b, PAD:], back, ALU.subtract)\
                           .then_inc(*ve.done(f"window {m}"))
                        dve.wait_ge(*ve.at(f"window {m}", i))
                        dve.tensor_tensor(d[:, b, :], d[:, b, :], rcnt[:, 3 if last else ds(i, 1), :], ALU.mult)\
                           .then_inc(*ve.done(f"mean {m}"))
                        dve.wait_ge(*ve.at(f"mean {m}", i))
                        dve.tensor_tensor(u[:, m, :], d[:, b, :], u[:, m, :], ALU.subtract)\
                           .then_inc(*ve.done(f"p {m}"))
                        dve.wait_ge(*ve.at(f"p {m}", i))
                        dve.tensor_copy(ph[:, m, :], u[:, m, :]).then_inc(*ve.done(f"p hi {m}"))
                        dve.wait_ge(*ve.at(f"p hi {m}", i))
                        dve.tensor_tensor(pl[:, m, :], u[:, m, :], ph[:, m, :].bitcast(F32), ALU.subtract)\
                           .then_inc(*ve.done(f"p lo {m}"))
                    for m in range(G):
                        dve.wait_ge(*tile_done(sec, i, 4 + m, 0))
                        dve.tensor_tensor(g[:, m, :], tile(sec, 4 + m, 0), R[:, :], ALU.mult)\
                           .then_inc(*taken(sec, 4 + m, 0))
                    for m in range(G):
                        dve.wait_ge(*ae.at(f"silu {m}", i))
                        dve.wait_ge(*tile_done(sec, i, 8 + m // 2, m % 2))
                        dve.scalar_tensor_tensor(out=u[:, m, :], in0=tile(sec, 8 + m // 2, m % 2),
                                                 scalar=scale[:, 12 + m:13 + m] if last else
                                                 scale[:, ds(i * G + m, 1)],
                                                 in1=g[:, m, :], op0=ALU.mult, op1=ALU.mult)\
                           .then_inc(*taken(sec, 8 + m // 2, m % 2))
                        dve.wait_ge(*tile_taken(sec, i, 8 + m // 2, m % 2))
                        dve.tensor_copy(yh[:, m, :], u[:, m, :]).then_inc(*ve.done(f"y hi {m}"))
                        dve.wait_ge(*ve.at(f"y hi {m}", i))
                        dve.tensor_tensor(yl[:, m, :], u[:, m, :], yh[:, m, :].bitcast(F32), ALU.subtract)\
                           .then_inc(*ve.done(f"y lo {m}"))
                    for j in range(4):
                        add_to_x(dve, sec, i, 10 + j, (2 * j, 2 * j + 1))
                loop(dve, 4, turn)

            x_ready_before = x_ready[-1]
            x_ready.append(tile_taken(sec, 3, 13, 1))
            me = {"sync": sync, "gpsimd": split_slots(sec), "scalar": scalar, "tensor": tensor, "vector": vector,
                  "steps": {"scalar": [ae], "tensor": [te], "vector": [ve]}}
            return merge({"scalar": tables}, nv, me)

        def final_norm(n, l):
            return norm(n, param("final_g"), rewrite=True)

        def store_x(n, l):
            y = sb("y", [P, 2, D])
            te, ve = steps("store_x", "tensor", "vector")
            before = x_ready[-1]

            def tensor(pe):
                pe.wait_ge(*before)
                for t in range(NCH):
                    for h in range(2):
                        b = (2 * t + h) % BANKS
                        if 2 * t + h >= BANKS:
                            pe.wait_ge(*ve.at(f"y {t - 2} {h}"))
                        for k in range(4):
                            last = pe.transpose(wbank(b)[:, k * P:(k + 1) * P],
                                                xT[:, 4 * h + k, t * P:(t + 1) * P], ident)
                        last.then_inc(*te.done(f"y {t} {h}"))

            def vector(dve):
                for t in range(NCH):
                    if t >= 2:
                        dve.wait_ge(out_stored, 16 * (t - 1))
                    for h in range(2):
                        dve.wait_ge(*te.at(f"y {t} {h}"))
                        dve.tensor_copy(y[:, t % 2, h * 512:(h + 1) * 512], wbank((2 * t + h) % BANKS))\
                           .then_inc(*ve.done(f"y {t} {h}"))

            def sync(sp):
                for t in range(NCH):
                    sp.wait_ge(*ve.at(f"y {t} 1"))
                    if t:
                        sp.wait_ge(out_stored, 16 * t)
                    sp.dma_start(out[0, t * P:(t + 1) * P, :], y[:, t % 2, :]).then_inc(out_stored, 16)
                sp.wait_ge(out_stored, 16 * NCH)

            return {"sync": sync, "tensor": tensor, "vector": vector, "steps": {"tensor": [te], "vector": [ve]}}

        def even_layer(n, l):
            nv = norm(n, param("a_norm_w"))
            dt_sec, glu_sec, first_sec, sec, last_sec = (f"ev_{s}{n}" for s in ("dt", "glu", "first", "ssd", "last"))
            zf_sec, z_sec, zl_sec = (f"ev_{s}{n}" for s in ("zfirst", "z", "zlast"))
            GROUPS, HG, H, TAPS = 4, 4, 16, 31
            PADU = TAPS - 1
            ue = sb("e_ue", [P, PADU + SEQ])
            uk = sb("e_uk", [P, GROUPS, PADU + SEQ])
            conv31 = sb("e_c", [P, KD, SEQ])
            pre = sb("e_pre", [P, 4, 3 + SEQ])
            stg = sb("e_stg", [P, 4, SEQ])
            gp = sb("e_gp", [P, 2, SEQ])
            gs = sb("e_gs", [P, 2, SEQ])
            ecs = sb("e_ecs", [P, 2, SEQ])
            Dd = sb("e_D", [P, 2, SEQ])
            Gm = sb("e_Gm", [16, 2, SEQ])
            xds = sb("e_xd", [P, 2, NCH, 2 * P])
            xd, xw = xds[:, 0, :, :], xds[:, 1, :, :]
            btok = sb("e_btok", [P, NCH, P])
            cbm = sb("e_cbm", [P, NCH, P])
            HS = sb("e_HS", [P, 3, 2 * P])
            yh = sb("e_yh", [P, 2, SEQ], F32R)
            yl = sb("e_yl", [P, 2, SEQ], F32R)
            Q = sb("e_Q", [P, SEQ])
            gcol = sb("e_gcol", [P, 3, NCH, H])
            ecl = sb("e_ecl", [P, H, NCH])
            small_ = sb("e_small", [P, 3 * 64])
            mU = sb("e_mU", [P, P])
            wt = sb("e_wt", [P, 32])
            yf = xds[:, :, :, :].rearrange("p a c v -> p (a c v)")[:, 0:2 * SEQ].rearrange("p (d s) -> p d s", d=2)
            acc = sb("e_acc", [P, SEQ])
            tmp = [pre[:, x, 0:SEQ] for x in range(4)] + [gp[:, 0, :], gp[:, 1, :]]
            dtb, alog = param("a_dt_bias"), param("a_a_log")
            conv, dw = param("a_conv"), param("a_dw")
            dskip, snw = param("a_d_skip"), param("a_ssd_norm_w")
            lnw, lnb = param("a_ln_w"), param("a_ln_b")
            mask_in = sem("even_mask_in")
            ab, tb, vbs = steps(f"ev_dt{n}", "scalar", "tensor", "vector")
            ag, vg = steps(f"ev_glu{n}", "scalar", "vector")
            ap_, vp = steps(f"ev_prep{n}", "scalar", "vector")
            ae, te, ve = steps(sec, "scalar", "tensor", "vector")
            al, tl, vl = steps(f"ev_ln{n}", "scalar", "tensor", "vector")
            az, vz = steps(f"ev_z{n}", "scalar", "vector")
            x_ready_before = x_ready[-1]
            h16 = slice(0, 16)
            cs16 = slice(32, 48)

            def chunks(ap):
                return ap.rearrange("p (c n) -> p c n", c=NCH)

            def at(ap, i, per, k=0, w=1):
                return ap[:, ds(i * per + k, w)] if not isinstance(i, int) else ap[:, i * per + k:i * per + k + w]

            def dt_take(dve):
                dve.wait_ge(*tile_done(dt_sec, 0, 0, 0))
                dve.tensor_tensor(tmp[0], tile(dt_sec, 0, 0), R[:, :], ALU.mult).then_inc(*taken(dt_sec, 0, 0))
                dve.memset(Q[:, :], 0.0).then_inc(*vbs.done("Q zero"))
                dve.memset(ue[:, 0:PADU], 0.0).then_inc(*vbs.done("pad of ue"))
                dve.memset(uk[:, :, 0:PADU], 0.0).then_inc(*vbs.done("pads of uk"))
                dve.wait_ge(*vbs.at("pads of uk"))

            def dt_vector(dve):
                q = tmp[0][h16]
                dve.wait_ge(*tile_taken(dt_sec, 0, 0, 0))
                dve.tensor_scalar(tmp[1][h16], q, dtb[h16], None, ALU.add).then_inc(*vbs.done("z"))
                dve.wait_ge(*ab.at("exp z"))
                dve.tensor_scalar(tmp[3][h16], tmp[2][h16], 1.0, None, ALU.add).then_inc(*vbs.done("u"))
                dve.wait_ge(*vbs.at("u"))
                dve.tensor_scalar(tmp[4][h16], tmp[3][h16], -1.0, None, ALU.add).then_inc(*vbs.done("u-1"))
                dve.wait_ge(*vbs.at("u-1"))
                dve.tensor_scalar(tmp[5][h16], tmp[4][h16], 0.0, None, ALU.is_equal).then_inc(*vbs.done("is 0"))
                dve.wait_ge(*vbs.at("is 0"))
                dve.tensor_tensor(tmp[4][h16], tmp[4][h16], tmp[5][h16], ALU.add).then_inc(*vbs.done("den"))
                dve.wait_ge(*vbs.at("den"))
                dve.reciprocal(tmp[4][h16], tmp[4][h16]).then_inc(*vbs.done("1/den"))
                dve.wait_ge(*ab.at("ln u"))
                dve.wait_ge(*vbs.at("1/den"))
                dve.tensor_tensor(tmp[3][h16], tmp[3][h16], tmp[4][h16], ALU.mult).then_inc(*vbs.done("ln/den"))
                dve.wait_ge(*vbs.at("ln/den"))
                dve.tensor_tensor(tmp[3][h16], tmp[3][h16], tmp[5][h16], ALU.add).then_inc(*vbs.done("ratio"))
                dve.wait_ge(*vbs.at("ratio"))
                dve.tensor_tensor(tmp[3][h16], tmp[3][h16], tmp[2][h16], ALU.mult).then_inc(*vbs.done("log1p"))
                dve.wait_ge(*vbs.at("log1p"))
                dve.scalar_tensor_tensor(out=Q[h16, :], in0=tmp[1][h16], scalar=0.0, in1=tmp[3][h16], op0=ALU.max,
                                         op1=ALU.add).then_inc(*vbs.done("dt"))
                dve.wait_ge(*vbs.at("dt"))
                dve.wait_ge(*ab.at("exp a"))
                dve.tensor_scalar(tmp[3][cs16], Q[h16, :], small_[h16, 0:1], -1.0, ALU.mult, ALU.mult)\
                   .then_inc(*vbs.done("da"))
                dve.memset(tmp[5], 1.0).then_inc(*vbs.done("ones"))
                dve.wait_ge(*vbs.at("ones"))
                for c in range(NCH):
                    s = slice(c * P, (c + 1) * P)
                    dve.tensor_tensor_scan(Q[cs16, s], tmp[5][cs16, s], tmp[3][cs16, s], 0.0, ALU.mult, ALU.add)\
                       .then_inc(*vbs.done(f"cumsum {c}"))
                for c in range(NCH):
                    s = slice(c * P, (c + 1) * P)
                    dve.wait_ge(*vbs.at(f"cumsum {c}"))
                    dve.tensor_scalar(tmp[4][cs16, s], Q[cs16, s], Q[cs16, c * P + P - 1:(c + 1) * P], None,
                                      ALU.subtract).then_inc(*vbs.done(f"cs-last {c}"))
                dve.tensor_copy(small_[h16, 64:68], Q[cs16, P - 1::P]).then_inc(*vbs.done("last"))
                dve.wait_ge(*vbs.at("last"))
                dve.tensor_tensor(small_[h16, 128:192].rearrange("p (h c) -> p h c", c=NCH),
                                  ident[h16, 0:16].unsqueeze(2).to_broadcast([16, H, NCH]),
                                  small_[h16, 64:68].unsqueeze(1).to_broadcast([16, H, NCH]), ALU.mult)\
                   .then_inc(*vbs.done("last diagonal"))
                dve.wait_ge(*ab.at("exp last-cs"))
                dve.tensor_tensor(Q[64:80, :], Q[h16, :], tmp[1][h16], ALU.mult).then_inc(*vbs.done("dt exp"))
                dve.wait_ge(*tb.at("columns"))
                dve.tensor_copy(gcol[:, :, :, :],
                                wbank(0).rearrange("p (c q h) -> p q c h", c=NCH, q=4)[:, 0:3, :, 0:H])\
                   .then_inc(*vbs.done("columns"))
                dve.memset(pre[:, :, 0:3], 0.0).then_inc(*vbs.done("pads"))
                dve.wait_ge(*vbs.at("pads"))
                dve.wait_ge(mask_in, 16)

            def dt_scalar(act):
                act.wait_ge(*vbs.at("z"))
                act.activation(tmp[2][h16], tmp[1][h16], ACT.Abs).then_inc(*ab.done("abs z"))
                act.wait_ge(*ab.at("abs z"))
                act.activation(tmp[2][h16], tmp[2][h16], ACT.Exp, scale=-1.0).then_inc(*ab.done("exp z"))
                act.activation(small_[h16, 0:1], alog[h16], ACT.Exp).then_inc(*ab.done("exp a"))
                act.wait_ge(*vbs.at("u-1"))
                act.activation(tmp[3][h16], tmp[3][h16], ACT.Ln).then_inc(*ab.done("ln u"))
                act.wait_ge(*vbs.at("cs-last 3"))
                act.activation(tmp[1][h16], tmp[4][cs16], ACT.Exp, scale=-1.0).then_inc(*ab.done("exp last-cs"))
                act.wait_ge(*tb.at("last"))
                act.activation(ecl[:, :, :], wbank(1)[:, 0:64].rearrange("p (h c) -> p h c", c=NCH), ACT.Exp)\
                   .then_inc(*ab.done("exp last"))

            def dt_tensor(pe):
                pe.wait_ge(*vbs.at("last diagonal"))
                pe.matmul(wbank(1)[:, 0:64], ones[h16, :], small_[h16, 128:192], start=True, stop=True)\
                  .then_inc(*tb.done("last"))
                pe.wait_ge(*vbs.at("dt exp"))
                for c in range(NCH):
                    last = pe.transpose(wbank(0)[:, c * P:(c + 1) * P], Q[:, c * P:(c + 1) * P], ident)
                last.then_inc(*tb.done("columns"))

            def taps(dve, st, i, source, k0, k1):
                for k in range(k0, k1):
                    if k == 0:
                        dve.tensor_scalar(acc[:, :], source[:, 0:SEQ], wt[:, 0:1], wt[:, TAPS:TAPS + 1],
                                          ALU.mult, ALU.add).then_inc(*st.done("tap 0"))
                    else:
                        dve.wait_ge(*st.at(f"tap {k - 1}", i))
                        dve.scalar_tensor_tensor(out=acc[:, :], in0=source[:, k:k + SEQ], scalar=wt[:, k:k + 1],
                                                 in1=acc[:, :], op0=ALU.mult, op1=ALU.add)\
                           .then_inc(*st.done(f"tap {k}"))

            def channel(ap, i, per, k):
                return ap[:, i * per + k, :] if isinstance(i, int) else ap[:, ds(i * per + k, 1), :]\
                    .rearrange("p a s -> p (a s)")

            def glu_vector(dve, i):
                vg.turn()
                dve.tensor_copy(wt[:, :], at(dw, i, 64, 0, 32)).then_inc(*vg.done("taps"))
                for x in range(2):
                    dve.wait_ge(*tile_done(glu_sec, i, 2 * x, 0))
                    dve.tensor_tensor(stg[:, 2 * x, :], tile(glu_sec, 2 * x, 0), R[:, :], ALU.mult)\
                       .then_inc(*taken(glu_sec, 2 * x, 0))
                    dve.wait_ge(*tile_done(glu_sec, i, 2 * x + 1, 0))
                    dve.tensor_tensor(stg[:, 2 * x + 1, :], tile(glu_sec, 2 * x + 1, 0), R[:, :], ALU.mult)\
                       .then_inc(*taken(glu_sec, 2 * x + 1, 0))
                    if x == 0:
                        dve.wait_ge(*ag.at("sigmoid 0", i))
                        dve.tensor_tensor(ue[:, PADU:], stg[:, 0, :], stg[:, 1, :], ALU.mult).then_inc(*vg.done("u 0"))
                        dve.wait_ge(*vg.at("u 0", i))
                        taps(dve, vg, i, ue, 0, 15)
                dve.wait_ge(*ag.at("sigmoid 1", i))
                dve.tensor_tensor(channel(uk[:, :, PADU:], i, 1, 0), stg[:, 2, :], stg[:, 3, :], ALU.mult)\
                   .then_inc(*vg.done("u 1"))
                taps(dve, vg, i, ue, 15, TAPS)
                dve.wait_ge(*vg.at(f"tap {TAPS - 1}", i))
                dve.tensor_copy(channel(conv31[:, :, :], i, 2, 0), acc[:, :]).then_inc(*vg.done("conv"))
                dve.wait_ge(*vg.at("conv", i))

            def glu_scalar(act, i, last):
                ag.turn()
                for x in range(2):
                    hi_after(act, glu_sec, i, 2 * x, last)
                    hi_after(act, glu_sec, i, 2 * x + 1, last)
                    act.wait_ge(*tile_taken(glu_sec, i, 2 * x + 1, 0))
                    act.activation(stg[:, 2 * x + 1, :], stg[:, 2 * x + 1, :], ACT.Sigmoid)\
                       .then_inc(*ag.done(f"sigmoid {x}"))

            def in_pieces(pe, s, i):
                for t in range(6):
                    for k in range(0, KD, 2):
                        product(pe, s, i, t, 0, xh, xl, None, k, k + 2)
                        yield

            def evac(dve, s, i, t):
                dve.wait_ge(*tile_done(s, i, t, 0))
                dst = pre[:, t, 3:] if t < 4 else gp[:, t - 4, :]
                dve.tensor_tensor(dst, tile(s, t, 0), R[:, :], ALU.mult).then_inc(*taken(s, t, 0))

            def prep_vector(dve, s, i, h, adds=None):
                vp.turn()
                dve.wait_ge(*tile_taken(s, i, 3, 0))
                dve.wait_ge(*te.at("y 3", h, 1))
                for tap in range(4):
                    for x in range(4):
                        w = at(conv, h, 20, x * 5 + tap)
                        if tap == 0:
                            dve.tensor_scalar(stg[:, x, :], pre[:, x, 0:SEQ], w, None, ALU.mult)\
                               .then_inc(*vp.done(f"tap {tap} {x}"))
                        else:
                            dve.wait_ge(*vp.at(f"tap {tap - 1} {x}", h))
                            dve.scalar_tensor_tensor(out=stg[:, x, :], in0=pre[:, x, tap:tap + SEQ], scalar=w,
                                                     in1=stg[:, x, :], op0=ALU.mult, op1=ALU.add)\
                               .then_inc(*vp.done(f"tap {tap} {x}"))
                    if adds:
                        adds(2 * tap)
                        adds(2 * tap + 1)

            def prep_scalar(act, s, i, h):
                ap_.turn()
                for x in (2, 3, 0, 1):
                    act.wait_ge(*vp.at(f"tap 3 {x}", h))
                    act.activation(stg[:, x, :], stg[:, x, :], ACT.Silu, bias=at(conv, h, 20, x * 5 + 4))\
                       .then_inc(*ap_.done(f"silu {x}"))
                act.wait_ge(*ve.at("y z 1", h, 1))
                act.wait_ge(*tile_taken(s, i, 5, 0))
                act.activation(gs[:, :, :], gp[:, :, :], ACT.Silu).then_inc(*ap_.done("silu z"))

            def work_tensor(pe, i, more):
                te.turn()
                pe.wait_ge(*ap_.at("silu 2", i))
                pe.wait_ge(*ve.at("y skip 1", i, 1))
                for c in range(NCH):
                    last = pe.transpose(wbank(2)[:, c * P:(c + 1) * P], stg[:, 2, c * P:(c + 1) * P], ident)
                last.then_inc(*te.done("B tokens"))
                pe.wait_ge(*ap_.at("silu 3", i))
                for c in range(NCH):
                    s = slice(c * P, (c + 1) * P)
                    last = pe.matmul(wbank(3)[:, s], stg[:, 2, s], stg[:, 3, s], start=True, stop=True)
                last.then_inc(*te.done("cb"))
                pe.wait_ge(*ap_.at("silu 1", i))
                pe.wait_ge(*ae.at("ln y", i, 1))
                for c in range(NCH):
                    for d in range(2):
                        a = (c % 2) * 2 * P + d * P
                        last = pe.transpose(wbank(c // 2)[:, a:a + P], stg[:, d, c * P:(c + 1) * P], ident)
                last.then_inc(*te.done("x tokens"))
                more()
                more()
                for c in range(3):
                    b = 2 + c % 2
                    if c == 0:
                        pe.wait_ge(*ae.at("B tokens", i))
                        pe.wait_ge(*ve.at("x w 1", i))
                    elif c == 2:
                        pe.wait_ge(*ve.at("state 0", i))
                    pe.matmul(wbank(b)[:, 0:2 * P], btok[:, c, :], xw[:, c, :], start=True, stop=True)\
                      .then_inc(*te.done(f"state {c}"))
                    more()
                pe.wait_ge(*ve.at("x dt 1", i))
                for h in range(HG):
                    if h >= 2:
                        pe.wait_ge(*ve.at(f"row {h}", i))
                    pe.matmul(wbank(h % 2), ones[h16, :], Gm[:, h % 2, :], start=True, stop=True)\
                      .then_inc(*te.done(f"cs row {h}"))
                    more()
                    if h:
                        y_head(pe, i, h - 1)
                        more()
                        more()
                y_head(pe, i, HG - 1)
                more()
                for d in range(2):
                    pe.wait_ge(*ae.at(f"y square {d}", i))
                    pe.matmul(wbank(0), ones, ecs[:, d, :], start=d == 0, stop=d == 1).then_inc(*te.done(f"y sum {d}"))

            def y_head(pe, i, h):
                b, r = 2 + h // 2, slice(64 * (h % 2), 64 * (h % 2) + 64)
                hc = slice(64 * h, 64 * h + 64)
                pe.wait_ge(*ve.at(f"M {h}", i))
                for c in range(NCH):
                    s = slice(c * P, (c + 1) * P)
                    if c:
                        pe.matmul(wbank(b)[r, s], HS[:, c - 1, hc], ecs[:, h % 2, s], start=True, stop=False)
                    last = pe.matmul(wbank(b)[r, s], xd[:, c, hc], Dd[:, h % 2, s], start=c == 0, stop=True)
                last.then_inc(*te.done(f"y {h}"))

            def work_scalar(act, i, between):
                ae.turn()
                act.wait_ge(*te.at("B tokens", i))
                act.activation(btok[:, :, :], chunks(wbank(2)), ACT.Copy).then_inc(*ae.done("B tokens"))
                for h in range(HG):
                    act.wait_ge(*te.at(f"cs row {h}", i))
                    act.activation(ecs[:, h % 2, :], wbank(h % 2), ACT.Exp).then_inc(*ae.done(f"exp cs {h}"))
                    act.wait_ge(*ve.at(f"d {h}", i))
                    act.activation(Dd[:, h % 2, :], Dd[:, h % 2, :], ACT.Exp).then_inc(*ae.done(f"exp d {h}"))
                    between(h)
                for d in range(2):
                    act.wait_ge(*ve.at(f"y z {d}", i))
                    act.activation(ecs[:, d, :], yf[:, d, :], ACT.Square).then_inc(*ae.done(f"y square {d}"))
                act.wait_ge(*te.at("y sum 1", i))
                act.activation(Rt[:, :], wbank(0), ACT.Ln, scale=1.0 / (2 * P), bias=bias[:, 0:1])\
                   .then_inc(*ae.done("ln y"))
                act.wait_ge(*ae.at("ln y", i))
                act.activation(Rt[:, :], Rt[:, :], ACT.Exp, scale=-0.5).then_inc(*ae.done("1/rms y"))
                between(4)
                between(5)

            def work_vector(dve, i, evac):
                ve.turn()
                csc = slice(4 * i, 4 * i + 4) if isinstance(i, int) else ds(i * 4, 4)

                def row(h):
                    sel = ident[cs16, 32 + 4 * i + h:33 + 4 * i + h] if isinstance(i, int) else \
                        ident[cs16, ds(i * 4 + (32 + h), 1)]
                    if h >= 2:
                        dve.wait_ge(*te.at(f"cs row {h - 2}", i))
                    dve.tensor_scalar(Gm[:, h % 2, :], Q[cs16, :], sel, None, ALU.mult).then_inc(*ve.done(f"row {h}"))

                row(0)
                row(1)
                dve.tensor_copy(wt[:, :], at(dw, i, 64, 32, 32)).then_inc(*ve.done("taps"))
                dve.tensor_copy(ue[:, PADU:], channel(uk[:, :, PADU:], i, 1, 0)).then_inc(*ve.done("u"))
                dve.wait_ge(*te.at("cb", i))
                dve.tensor_tensor(cbm[:, :, :], chunks(wbank(3)), mU[:, :].unsqueeze(1).to_broadcast([P, NCH, P]),
                                  ALU.mult).then_inc(*ve.done("cb"))
                for q, dst, name in ((2, xw, "x w"), (0, xd, "x dt")):
                    for h in range(2):
                        dve.wait_ge(*te.at("x tokens", i))
                        c = gcol[:, q, 2 * h:2 * h + 2, csc].unsqueeze(3).to_broadcast([P, 2, HG, 64])
                        dve.tensor_tensor(dst[:, 2 * h:2 * h + 2, :].rearrange("p c (h v) -> p c h v", h=HG),
                                          wbank(h).rearrange("p (c h v) -> p c h v", c=2, h=HG), c, ALU.mult)\
                           .then_inc(*ve.done(f"{name} {h}"))
                dve.wait_ge(*ve.at("u", i))
                dve.wait_ge(*te.at("state 0", i))
                dve.tensor_copy(HS[:, 0, :], wbank(2)[:, 0:2 * P]).then_inc(*ve.done("state 0"))
                for c in (1, 2):
                    dve.wait_ge(*ve.at(f"state {c - 1}", i))
                    e = ecl[:, csc, c:c + 1].rearrange("p h a -> p (h a)").unsqueeze(2).to_broadcast([P, HG, 64])
                    dve.tensor_tensor(HS[:, c, :].rearrange("p (h v) -> p h v", h=HG),
                                      HS[:, c - 1, :].rearrange("p (h v) -> p h v", h=HG), e, ALU.mult)\
                       .then_inc(*ve.done(f"decayed {c}"))
                    dve.wait_ge(*ve.at(f"decayed {c}", i))
                    dve.wait_ge(*te.at(f"state {c}", i))
                    dve.tensor_tensor(HS[:, c, :], HS[:, c, :], wbank(2 + c % 2)[:, 0:2 * P], ALU.add)\
                       .then_inc(*ve.done(f"state {c}"))
                taps(dve, ve, i, ue, 0, 4)
                for h in range(HG):
                    dve.wait_ge(*ae.at(f"exp cs {h}", i))
                    for c in range(NCH):
                        s = slice(c * P, (c + 1) * P)
                        col = gcol[:, 1, c, ds(i * 4 + h, 1)] if not isinstance(i, int) else \
                            gcol[:, 1, c, 4 * i + h:4 * i + h + 1]
                        last = dve.tensor_scalar(Dd[:, h % 2, s], wbank(h % 2)[:, s], col, 0.0, ALU.subtract, ALU.min)
                    last.then_inc(*ve.done(f"d {h}"))
                    dve.tensor_tensor(ecs[:, h % 2, :], ecs[:, h % 2, :], stg[:, 3, :], ALU.mult)\
                       .then_inc(*ve.done(f"C exp cs {h}"))
                    dve.wait_ge(*ae.at(f"exp d {h}", i))
                    dve.tensor_tensor(Dd[:, h % 2, :], Dd[:, h % 2, :],
                                      cbm[:, :, :].rearrange("p c n -> p (c n)"), ALU.mult).then_inc(*ve.done(f"M {h}"))
                    if h < 2:
                        row(h + 2)
                    evac(h)
                    taps(dve, ve, i, ue, 4 + 5 * h, 9 + 5 * h)
                for d in range(2):
                    dve.wait_ge(*te.at("y 3", i))
                    w = at(dskip, i, 2, d)
                    dve.scalar_tensor_tensor(out=yf[:, d, :], in0=stg[:, d, :], scalar=w, in1=wbank(2 + d),
                                             op0=ALU.mult, op1=ALU.add).then_inc(*ve.done(f"y skip {d}"))
                    dve.wait_ge(*ve.at(f"y skip {d}", i))
                    dve.wait_ge(*ap_.at("silu z", i))
                    dve.tensor_tensor(yf[:, d, :], yf[:, d, :], gs[:, d, :], ALU.mult).then_inc(*ve.done(f"y z {d}"))
                taps(dve, ve, i, ue, 24, TAPS)
                for d in range(2):
                    dve.wait_ge(*ae.at("1/rms y", i))
                    dve.scalar_tensor_tensor(out=yf[:, d, :], in0=yf[:, d, :], scalar=at(snw, i, 2, d), in1=Rt[:, :],
                                             op0=ALU.mult, op1=ALU.mult).then_inc(*ve.done(f"y {d}"))
                for d in range(2):
                    dve.wait_ge(*ve.at(f"y {d}", i))
                    dve.tensor_copy(yh[:, d, :], yf[:, d, :]).then_inc(*ve.done(f"y hi {d}"))
                for d in range(2):
                    dve.wait_ge(*ve.at(f"y hi {d}", i))
                    dve.tensor_tensor(yl[:, d, :], yf[:, d, :], yh[:, d, :].bitcast(F32), ALU.subtract)\
                       .then_inc(*ve.done(f"y lo {d}"))
                dve.wait_ge(*ve.at(f"tap {TAPS - 1}", i))
                dve.tensor_copy(channel(conv31[:, :, :], i, 2, 1), acc[:, :]).then_inc(*ve.done("conv"))
                evac(4)
                evac(5)

            def out_tensor(pe, s, i, j, waits):
                for m in range(KD):
                    product(pe, s, i, j + m // 4, m % 4, yh, yl, waits)

            def adds_of(dve, s, i, j):
                def add(m):
                    a = (j + m // 4, m % 4)
                    dve.wait_ge(*tile_done(s, i, *a))
                    dve.tensor_tensor(xT[:, m, :], tile(s, *a), xT[:, m, :], ALU.add).then_inc(*taken(s, *a))
                return add

            def ln_tensor_mean(pe):
                pe.wait_ge(*ve.at("conv", GROUPS - 1))
                for k in range(KD):
                    last = pe.matmul(wbank(0), ones, conv31[:, k, :], start=k == 0, stop=k == KD - 1)
                last.then_inc(*tl.done("mean"))

            def ln_tensor_var(pe):
                for k in range(KD):
                    pe.wait_ge(*al.at(f"square {k}"))
                    pe.matmul(wbank(1), ones, sq[:, k % 2, :], start=k == 0, stop=k == KD - 1)\
                      .then_inc(*tl.done(f"sum {k}"))

            def ln_vector(dve):
                dve.wait_ge(*al.at("mean"))
                for k in range(KD):
                    dve.tensor_tensor(conv31[:, k, :], conv31[:, k, :], acc[:, :], ALU.subtract)\
                       .then_inc(*vl.done(f"centered {k}"))

            def ln_scalar(act):
                act.wait_ge(*tl.at("mean"))
                act.activation(acc[:, :], wbank(0), ACT.Copy, scale=1.0 / D).then_inc(*al.done("mean"))
                for k in range(KD):
                    if k >= 2:
                        act.wait_ge(*tl.at(f"sum {k - 2}"))
                    act.wait_ge(*vl.at(f"centered {k}"))
                    act.activation(sq[:, k % 2, :], conv31[:, k, :], ACT.Square).then_inc(*al.done(f"square {k}"))
                act.wait_ge(*tl.at(f"sum {KD - 1}"))
                act.activation(Rt[:, :], wbank(1), ACT.Ln, scale=1.0 / D, bias=bias[:, 3:4]).then_inc(*al.done("ln"))
                act.wait_ge(*al.at("ln"))
                act.activation(Rt[:, :], Rt[:, :], ACT.Exp, scale=-0.5).then_inc(*al.done("1/std"))

            def z_evac(dve, s, i, x):
                dve.wait_ge(*tile_done(s, i, x, 0))
                dve.tensor_tensor(gp[:, x, :], tile(s, x, 0), R[:, :], ALU.mult).then_inc(*taken(s, x, 0))

            def z_vector(dve, i):
                vz.turn()
                for x in range(2):
                    dve.tensor_tensor(stg[:, x, :], channel(conv31[:, :, :], i, 2, x), Rt[:, :], ALU.mult)\
                       .then_inc(*vz.done(f"normed {x}"))
                for x in range(2):
                    dve.wait_ge(*az.at(f"silu {x}", i))
                    dve.tensor_tensor(yf[:, x, :], stg[:, x, :], gs[:, x, :], ALU.mult).then_inc(*vz.done(f"y {x}"))
                    dve.wait_ge(*vz.at(f"y {x}", i))
                    dve.tensor_copy(yh[:, x, :], yf[:, x, :]).then_inc(*vz.done(f"y hi {x}"))
                    dve.wait_ge(*vz.at(f"y hi {x}", i))
                    dve.tensor_tensor(yl[:, x, :], yf[:, x, :], yh[:, x, :].bitcast(F32), ALU.subtract)\
                       .then_inc(*vz.done(f"y lo {x}"))

            def z_scalar(act, s, si, i):
                az.turn()
                act.wait_ge(*tile_taken(s, si, 1, 0))
                act.activation(gs[:, :, :], gp[:, :, :], ACT.Silu).then_inc(*az.done("silu z"))
                for x in range(2):
                    act.wait_ge(*vz.at(f"normed {x}", i))
                    act.activation(stg[:, x, :], stg[:, x, :], ACT.Silu, scale=at(lnw, i, 2, x), bias=at(lnb, i, 2, x))\
                       .then_inc(*az.done(f"silu {x}"))

            def tensor(pe):
                product(pe, dt_sec, 0, 0, 0, xh, xl, operand_waits(nv))

                def glu(i, last):
                    for j in range(4):
                        product(pe, glu_sec, i, j, 0, xh, xl)
                loop(pe, GROUPS, glu)
                dt_tensor(pe)
                for _ in in_pieces(pe, first_sec, 0):
                    pass

                def turn(i, last):
                    rest = in_pieces(pe, sec, i)
                    work_tensor(pe, i, lambda: next(rest, None))
                    for _ in rest:
                        pass
                    out_tensor(pe, sec, i, 6, [ve.at(f"y lo {k}", i) for k in range(2)])
                loop(pe, GROUPS - 1, turn)
                work_tensor(pe, GROUPS - 1, lambda: None)
                out_tensor(pe, last_sec, 0, 0, [ve.at(f"y lo {k}", GROUPS - 1) for k in range(2)])
                pe.wait_ge(*ae.at("ln y", GROUPS - 1))
                ln_tensor_mean(pe)
                for x in range(2):
                    product(pe, zf_sec, 0, x, 0, xh, xl)
                ln_tensor_var(pe)

                def zturn(i, last):
                    for x in range(2):
                        product(pe, z_sec, i, x, 0, xh, xl)
                    out_tensor(pe, z_sec, i, 2, [vz.at(f"y lo {k}", i) for k in range(2)])
                loop(pe, GROUPS - 1, zturn)
                out_tensor(pe, zl_sec, 0, 0, [vz.at(f"y lo {k}", GROUPS - 1) for k in range(2)])

            def scalar(act):
                hi_after(act, dt_sec, 0, 0, True)
                loop(act, GROUPS, lambda i, last: glu_scalar(act, i, last))
                dt_scalar(act)
                for j in range(6):
                    hi_after(act, first_sec, 0, j, True)
                prep_scalar(act, first_sec, 0, 0)

                def turn(i, last):
                    work_scalar(act, i, lambda j: hi_after(act, sec, i, j, last))
                    prep_scalar(act, sec, i, i + 1)
                    for j in (6, 7):
                        hi_after(act, sec, i, j, last)
                loop(act, GROUPS - 1, turn)
                work_scalar(act, GROUPS - 1, lambda j: None)
                for j in (0, 1):
                    hi_after(act, last_sec, 0, j, True)
                ln_scalar(act)
                for j in (0, 1):
                    hi_after(act, zf_sec, 0, j, True)
                z_scalar(act, zf_sec, 0, 0)

                def zturn(i, last):
                    for j in range(4):
                        hi_after(act, z_sec, i, j, last)
                    z_scalar(act, z_sec, i, i + 1)
                loop(act, GROUPS - 1, zturn)
                for j in (0, 1):
                    hi_after(act, zl_sec, 0, j, True)

            def vector(dve):
                dt_take(dve)
                loop(dve, GROUPS, lambda i, last: glu_vector(dve, i))
                dt_vector(dve)
                for t in range(6):
                    evac(dve, first_sec, 0, t)
                prep_vector(dve, first_sec, 0, 0)

                def turn(i, last):
                    work_vector(dve, i, lambda t: evac(dve, sec, i, t))
                    prep_vector(dve, sec, i, i + 1, adds_of(dve, sec, i, 6))
                loop(dve, GROUPS - 1, turn)
                work_vector(dve, GROUPS - 1, lambda t: None)
                for j in (0, 1):
                    add_to_x(dve, last_sec, 0, j, range(4 * j, 4 * j + 4))
                ln_vector(dve)
                for x in range(2):
                    z_evac(dve, zf_sec, 0, x)
                dve.wait_ge(*al.at("1/std"))
                z_vector(dve, 0)

                def zturn(i, last):
                    dve.wait_ge(*az.at("silu z", i))
                    for x in range(2):
                        z_evac(dve, z_sec, i, x)
                    for j in (2, 3):
                        add_to_x(dve, z_sec, i, j, range(4 * (j - 2), 4 * (j - 2) + 4))
                    z_vector(dve, i + 1)
                loop(dve, GROUPS - 1, zturn)
                for j in (0, 1):
                    add_to_x(dve, zl_sec, 0, j, range(4 * j, 4 * j + 4))

            def tables(act):
                act.wait_ge(*x_ready_before)
                act.dma_start(mU[:, :], T["gdn_masks"][:, 0:P]).then_inc(mask_in, 16)

            def sync(sp):
                for s in (dt_sec, glu_sec, first_sec, sec, last_sec, zf_sec, z_sec, zl_sec):
                    load_slots(s)(sp)

            def gpsimd(pool):
                for s in (dt_sec, glu_sec, first_sec, sec, last_sec, zf_sec, z_sec, zl_sec):
                    split_slots(s)(pool)

            x_ready.append(tile_taken(zl_sec, 0, 1, 3))
            me = {"sync": sync, "gpsimd": gpsimd, "scalar": scalar, "tensor": tensor, "vector": vector,
                  "steps": {"scalar": [ab, ag, ap_, ae, al, az], "tensor": [tb, te, tl],
                            "vector": [vbs, vg, vp, ve, vl, vz]}}
            return merge({"scalar": tables}, nv, me)

        def gdn_layer(n, l):
            nv = norm(n, param("norm_g1"))
            gate_sec, first_sec, sec, last_sec = f"gdn_ba{n}", f"gdn_first{n}", f"gdn{n}", f"gdn_last{n}"
            H, DK = 8, 128
            DV = 256
            pre = sb("pre", [P, 4, 3 + SEQ])
            gp = sb("gp", [P, 2, SEQ])
            gs = sb("gs", [P, 2, SEQ])
            stg = sb("stg", [P, 4, SEQ])
            qn, kn, vs = stg[:, 0, :], stg[:, 1, :], stg[:, 2:4, :]
            rqk = sb("rqk", [P, 2, SEQ])
            kbe = sb("kbe", [P, NCH, P])
            kdec = sb("kdec", [P, NCH, P])
            vb = sb("vb", [P, NCH, DV])
            d1 = sb("d1", [P, NCH, P])
            d2 = sb("d2", [P, NCH, P])
            eg = sb("eg", [P, SEQ])
            egl = sb("egl", [P, NCH])
            N = sb("N", [P, NCH, P])
            A = sb("A", [P, NCH, P])
            U = sb("U", [P, NCH, P])
            NA = sb("NA", [P, 2, NCH, P])
            NB = sb("NB", [P, 2, NCH, P])
            yh = sb("gyh", [P, 2, SEQ], F32R)
            yl = sb("gyl", [P, 2, SEQ], F32R)
            Q = sb("Q", [P, SEQ])
            Gm = sb("Gm", [8, SEQ])
            gcol = sb("gcol", [P, 4, H, NCH])
            dmax, dmin = d2, d1
            Y, Dinv = d1, d2
            nwT = NB[:, 0, :, :]
            vn = NB[:, 1, :, :].rearrange("p c n -> p (c n)").rearrange("p (b v) -> p b v", b=2)
            S = NA[:, 0, :, :].rearrange("p c n -> p (c n)").rearrange("p (b v) -> p b v", b=2)
            yf = vb[:, :, :].rearrange("p c v -> p (c v)").rearrange("p (d s) -> p d s", d=2)
            osq = NA[:, :, :, :].rearrange("p a c n -> p a (c n)")
            ro = U[:, :, :].rearrange("p c n -> p (c n)")
            tmp = [pre[:, x, 0:SEQ] for x in range(4)] + [gp[:, 0, :], gp[:, 1, :]]
            conv = param("gdn_conv")
            ng = param("gdn_norm_g")
            dtb, alog = param("gdn_dt_bias"), param("gdn_a_log")
            onesrow = sb("g_onesrow", [P, SEQ])
            masks = sb("g_masks", [P, 6, P])
            maskU, nstrict, bd16, mT = masks[:, 0, :], masks[:, 1, :], masks[:, 2, :], \
                [masks[:, 3 + s, :] for s in range(3)]
            masks_in = sem("gdn_masks_in")
            ab, tb, vbs = steps(f"gdn_gate{n}", "scalar", "tensor", "vector")
            ap_, tp, vp = steps(f"gdn_prep{n}", "scalar", "tensor", "vector")
            ae, te, ve = steps(sec, "scalar", "tensor", "vector")
            x_ready_before = x_ready[-1]

            def chunks(ap):
                return ap.rearrange("p (c n) -> p c n", c=NCH)

            def over(ap):
                return ap.unsqueeze(1).to_broadcast([P, NCH, P])

            def each(q, i, width=P):
                c = gcol[:, q, ds(i, 1), :] if not isinstance(i, int) else gcol[:, q, i:i + 1, :]
                return c.rearrange("p a c -> p (a c)").unsqueeze(2).to_broadcast([P, NCH, width])

            def colv(ap, i, per, k):
                return ap[:, ds(i * per + k, 1)] if not isinstance(i, int) else ap[:, i * per + k:i * per + k + 1]

            b8, a8 = slice(0, 8), slice(32, 40)

            def gate_vector(dve):
                dve.wait_ge(*tile_done(gate_sec, 0, 0, 0))
                dve.tensor_tensor(tmp[0], tile(gate_sec, 0, 0), R[:, :], ALU.mult).then_inc(*taken(gate_sec, 0, 0))
                dve.memset(onesrow[:, :], 1.0).then_inc(*vbs.done("ones"))
                dve.memset(Q[:, :], 0.0).then_inc(*vbs.done("Q zero"))
                dve.wait_ge(*tile_taken(gate_sec, 0, 0, 0))
                dve.tensor_scalar(tmp[1][a8], tmp[0][a8], dtb[a8], None, ALU.add).then_inc(*vbs.done("z"))
                dve.wait_ge(*ab.at("exp b"))
                dve.tensor_scalar(tmp[2][b8], tmp[2][b8], 1.0, None, ALU.add).then_inc(*vbs.done("1+exp"))
                dve.wait_ge(*vbs.at("1+exp"))
                dve.reciprocal(Q[b8, :], tmp[2][b8]).then_inc(*vbs.done("beta"))
                dve.wait_ge(*ab.at("exp z"))
                dve.tensor_scalar(tmp[3][a8], tmp[2][a8], 1.0, None, ALU.add).then_inc(*vbs.done("u"))
                dve.wait_ge(*vbs.at("u"))
                dve.tensor_scalar(tmp[4][a8], tmp[3][a8], -1.0, None, ALU.add).then_inc(*vbs.done("u-1"))
                dve.wait_ge(*vbs.at("u-1"))
                dve.tensor_scalar(tmp[5][a8], tmp[4][a8], 0.0, None, ALU.is_equal).then_inc(*vbs.done("is 0"))
                dve.wait_ge(*vbs.at("is 0"))
                dve.tensor_tensor(tmp[4][a8], tmp[4][a8], tmp[5][a8], ALU.add).then_inc(*vbs.done("den"))
                dve.wait_ge(*vbs.at("den"))
                dve.reciprocal(tmp[4][a8], tmp[4][a8]).then_inc(*vbs.done("1/den"))
                dve.wait_ge(*ab.at("ln u"))
                dve.wait_ge(*vbs.at("1/den"))
                dve.tensor_tensor(tmp[3][a8], tmp[3][a8], tmp[4][a8], ALU.mult).then_inc(*vbs.done("ln/den"))
                dve.wait_ge(*vbs.at("ln/den"))
                dve.tensor_tensor(tmp[3][a8], tmp[3][a8], tmp[5][a8], ALU.add).then_inc(*vbs.done("ratio"))
                dve.wait_ge(*vbs.at("ratio"))
                dve.tensor_tensor(tmp[3][a8], tmp[3][a8], tmp[2][a8], ALU.mult).then_inc(*vbs.done("log1p"))
                dve.wait_ge(*vbs.at("log1p"))
                dve.scalar_tensor_tensor(out=tmp[3][a8], in0=tmp[1][a8], scalar=0.0, in1=tmp[3][a8], op0=ALU.max,
                                         op1=ALU.add).then_inc(*vbs.done("softplus"))
                dve.wait_ge(*vbs.at("softplus"))
                dve.wait_ge(*ab.at("exp a"))
                dve.tensor_scalar(tmp[3][a8], tmp[3][a8], egl[a8, 0:1], -1.0, ALU.mult, ALU.mult)\
                   .then_inc(*vbs.done("g"))
                dve.wait_ge(*vbs.at("g"))
                for c in range(NCH):
                    s = slice(c * P, (c + 1) * P)
                    dve.tensor_tensor_scan(Q[a8, s], onesrow[a8, s], tmp[3][a8, s], 0.0, ALU.mult, ALU.add)\
                       .then_inc(*vbs.done(f"cumsum {c}"))
                for c in range(NCH):
                    s = slice(c * P, (c + 1) * P)
                    dve.wait_ge(*vbs.at(f"cumsum {c}"))
                    dve.tensor_scalar(tmp[4][a8, s], Q[a8, s], Q[a8, c * P + P - 1:(c + 1) * P], None, ALU.subtract)\
                       .then_inc(*vbs.done(f"g-last {c}"))
                dve.wait_ge(*ab.at("exp g"))
                dve.tensor_tensor(Q[64:72, :], Q[b8, :], tmp[1][b8], ALU.mult).then_inc(*vbs.done("beta exp g"))
                dve.wait_ge(*tb.at("columns"))
                dve.tensor_copy(gcol[:, :, :, :],
                                wbank(0).rearrange("p (c q h) -> p q h c", c=NCH, q=4)[:, :, 0:H, :])\
                   .then_inc(*vbs.done("columns"))
                dve.memset(pre[:, :, 0:3], 0.0).then_inc(*vbs.done("pads"))
                dve.wait_ge(*vbs.at("pads"))
                dve.wait_ge(masks_in, 16)

            def gate_scalar(act):
                hi_after(act, gate_sec, 0, 0, True)
                act.wait_ge(*vbs.at("z"))
                act.activation(tmp[2][a8], tmp[1][a8], ACT.Abs).then_inc(*ab.done("abs z"))
                act.activation(tmp[2][b8], tmp[0][b8], ACT.Exp, scale=-1.0).then_inc(*ab.done("exp b"))
                act.wait_ge(*ab.at("abs z"))
                act.activation(tmp[2][a8], tmp[2][a8], ACT.Exp, scale=-1.0).then_inc(*ab.done("exp z"))
                act.activation(egl[a8, 0:1], alog[a8], ACT.Exp).then_inc(*ab.done("exp a"))
                act.wait_ge(*vbs.at("u-1"))
                act.activation(tmp[3][a8], tmp[3][a8], ACT.Ln).then_inc(*ab.done("ln u"))
                act.wait_ge(*vbs.at("g-last 3"))
                act.activation(tmp[1][b8], Q[a8, :], ACT.Exp).then_inc(*ab.done("exp g"))
                act.activation(Q[96:104, :], tmp[4][a8], ACT.Exp, scale=-1.0).then_inc(*ab.done("exp last-g"))

            def gate_tensor(pe):
                product(pe, gate_sec, 0, 0, 0, xh, xl, operand_waits(nv))
                pe.wait_ge(*vbs.at("beta exp g"))
                pe.wait_ge(*ab.at("exp last-g"))
                for c in range(NCH):
                    last = pe.transpose(wbank(0)[:, c * P:(c + 1) * P], Q[:, c * P:(c + 1) * P], ident)
                last.then_inc(*tb.done("columns"))

            def evacuate(dve, s, i, t, h):
                j, m = t, 0
                dve.wait_ge(*tile_done(s, i, j, m))
                if t == 0:
                    dve.wait_ge(*ap_.at("silu gate", h, 1))
                dst = pre[:, t, 3:] if t < 4 else gp[:, t - 4, :]
                dve.tensor_tensor(dst, tile(s, j, m), R[:, :], ALU.mult).then_inc(*taken(s, j, m))

            def prep_vector(dve, s, i, h, adds=None):
                vp.turn()
                dve.wait_ge(*tile_taken(s, i, 3, 0))
                dve.wait_ge(*te.at("kq", h, 1))
                for tap in range(4):
                    for x in range(4):
                        w = colv(conv, h, 16, x * 4 + tap)
                        if tap == 0:
                            dve.tensor_scalar(stg[:, x, :], pre[:, x, 0:SEQ], w, None, ALU.mult)\
                               .then_inc(*vp.done(f"tap {tap} {x}"))
                        else:
                            dve.wait_ge(*vp.at(f"tap {tap - 1} {x}", h))
                            dve.scalar_tensor_tensor(out=stg[:, x, :], in0=pre[:, x, tap:tap + SEQ], scalar=w,
                                                     in1=stg[:, x, :], op0=ALU.mult, op1=ALU.add)\
                               .then_inc(*vp.done(f"tap {tap} {x}"))
                    if adds:
                        adds(2 * tap)
                        adds(2 * tap + 1)
                for x, name in ((1, "k"), (0, "q")):
                    dve.wait_ge(*ap_.at(f"1/norm {name}", h))
                    dve.tensor_tensor(stg[:, x, :], stg[:, x, :], rqk[:, x, :], ALU.mult)\
                       .then_inc(*vp.done(f"{name} normed"))

            def prep_scalar(act, h):
                ap_.turn()
                act.wait_ge(*te.at("v tokens", h, 1))
                for x in (1, 0, 2, 3):
                    act.wait_ge(*vp.at(f"tap 3 {x}", h))
                    act.activation(stg[:, x, :], stg[:, x, :], ACT.Silu).then_inc(*ap_.done(f"silu {x}"))
                act.wait_ge(*ve.at("y gated 1", h, 1))
                act.wait_ge(*gate_taken(h))
                act.activation(gs[:, :, :], gp[:, :, :], ACT.Silu).then_inc(*ap_.done("silu gate"))
                for x in (1, 0):
                    act.wait_ge(*ap_.at(f"silu {x}", h))
                    act.activation(sq[:, x, :], stg[:, x, :], ACT.Square).then_inc(*ap_.done(f"square {x}"))
                for x, name in ((1, "k"), (0, "q")):
                    s = DK if name == "q" else 1.0
                    act.wait_ge(*tp.at(f"sum {x}", h))
                    act.activation(rqk[:, x, :], wbank(x), ACT.Ln, scale=float(s), bias=bias[:, 1 - x:2 - x])\
                       .then_inc(*ap_.done(f"ln {name}"))
                for x, name in ((1, "k"), (0, "q")):
                    act.wait_ge(*ap_.at(f"ln {name}", h))
                    act.activation(rqk[:, x, :], rqk[:, x, :], ACT.Exp, scale=-0.5).then_inc(*ap_.done(f"1/norm {name}"))

            def gate_taken(h):
                if isinstance(h, int) and h == 0:
                    return tile_taken(first_sec, 0, 5, 0)
                return tile_taken(sec, h - 1, 5, 0)

            def prep_tensor(pe, h):
                tp.turn()
                pe.wait_ge(*ve.at("y gated 1", h, 1))
                for x in (1, 0):
                    pe.wait_ge(*ap_.at(f"square {x}", h))
                    pe.matmul(wbank(x), ones, sq[:, x, :], start=True, stop=True).then_inc(*tp.done(f"sum {x}"))

            def work_tensor(pe, i, more):
                te.turn()

                def four(b, left, right, name, start=True, stop=True):
                    for c in range(NCH):
                        last = pe.matmul(wbank(b)[:, c * P:(c + 1) * P], left[:, c, :], right[:, c, :],
                                         start=True, stop=True)
                    last.then_inc(*te.done(name))

                def four_transposes(b, src, name):
                    for c in range(NCH):
                        last = pe.transpose(wbank(b)[:, c * P:(c + 1) * P], src[:, c, :], ident)
                    last.then_inc(*te.done(name))

                knc, qnc = chunks(kn), chunks(qn)
                pe.wait_ge(*ve.at("G masked", i))
                pe.matmul(wbank(3), ones[0:8, :], Gm[:, :], start=True, stop=True).then_inc(*te.done("G row"))
                pe.wait_ge(*vp.at("k normed", i))
                four_transposes(0, knc, "k tokens")
                pe.wait_ge(*ap_.at("silu 3", i))
                for c in range(NCH):
                    for d in range(2):
                        at = (c % 2) * DV + d * P
                        last = pe.transpose(wbank(1 + c // 2)[:, at:at + P], vs[:, d, c * P:(c + 1) * P], ident)
                last.then_inc(*te.done("v tokens"))
                more()
                pe.wait_ge(*ve.at("k dec", i))
                four(0, knc, knc, "kk")
                pe.wait_ge(*ve.at("v beta 1", i))
                pe.wait_ge(*vp.at("q normed", i))
                four(1, knc, qnc, "kq")
                more()
                pe.wait_ge(*ve.at("N", i))
                four_transposes(2, N, "N transposed")
                more()
                pe.wait_ge(*ve.at("U1", i))
                Nt = NB[:, 0, :, :]
                four(0, Nt, N, "N2")
                pe.wait_ge(*ve.at("A", i))
                four(1, N, Nt, "N2 transposed")
                more()
                pe.wait_ge(*ve.at("N2", i))
                four(2, NA[:, 0], U, "U2")
                pe.wait_ge(*ve.at("N2 transposed", i))
                four(0, NA[:, 1], NA[:, 0], "N4")
                four(1, NA[:, 0], NA[:, 1], "N4 transposed")
                more()
                pe.wait_ge(*ae.at("N4", i))
                pe.wait_ge(*ve.at("U2", i))
                four(2, NB[:, 0], U, "U4")
                pe.wait_ge(*ve.at("N4 transposed", i))
                four(0, NB[:, 1], NB[:, 0], "N8")
                more()
                pe.wait_ge(*ae.at("N8", i))
                pe.wait_ge(*ve.at("U4", i))
                four(1, NA[:, 0], U, "U8")
                more()
                for s in range(3):
                    pe.wait_ge(*ve.at("U8" if s == 0 else f"U join {s - 1}", i))
                    four(0, N, U, f"join {s}")
                    four_transposes(2, U, f"U transposed {s}")
                    more()
                    pe.wait_ge(*ve.at(f"Y {s}", i))
                    pe.wait_ge(*ae.at(f"U transposed {s}", i))
                    four(1, Dinv, Y, f"joined {s}")
                    more()
                pe.wait_ge(*ve.at("U join 2", i))
                four(0, kbe, U, "w")
                for c in range(NCH):
                    if c >= 1:
                        pe.wait_ge(*ve.at(f"state {c - 1}", i))
                        pe.wait_ge(*ae.at("-w", i))
                    pe.matmul(wbank(1)[:, 0:DV], U[:, c, :], vb[:, c, :], start=True, stop=c == 0)\
                      .then_inc(*te.done(f"v new {c} a"))
                    if c:
                        pe.matmul(wbank(1)[:, 0:DV], nwT[:, c, :], S[:, (c - 1) % 2, :], start=False, stop=True)\
                          .then_inc(*te.done(f"v new {c}"))
                        for d in range(2):
                            pe.matmul(wbank(2 + d)[:, c * P:(c + 1) * P], S[:, (c - 1) % 2, d * P:(d + 1) * P],
                                      chunks(eg[:, :])[:, c, :], start=True, stop=False)
                            pe.wait_ge(*ve.at(f"v new {c}", i))
                            last = pe.matmul(wbank(2 + d)[:, c * P:(c + 1) * P], vn[:, c % 2, d * P:(d + 1) * P],
                                             A[:, c, :], start=False, stop=True)
                    else:
                        pe.wait_ge(*ve.at(f"v new {c}", i))
                        for d in range(2):
                            last = pe.matmul(wbank(2 + d)[:, c * P:(c + 1) * P], vn[:, c % 2, d * P:(d + 1) * P],
                                             A[:, c, :], start=True, stop=True)
                    last.then_inc(*te.done(f"o {c}"))
                    if c < NCH - 1:
                        if c == 0:
                            pe.wait_ge(*ae.at("-w", i))
                        pe.matmul(wbank(0)[:, 0:DV], kdec[:, c, :], vn[:, c % 2, :], start=True, stop=True)\
                          .then_inc(*te.done(f"state {c}"))
                    more()
                for d in range(2):
                    pe.wait_ge(*ae.at(f"o square {d}", i))
                    pe.matmul(wbank(1), ones, osq[:, d, :], start=d == 0, stop=d == 1).then_inc(*te.done(f"o sum {d}"))

            def work_scalar(act, i, between):
                ae.turn()
                act.wait_ge(*te.at("G row", i))
                act.activation(eg[:, :], wbank(3), ACT.Exp).then_inc(*ae.done("exp G"))
                act.wait_ge(*ve.at("d min", i))
                act.activation(dmin[:, :, :], dmin[:, :, :], ACT.Exp).then_inc(*ae.done("E1"))
                act.wait_ge(*ve.at("d max", i))
                act.activation(dmax[:, :, :], dmax[:, :, :], ACT.Exp, scale=-1.0).then_inc(*ae.done("E2"))
                between(0)
                act.wait_ge(*te.at("N4", i))
                act.activation(NB[:, 0, :, :], chunks(wbank(0)), ACT.Copy).then_inc(*ae.done("N4"))
                act.wait_ge(*te.at("N8", i))
                act.activation(NA[:, 0, :, :], chunks(wbank(0)), ACT.Copy).then_inc(*ae.done("N8"))
                for s in range(3):
                    act.wait_ge(*te.at(f"U transposed {s}", i))
                    act.activation(Dinv[:, :, :], chunks(wbank(2)), ACT.Copy).then_inc(*ae.done(f"U transposed {s}"))
                    if s != 1:
                        between(1 if s == 0 else 2)
                act.wait_ge(*te.at("w", i))
                act.activation(nwT, chunks(wbank(0)), ACT.Copy, scale=-1.0).then_inc(*ae.done("-w"))
                between(3)
                act.wait_ge(*te.at("o 3", i))
                for d in range(2):
                    act.activation(osq[:, d, :], wbank(2 + d), ACT.Square).then_inc(*ae.done(f"o square {d}"))
                act.wait_ge(*te.at("o sum 1", i))
                act.activation(ro, wbank(1), ACT.Ln, scale=1.0 / DV, bias=bias[:, 0:1]).then_inc(*ae.done("ln o"))
                act.wait_ge(*ae.at("ln o", i))
                act.activation(ro, ro, ACT.Exp, scale=-0.5).then_inc(*ae.done("1/rms o"))
                between(4)
                between(5)

            def work_vector(dve, i, evac):
                ve.turn()
                dve.tensor_scalar(Gm[:, :], Q[a8, :], ident[a8, ds(i + 32, 1)] if not isinstance(i, int) else
                                  ident[a8, 32 + i:33 + i], None, ALU.mult).then_inc(*ve.done("G masked"))
                dve.wait_ge(*ae.at("exp G", i))
                dve.tensor_tensor(d1[:, :, :], chunks(wbank(3)), each(1, i), ALU.subtract).then_inc(*ve.done("d"))
                dve.wait_ge(*ve.at("d", i))
                dve.tensor_scalar(d2[:, :, :], d1[:, :, :], 0.0, None, ALU.max).then_inc(*ve.done("d max"))
                dve.wait_ge(*ve.at("d max", i))
                dve.tensor_scalar(d1[:, :, :], d1[:, :, :], 0.0, None, ALU.min).then_inc(*ve.done("d min"))
                dve.wait_ge(*te.at("k tokens", i))
                dve.tensor_tensor(kbe[:, :, :], chunks(wbank(0)), each(2, i), ALU.mult).then_inc(*ve.done("k beta"))
                dve.tensor_tensor(kdec[:, :, :], chunks(wbank(0)), each(3, i), ALU.mult).then_inc(*ve.done("k dec"))
                dve.wait_ge(*te.at("v tokens", i))
                for h in range(2):
                    c = gcol[:, 0, ds(i, 1), 2 * h:2 * h + 2] if not isinstance(i, int) else \
                        gcol[:, 0, i:i + 1, 2 * h:2 * h + 2]
                    dve.tensor_tensor(vb[:, 2 * h:2 * h + 2, :], wbank(1 + h).rearrange("p (c v) -> p c v", c=2),
                                      c.rearrange("p a c -> p (a c)").unsqueeze(2).to_broadcast([P, 2, DV]),
                                      ALU.mult).then_inc(*ve.done(f"v beta {h}"))
                dve.wait_ge(*ae.at("E2", i))
                dve.tensor_tensor(d2[:, :, :], d2[:, :, :], over(nstrict), ALU.mult).then_inc(*ve.done("E2 masked"))
                dve.tensor_tensor(d1[:, :, :], d1[:, :, :], over(maskU), ALU.mult).then_inc(*ve.done("E1 masked"))
                dve.wait_ge(*ve.at("E2 masked", i))
                dve.tensor_tensor(d2[:, :, :], d2[:, :, :], each(0, i), ALU.mult).then_inc(*ve.done("E2 beta"))
                dve.wait_ge(*te.at("kk", i))
                dve.wait_ge(*ve.at("E2 beta", i))
                dve.tensor_tensor(N[:, :, :], chunks(wbank(0)), d2[:, :, :], ALU.mult).then_inc(*ve.done("N"))
                dve.wait_ge(*te.at("kq", i))
                dve.tensor_tensor(A[:, :, :], chunks(wbank(1)), d1[:, :, :], ALU.mult).then_inc(*ve.done("A"))
                dve.wait_ge(*ae.at("exp G", i))
                dve.tensor_copy(egl[:, :], eg[:, P - 1::P]).then_inc(*ve.done("exp G last"))
                dve.wait_ge(*te.at("N transposed", i))
                dve.tensor_tensor(NB[:, 0, :, :], chunks(wbank(2)), over(bd16), ALU.mult).then_inc(*ve.done("Nt"))
                dve.wait_ge(*ve.at("Nt", i))
                dve.tensor_tensor(U[:, :, :], NB[:, 0, :, :], over(ident), ALU.add).then_inc(*ve.done("U1"))
                dve.tensor_tensor(eg[:, :], qn, eg[:, :], ALU.mult).then_inc(*ve.done("q exp g"))
                dve.wait_ge(*te.at("N2", i))
                dve.tensor_tensor(NA[:, 0, :, :], chunks(wbank(0)), over(bd16), ALU.mult).then_inc(*ve.done("N2"))
                dve.wait_ge(*te.at("N2 transposed", i))
                dve.tensor_tensor(NA[:, 1, :, :], chunks(wbank(1)), over(bd16), ALU.mult)\
                   .then_inc(*ve.done("N2 transposed"))
                evac(0)
                dve.wait_ge(*te.at("U2", i))
                dve.wait_ge(*ve.at("N2 transposed", i))
                dve.tensor_tensor(U[:, :, :], U[:, :, :], chunks(wbank(2)), ALU.add).then_inc(*ve.done("U2"))
                dve.wait_ge(*te.at("N4 transposed", i))
                dve.tensor_copy(NB[:, 1, :, :], chunks(wbank(1))).then_inc(*ve.done("N4 transposed"))
                dve.wait_ge(*te.at("U4", i))
                dve.tensor_tensor(U[:, :, :], U[:, :, :], chunks(wbank(2)), ALU.add).then_inc(*ve.done("U4"))
                dve.wait_ge(*te.at("U8", i))
                dve.wait_ge(*ve.at("U4", i))
                dve.tensor_tensor(U[:, :, :], U[:, :, :], chunks(wbank(1)), ALU.add).then_inc(*ve.done("U8"))
                for s in range(3):
                    dve.wait_ge(*te.at(f"join {s}", i))
                    dve.tensor_tensor(Y[:, :, :], chunks(wbank(0)), over(mT[s]), ALU.mult).then_inc(*ve.done(f"Y {s}"))
                    if s != 1:
                        evac(1 if s == 0 else 2)
                    dve.wait_ge(*te.at(f"joined {s}", i))
                    dve.tensor_tensor(U[:, :, :], U[:, :, :], chunks(wbank(1)), ALU.add)\
                       .then_inc(*ve.done(f"U join {s}"))
                for c in range(NCH):
                    dve.wait_ge(*te.at(f"v new {c}" if c else "v new 0 a", i))
                    dve.tensor_copy(vn[:, c % 2, :], wbank(1)[:, 0:DV]).then_inc(*ve.done(f"v new {c}"))
                    if c < NCH - 1:
                        dve.wait_ge(*te.at(f"state {c}", i))
                        if c == 0:
                            dve.tensor_copy(S[:, 0, :], wbank(0)[:, 0:DV]).then_inc(*ve.done("state 0"))
                        else:
                            dve.wait_ge(*ve.at(f"state {c - 1}", i))
                            dve.scalar_tensor_tensor(out=S[:, c % 2, :], in0=S[:, (c - 1) % 2, :],
                                                     scalar=egl[:, c:c + 1], in1=wbank(0)[:, 0:DV],
                                                     op0=ALU.mult, op1=ALU.add).then_inc(*ve.done(f"state {c}"))
                    if c == 2:
                        evac(3)
                dve.wait_ge(*te.at("o 3", i))
                dve.wait_ge(*ap_.at("silu gate", i))
                for d in range(2):
                    dve.wait_ge(*ae.at(f"o square {d}", i))
                    dve.scalar_tensor_tensor(out=yf[:, d, :], in0=wbank(2 + d), scalar=ng[:, d:d + 1],
                                             in1=gs[:, d, :], op0=ALU.mult, op1=ALU.mult)\
                       .then_inc(*ve.done(f"y gated {d}"))
                dve.wait_ge(*ae.at("1/rms o", i))
                for d in range(2):
                    dve.wait_ge(*ve.at(f"y gated {d}", i))
                    dve.tensor_tensor(yf[:, d, :], yf[:, d, :], ro, ALU.mult).then_inc(*ve.done(f"y {d}"))
                for d in range(2):
                    dve.wait_ge(*ve.at(f"y {d}", i))
                    dve.tensor_copy(yh[:, d, :], yf[:, d, :]).then_inc(*ve.done(f"y hi {d}"))
                for d in range(2):
                    dve.wait_ge(*ve.at(f"y hi {d}", i))
                    dve.tensor_tensor(yl[:, d, :], yf[:, d, :], yh[:, d, :].bitcast(F32), ALU.subtract)\
                       .then_inc(*ve.done(f"y lo {d}"))
                evac(4)
                evac(5)

            def pieces(pe, s, i):
                for t in range(6):
                    for k in range(0, KD, 2):
                        product(pe, s, i, t, 0, xh, xl, None, k, k + 2)
                        yield

            def out_tensor(pe, s, i, h, j):
                for m in range(KD):
                    product(pe, s, i, j + m // 4, m % 4, yh, yl, [ve.at(f"y lo {k}", h) for k in range(2)])

            def adds_of(dve, s, i, j):
                def add(m):
                    at = (j + m // 4, m % 4)
                    dve.wait_ge(*tile_done(s, i, *at))
                    dve.tensor_tensor(xT[:, m, :], tile(s, *at), xT[:, m, :], ALU.add).then_inc(*taken(s, *at))
                return add

            def tensor(pe):
                gate_tensor(pe)
                for _ in pieces(pe, first_sec, 0):
                    pass
                prep_tensor(pe, 0)

                def turn(i, last):
                    rest = pieces(pe, sec, i)
                    work_tensor(pe, i, lambda: next(rest, None))
                    for _ in rest:
                        pass
                    out_tensor(pe, sec, i, i, 6)
                    prep_tensor(pe, i + 1)
                loop(pe, H - 1, turn)
                work_tensor(pe, H - 1, lambda: None)
                out_tensor(pe, last_sec, 0, H - 1, 0)

            def scalar(act):
                gate_scalar(act)
                for j in range(6):
                    hi_after(act, first_sec, 0, j, True)
                prep_scalar(act, 0)

                def turn(i, last):
                    work_scalar(act, i, lambda k: hi_after(act, sec, i, k, last))
                    prep_scalar(act, i + 1)
                    for j in (6, 7):
                        hi_after(act, sec, i, j, last)
                loop(act, H - 1, turn)
                work_scalar(act, H - 1, lambda k: None)
                for j in (0, 1):
                    hi_after(act, last_sec, 0, j, True)

            def vector(dve):
                gate_vector(dve)
                for t in range(6):
                    evacuate(dve, first_sec, 0, t, 0)
                prep_vector(dve, first_sec, 0, 0)

                def turn(i, last):
                    work_vector(dve, i, lambda t: evacuate(dve, sec, i, t, i + 1))
                    prep_vector(dve, sec, i, i + 1, adds_of(dve, sec, i, 6))
                loop(dve, H - 1, turn)
                work_vector(dve, H - 1, lambda t: None)
                for j in (0, 1):
                    add_to_x(dve, last_sec, 0, j, range(4 * j, 4 * j + 4))

            def tables(act):
                act.wait_ge(*x_ready_before)
                act.dma_start(masks[:, :, :], T["gdn_masks"].rearrange("p (k n) -> p k n", k=6)).then_inc(masks_in, 16)

            def sync(sp):
                for s in (gate_sec, first_sec, sec, last_sec):
                    load_slots(s)(sp)

            def gpsimd(pool):
                for s in (gate_sec, first_sec, sec, last_sec):
                    split_slots(s)(pool)

            x_ready.append(tile_taken(last_sec, 0, 1, 3))
            me = {"sync": sync, "gpsimd": gpsimd, "scalar": scalar, "tensor": tensor, "vector": vector,
                  "steps": {"scalar": [ab, ap_, ae], "tensor": [tb, tp, te], "vector": [vbs, vp, ve]}}
            return merge({"scalar": tables}, nv, me)

        def rotary_tables(dve, act, st, sa, which, pos_i, cosT, sinT, tmp, inv, engine):
            a, k, m = tmp
            if engine == "vector":
                dve.tensor_copy(a, pos_i).then_inc(*st.done("pos"))
                dve.wait_ge(*st.at("pos"))
                dve.tensor_scalar(a, a, inv, None, ALU.mult).then_inc(*st.done("angle"))
                dve.wait_ge(*st.at("angle"))
                dve.tensor_scalar(k, a, 1.0 / (2 * math.pi), ROUND, ALU.mult, ALU.add).then_inc(*st.done("turns a"))
                dve.wait_ge(*st.at("turns a"))
                dve.tensor_scalar(k, k, -ROUND, None, ALU.add).then_inc(*st.done("turns"))
                dve.wait_ge(*st.at("turns"))
                for x, part in enumerate(TWO_PI):
                    dve.scalar_tensor_tensor(out=a, in0=k, scalar=-part, in1=a, op0=ALU.mult, op1=ALU.add)\
                       .then_inc(*st.done(f"less {x}"))
                    dve.wait_ge(*st.at(f"less {x}"))
                dve.tensor_scalar(a, a, PI_BELOW, -PI_BELOW, ALU.min, ALU.max).then_inc(*st.done("r"))
            else:
                act.wait_ge(*st.at("r"))
                act.activation(m, a, ACT.Abs).then_inc(*sa.done("|r|"))
                act.activation(sinT, a, ACT.Sin).then_inc(*sa.done("sin"))
                act.wait_ge(*sa.at("|r|"))
                act.activation(cosT, m, ACT.Sin, scale=-1.0, bias=bias[:, 2:3]).then_inc(*sa.done("cos"))

        def mla_layer(n, l):
            nv = norm(n, param("norm_g2"))
            c_sec, first_sec, sec, last_sec = f"mla_c{n}", f"mla_first{n}", f"mla{n}", f"mla_last{n}"
            PAIRS, CQ, CKV = 8, 6, 4
            SCALE = 192 ** -0.5
            qh = sb("cqh", [P, CQ, SEQ], F32R)
            ql = sb("cql", [P, CQ, SEQ], F32R)
            kh = sb("ckvh", [P, CKV, SEQ], F32R)
            kl = sb("ckvl", [P, CKV, SEQ], F32R)
            cosT = sb("cosT", [P, SEQ])
            sinT = sb("sinT", [P, SEQ])
            kr = sb("kr", [P, SEQ])
            mk = sb("mk", [P, 2, P])
            rot, causal = mk[:, 0, :], mk[:, 1, :]
            mxs = sb("mxs", [P, 8])
            nmx = sb("nmx", [P, 8])
            rs = sb("rs", [P, 8])
            ri = sb("ri", [P, 8])
            work = sb("mwork", [P, 20 * SEQ])

            def part(at, k):
                return work[:, at * SEQ:(at + k) * SEQ].rearrange("p (k s) -> p k s", s=SEQ)
            qn, kn, qrz, vT = part(0, 2), part(2, 2), part(4, 2), part(6, 2)
            gs, vt = part(8, 2), part(10, 2)
            vt = vt.rearrange("p k (c v) -> p (k c) v", v=2 * P)
            prob = work[:, 12 * SEQ:17 * SEQ].rearrange("p (h n) -> p h n", h=2)
            pT = work[:, 17 * SEQ:17 * SEQ + 1280]
            c = part(0, CQ + CKV)
            pos_i = part(12, 1)[:, 0, :].bitcast(I32)
            tmp = [part(13, 1)[:, 0, :], part(14, 1)[:, 0, :], part(15, 1)[:, 0, :]]
            krx = part(16, 1)[:, 0, :]
            rc = [part(17, 1)[:, 0, :], part(18, 1)[:, 0, :]]
            yh = sb("myh", [P, 2, SEQ], F32R)
            yl = sb("myl", [P, 2, SEQ], F32R)
            xr, xt = sq[:, 0, :], sq[:, 1, :]
            pos_in = sem("mla_pos_in")
            gq, gkv = param("mla_q_norm_g"), param("mla_kv_norm_g")
            ab, tb, vbs = steps(f"mla_c{n}", "scalar", "tensor", "vector")
            ap_, tp, vp = steps(f"mla_prep{n}", "scalar", "tensor", "vector")
            ae, te, ve = steps(sec, "scalar", "tensor", "vector")
            x_ready_before = x_ready[-1]
            TILES = [(0, 0), (0, 1), (1, 0), (1, 1), (2, 0), (3, 0), (4, 0), (5, 0), (6, 0)]
            KV = range(0, CKV)
            off_q = [sum(range(t + 1)) * P for t in range(NCH)]
            off_k = [sum(NCH - u for u in range(t)) * P for t in range(NCH)]

            def c_slot(t):
                return t if t < CKV else t + 1

            def c_vector(dve):
                dve.wait_ge(pos_in, 32)
                rotary_tables(dve, None, vbs, ab, "vector", pos_i, cosT[:, :], sinT[:, :], tmp, param("mla_inv"),
                              "vector")

                def take(t):
                    dve.wait_ge(*tile_done(c_sec, 0, c_slot(t), 0))
                    dve.tensor_tensor(c[:, t, :], tile(c_sec, c_slot(t), 0), R[:, :], ALU.mult)\
                       .then_inc(*taken(c_sec, c_slot(t), 0))

                def operand(t):
                    q = t >= CKV
                    hi, lo = (qh[:, t - CKV, :], ql[:, t - CKV, :]) if q else (kh[:, t, :], kl[:, t, :])
                    g = gq[:, t - CKV:t - CKV + 1] if q else gkv[:, t:t + 1]
                    dve.scalar_tensor_tensor(out=c[:, t, :], in0=c[:, t, :], scalar=g, in1=rc[q],
                                             op0=ALU.mult, op1=ALU.mult).then_inc(*vbs.done(f"c {t}"))
                    dve.wait_ge(*vbs.at(f"c {t}"))
                    dve.tensor_copy(hi, c[:, t, :]).then_inc(*vbs.done(f"c hi {t}"))
                    dve.wait_ge(*vbs.at(f"c hi {t}"))
                    dve.tensor_tensor(lo, c[:, t, :], hi.bitcast(F32), ALU.subtract).then_inc(*vbs.done(f"c lo {t}"))

                for t in range(CKV):
                    take(t)
                dve.wait_ge(*tile_done(c_sec, 0, CKV, 0))
                dve.tensor_tensor(krx, tile(c_sec, CKV, 0), R[:, :], ALU.mult).then_inc(*taken(c_sec, CKV, 0))
                dve.wait_ge(*ab.at("1/rms kv"))
                for t in range(CKV):
                    take(CKV + t)
                    operand(t)
                dve.wait_ge(*tile_taken(c_sec, 0, CKV, 0))
                dve.wait_ge(*ab.at("cos"))
                dve.tensor_tensor(kr[:, :], krx, cosT[:, :], ALU.mult).then_inc(*vbs.done("k cos"))
                dve.wait_ge(*vbs.at("k cos"))
                dve.wait_ge(*tb.at("k rotated"))
                dve.tensor_tensor(krx, wbank(2), sinT[:, :], ALU.mult).then_inc(*vbs.done("k sin"))
                dve.wait_ge(*vbs.at("k sin"))
                dve.tensor_tensor(kr[:, :], kr[:, :], krx, ALU.add).then_inc(*vbs.done("k rope"))
                for t in range(2 * CKV, CQ + CKV):
                    take(t)
                dve.wait_ge(*ab.at("1/rms q"))
                for t in range(CKV, CQ + CKV):
                    operand(t)
                dve.wait_ge(*vbs.at(f"c lo {CQ + CKV - 1}"))
                dve.memset(qrz[:, :, :], 0.0).then_inc(*vbs.done("q rope 0"))
                dve.wait_ge(*vbs.at("q rope 0"))

            def c_scalar(act):
                rotary_tables(None, act, vbs, ab, "scalar", pos_i, cosT[:, :], sinT[:, :], tmp, None, "scalar")
                for j in range(CKV + 1 + CQ):
                    hi_after(act, c_sec, 0, j, True)
                    if j == CKV:
                        continue
                    t = j if j < CKV else j - 1
                    if t >= 2:
                        act.wait_ge(*tb.at(f"sum {t - 2}"))
                    act.wait_ge(*tile_taken(c_sec, 0, j, 0))
                    act.activation(sq[:, t % 2, :], c[:, t, :], ACT.Square).then_inc(*ab.done(f"square {t}"))
                    if t in (CKV - 1, CKV + CQ - 1):
                        q = t >= CKV
                        act.wait_ge(*tb.at(f"sum {t}"))
                        act.activation(Rt[:, :], wbank(int(q)), ACT.Ln, scale=1.0 / ((CQ if q else CKV) * P),
                                       bias=bias[:, 0:1]).then_inc(*ab.done(f"ln {t}"))
                        act.wait_ge(*ab.at(f"ln {t}"))
                        act.activation(rc[q], Rt[:, :], ACT.Exp, scale=-0.5)\
                           .then_inc(*ab.done("1/rms q" if q else "1/rms kv"))

            def c_tensor(pe):
                def total(t):
                    q = t >= CKV
                    pe.wait_ge(*ab.at(f"square {t}"))
                    pe.matmul(wbank(int(q)), ones, sq[:, t % 2, :], start=t in (0, CKV), stop=t in (CKV - 1, CKV + CQ - 1))\
                      .then_inc(*tb.done(f"sum {t}"))
                for j in range(CKV + 1 + CQ):
                    product(pe, c_sec, 0, j, 0, xh, xl, operand_waits(nv) if j == 0 else None)
                    if 1 <= j <= CKV:
                        total(j - 1)
                    elif j > CKV + 1:
                        total(j - 2)
                    if j == CKV + 2:
                        pe.wait_ge(*tile_taken(c_sec, 0, CKV, 0))
                        pe.matmul(wbank(2), rot, krx, start=True, stop=True).then_inc(*tb.done("k rotated"))
                total(CKV + CQ - 1)

            def in_pieces(pe, s, i, waits=False):
                for t, (j, m) in enumerate(TILES):
                    nk = W.sec[s]["items"][j][0]
                    hi, lo = (kh, kl) if j < 2 else (qh, ql) if j < 5 else (xh, xl)
                    w = None
                    if waits and j < 5:
                        w = [vbs.at(f"c lo {k + (0 if j < 2 else CKV)}") for k in range(nk)]
                    for k in range(0, nk, 2):
                        product(pe, s, i, j, m, hi, lo, w, k, k + 2)
                        yield

            def evac_scalar(act, s, i, t):
                j, m = TILES[t]
                act.wait_ge(*tile_done(s, i, j, m))
                dst = [vT[:, 0, :], vT[:, 1, :], kn[:, 0, :], kn[:, 1, :], qn[:, 0, :], qn[:, 1, :], xr][t]
                act.activation(dst, tile(s, j, m), ACT.Copy).then_inc(*taken(s, j, m))

            def evac_gate(dve, s, i, x):
                j, m = TILES[7 + x]
                dve.wait_ge(*tile_done(s, i, j, m))
                dve.tensor_tensor(gs[:, x, :], tile(s, j, m), R[:, :], ALU.mult).then_inc(*taken(s, j, m))

            def prep_tensor(pe, s, i, h):
                tp.turn()
                pe.wait_ge(*tile_taken(s, i, *TILES[6]))
                pe.wait_ge(*ve.at("y 1", h, 1))
                pe.matmul(wbank(2), rot, xr, start=True, stop=True).then_inc(*tp.done("rotated"))

            def prep_vector(dve, s, i, h):
                vp.turn()
                dve.wait_ge(*tile_taken(s, i, *TILES[6]))
                dve.tensor_tensor(xt, xr, cosT[:, :], ALU.mult).then_inc(*vp.done("cos"))
                dve.wait_ge(*tp.at("rotated", h))
                dve.tensor_tensor(Rt[:, :], wbank(2), sinT[:, :], ALU.mult).then_inc(*vp.done("sin"))
                dve.wait_ge(*vp.at("sin", h))
                for x in range(2):
                    r = slice(64 * x, 64 * x + 64)
                    dve.tensor_tensor(qrz[r, x, :], xt[r, :], Rt[r, :], ALU.add).then_inc(*vp.done(f"q rope {x}"))

            def prep_scalar(act, s, i, h):
                ap_.turn()
                act.wait_ge(*tile_taken(s, i, *TILES[7]))
                act.wait_ge(*tile_taken(s, i, *TILES[8]))
                act.activation(gs[:, :, :], gs[:, :, :], ACT.Silu).then_inc(*ap_.done("silu"))

            def work_tensor(pe, s, i, h, more):
                te.turn()
                pe.wait_ge(*vp.at("q rope 1", h))
                for cc in range(NCH):
                    for d in range(2):
                        at = (cc % 2) * 2 * P + d * P
                        last = pe.transpose(wbank(cc // 2)[:, at:at + P], vT[:, d, cc * P:(cc + 1) * P], ident)
                last.then_inc(*te.done("v tokens"))
                for x in range(2 * NCH):
                    hd, t = x // NCH, x % NCH
                    b, w = x % 4, (t + 1) * P
                    if x < 2:
                        pe.wait_ge(*ae.at(f"v {x}", i))
                    elif x >= NCH:
                        pe.wait_ge(*ae.at(f"exp {x - NCH}", i))
                    q = slice(t * P, (t + 1) * P)
                    pe.matmul(wbank(b)[:, 0:w], qn[:, hd, q], kn[:, hd, 0:w], start=True, stop=False)
                    pe.matmul(wbank(b)[:, 0:w], qrz[:, hd, q], kr[:, 0:w], start=False, stop=False)
                    pe.matmul(wbank(b)[:, t * P:w], ident, causal, start=False, stop=True)\
                      .then_inc(*te.done(f"scores {x}"))
                    more()
                for hd in range(2):
                    for t in range(NCH):
                        b = t % 3
                        if t == 3:
                            pe.wait_ge(*ve.at(f"p transposed {hd} 0", i))
                        elif hd:
                            pe.wait_ge(*ve.at("p transposed 0 3", i))
                        elif t == 0:
                            pe.wait_ge(*ae.at("exp 7", i))
                        for u in range(t, NCH):
                            if t == 0 and hd == 0:
                                pe.wait_ge(*ve.at(f"p {hd * NCH + u}", i))
                            a = off_q[u] + t * P
                            last = pe.transpose(wbank(b)[:, (u - t) * P:(u - t + 1) * P],
                                                prob[:, hd, a:a + P], ident)
                        last.then_inc(*te.done(f"p transposed {hd} {t}"))
                    more()
                    more()
                    for t in range(NCH):
                        pe.wait_ge(*ve.at(f"p transposed {hd} {t}", i))
                        last = pe.matmul(wbank(3)[:, t * P:], vt[:, t, hd * P:(hd + 1) * P],
                                         pT[:, off_k[t]:off_k[t] + (NCH - t) * P], start=t == 0, stop=t == NCH - 1)
                    last.then_inc(*te.done(f"o {hd}"))
                    more()

            def work_scalar(act, i, evac, after):
                ae.turn()
                act.wait_ge(*te.at("v tokens", i))
                for x in range(2):
                    act.activation(vt[:, 2 * x:2 * x + 2, :], wbank(x).rearrange("p (c v) -> p c v", c=2), ACT.Copy)\
                       .then_inc(*ae.done(f"v {x}"))
                for x in range(2 * NCH):
                    hd, t = x // NCH, x % NCH
                    w = (t + 1) * P
                    act.wait_ge(*ve.at(f"max {x}", i))
                    act.activation(prob[:, hd, off_q[t]:off_q[t] + w], wbank(x % 4)[:, 0:w], ACT.Exp, scale=SCALE,
                                   bias=nmx[:, x:x + 1], accum_out=rs[:, x:x + 1]).then_inc(*ae.done(f"exp {x}"))
                    if x == NCH - 1:
                        evac(0)
                        evac(1)
                        after(0)
                for t in range(2, 4):
                    evac(t)
                after(1)
                for t in (4, 5, 6):
                    evac(t)
                    after(t - 2)

            def work_vector(dve, i, evac):
                ve.turn()

                def normalize(x):
                    hd, t = x // NCH, x % NCH
                    s = slice(off_q[t], off_q[t] + (t + 1) * P)
                    dve.wait_ge(*ae.at(f"exp {x}", i))
                    dve.reciprocal(ri[:, x:x + 1], rs[:, x:x + 1]).then_inc(*ve.done(f"1/sum {x}"))
                    dve.wait_ge(*ve.at(f"1/sum {x}", i))
                    dve.tensor_scalar(prob[:, hd, s], prob[:, hd, s], ri[:, x:x + 1], None, ALU.mult)\
                       .then_inc(*ve.done(f"p {x}"))
                for x in range(2 * NCH):
                    w = (x % NCH + 1) * P
                    dve.wait_ge(*te.at(f"scores {x}", i))
                    dve.reduce_max(mxs[:, x:x + 1], wbank(x % 4)[:, 0:w], AX.X).then_inc(*ve.done(f"max raw {x}"))
                    dve.wait_ge(*ve.at(f"max raw {x}", i))
                    dve.tensor_scalar(nmx[:, x:x + 1], mxs[:, x:x + 1], -SCALE, None, ALU.mult)\
                       .then_inc(*ve.done(f"max {x}"))
                    if x:
                        normalize(x - 1)
                normalize(2 * NCH - 1)
                for hd in range(2):
                    for t in range(NCH):
                        w = (NCH - t) * P
                        dve.wait_ge(*te.at(f"p transposed {hd} {t}", i))
                        dve.tensor_copy(pT[:, off_k[t]:off_k[t] + w], wbank(t % 3)[:, 0:w])\
                           .then_inc(*ve.done(f"p transposed {hd} {t}"))
                    dve.wait_ge(*te.at(f"o {hd}", i))
                    if hd == 0:
                        dve.wait_ge(*ap_.at("silu", i))
                    dve.tensor_tensor(prob[:, hd, 0:SEQ], wbank(3), gs[:, hd, :], ALU.mult).then_inc(*ve.done(f"y {hd}"))
                    dve.wait_ge(*ve.at(f"y {hd}", i))
                    dve.tensor_copy(yh[:, hd, :], prob[:, hd, 0:SEQ]).then_inc(*ve.done(f"y hi {hd}"))
                    dve.wait_ge(*ve.at(f"y hi {hd}", i))
                    dve.tensor_tensor(yl[:, hd, :], prob[:, hd, 0:SEQ], yh[:, hd, :].bitcast(F32), ALU.subtract)\
                       .then_inc(*ve.done(f"y lo {hd}"))
                evac(0)
                evac(1)

            def out_tensor(pe, s, i, h, j):
                for m in range(KD):
                    product(pe, s, i, j + m // 4, m % 4, yh, yl, [ve.at(f"y lo {k}", h) for k in range(2)])

            def tensor(pe):
                c_tensor(pe)
                for _ in in_pieces(pe, first_sec, 0, True):
                    pass
                prep_tensor(pe, first_sec, 0, 0)

                def turn(i, last):
                    rest = in_pieces(pe, sec, i)
                    work_tensor(pe, sec, i, i, lambda: next(rest, None))
                    for _ in rest:
                        pass
                    prep_tensor(pe, sec, i, i + 1)
                    out_tensor(pe, sec, i, i, 7)
                loop(pe, PAIRS - 1, turn)
                work_tensor(pe, None, PAIRS - 1, PAIRS - 1, lambda: None)
                out_tensor(pe, last_sec, 0, PAIRS - 1, 0)

            def scalar(act):
                c_scalar(act)
                act.wait_ge(*vbs.at("q rope 0"))
                for t in range(7):
                    evac_scalar(act, first_sec, 0, t)
                    if TILES[t][1] == W.sec[first_sec]["items"][TILES[t][0]][1] - 1:
                        hi_after(act, first_sec, 0, TILES[t][0], True)
                for j in (5, 6):
                    hi_after(act, first_sec, 0, j, True)
                prep_scalar(act, first_sec, 0, 0)

                def turn(i, last):
                    work_scalar(act, i, lambda t: evac_scalar(act, sec, i, t),
                                lambda j: hi_after(act, sec, i, j, last))
                    for j in (5, 6):
                        hi_after(act, sec, i, j, last)
                    prep_scalar(act, sec, i, i + 1)
                    for j in (7, 8):
                        hi_after(act, sec, i, j, last)
                loop(act, PAIRS - 1, turn)
                work_scalar(act, PAIRS - 1, lambda t: None, lambda j: None)
                for j in (0, 1):
                    hi_after(act, last_sec, 0, j, True)

            def vector(dve):
                c_vector(dve)
                for x in range(2):
                    evac_gate(dve, first_sec, 0, x)
                prep_vector(dve, first_sec, 0, 0)

                def turn(i, last):
                    work_vector(dve, i, lambda x: evac_gate(dve, sec, i, x))
                    prep_vector(dve, sec, i, i + 1)
                    for j in (7, 8):
                        add_to_x(dve, sec, i, j, range(4 * (j - 7), 4 * (j - 7) + 4))
                loop(dve, PAIRS - 1, turn)
                work_vector(dve, PAIRS - 1, lambda x: None)
                for j in (0, 1):
                    add_to_x(dve, last_sec, 0, j, range(4 * j, 4 * j + 4))

            def tables(act):
                act.wait_ge(*x_ready_before)
                act.dma_start(pos_i, T["positions"].to_broadcast([P, SEQ])).then_inc(pos_in, 16)
                act.dma_start(mk[:, :, :], T["mla_masks"].rearrange("p (k n) -> p k n", k=2)).then_inc(pos_in, 16)

            def sync(sp):
                for s in (c_sec, first_sec, sec, last_sec):
                    load_slots(s)(sp)

            def gpsimd(pool):
                for s in (c_sec, first_sec, sec, last_sec):
                    split_slots(s)(pool)

            x_ready.append(tile_taken(last_sec, 0, 1, 3))
            me = {"sync": sync, "gpsimd": gpsimd, "scalar": scalar, "tensor": tensor, "vector": vector,
                  "steps": {"scalar": [ab, ap_, ae], "tensor": [tb, tp, te], "vector": [vbs, vp, ve]}}
            return merge({"scalar": tables}, nv, me)

        def odd_layer(n, l):
            nv = norm(n, param("c_norm_w"))
            first_sec, sec, last_sec = f"odd_first{n}", f"odd{n}", f"odd_last{n}"
            PAIRS, TILE_K = 4, KD
            SCALE = 64 ** -0.5
            LAM0 = 0.8 - 0.6 * math.exp(-0.3 * 1)
            cosT = sb("o_cosT", [P, SEQ])
            sinT = sb("o_sinT", [P, SEQ])
            mk = sb("o_mk", [P, 3, P])
            rot, allowed, halves = mk[:, 0, :], mk[:, 1, :], mk[:, 2, :]
            mxs, nmx, rs, ri = (sb(f"o_{name}", [P, 16]) for name in ("mxs", "nmx", "rs", "ri"))
            lam = sb("o_lam", [P, 8])
            xq = sb("o_xq", [P, 4, SEQ])
            rr = sb("o_rr", [P, 4, SEQ])
            qz = sb("o_qz", [P, 2, 2, SEQ])
            kn = sb("o_kn", [P, 2, SEQ])
            vT = sb("o_vT", [P, 2, SEQ])
            vt = sb("o_vt", [P, NCH, 2 * P])
            gs = sb("o_gs", [P, 2, SEQ])
            prob = sb("o_prob", [P, 2, 1280])
            p1 = sb("o_p1", [P, 2, SEQ])
            pT = sb("o_pT", [P, 1280])
            yf = sb("o_yf", [P, 2, SEQ])
            yh = sb("o_yh", [P, 2, SEQ], F32R)
            yl = sb("o_yl", [P, 2, SEQ], F32R)
            pos_i = pT[:, 0:SEQ].bitcast(I32)
            tmp = [rr[:, 0, :], rr[:, 1, :], rr[:, 2, :]]
            pos_in = sem("odd_pos_in")
            wq, wk, subln = param("c_q_norm_w"), param("c_k_norm_w"), param("c_subln_w")
            lams = param("c_lams")
            ab, tb, vbs = steps(f"odd_tables{n}", "scalar", "tensor", "vector")
            ap_, tp, vp = steps(f"odd_prep{n}", "scalar", "tensor", "vector")
            ae, te, ve = steps(sec, "scalar", "tensor", "vector")
            x_ready_before = x_ready[-1]
            off_q = [sum(range(t + 1)) * P for t in range(NCH)]
            off_k = [sum(NCH - u for u in range(t)) * P for t in range(NCH)]
            X = [(hd, t, m) for hd in range(2) for t in range(NCH) for m in range(2)]

            def tables_vector(dve):
                dve.memset(qz[:, :, :, :], 0.0).then_inc(*vbs.done("q 0"))
                dve.wait_ge(pos_in, 32)
                rotary_tables(dve, None, vbs, ab, "vector", pos_i, cosT[:, :], sinT[:, :], tmp, param("odd_inv"),
                              "vector")
                dve.tensor_tensor(lam[0:64, 0:2], lams[0:64, 0:2], lams[0:64, 2:4], ALU.mult)\
                   .then_inc(*vbs.done("lq lk"))
                dve.tensor_scalar(lam[:, 4:5], subln, 1.0 - LAM0, None, ALU.mult).then_inc(*vbs.done("subln"))
                dve.wait_ge(*ab.at("exp"))
                dve.tensor_tensor(lam[:, 5:6], lam[:, 3:4], lam[:, 2:3], ALU.subtract).then_inc(*vbs.done("diff"))
                dve.wait_ge(*vbs.at("diff"))
                dve.tensor_scalar(lam[:, 6:7], lam[:, 5:6], -LAM0, None, ALU.add).then_inc(*vbs.done("-lam"))
                dve.wait_ge(*vbs.at("-lam"))
                dve.wait_ge(*ab.at("cos"))

            def tables_scalar(act):
                rotary_tables(None, act, vbs, ab, "scalar", pos_i, cosT[:, :], sinT[:, :], tmp, None, "scalar")
                act.wait_ge(*tb.at("lam"))
                act.activation(lam[:, 2:4], wbank(1)[:, 0:2], ACT.Exp).then_inc(*ab.done("exp"))

            def tables_tensor(pe):
                pe.wait_ge(*vbs.at("lq lk"))
                pe.matmul(wbank(1)[:, 0:2], ones[0:64, :], lam[0:64, 0:2], start=True, stop=True)\
                  .then_inc(*tb.done("lam"))

            def in_pieces(pe, s, i, waits=None):
                for t in range(8):
                    for k in range(0, KD, 2):
                        product(pe, s, i, t, 0, xh, xl, waits if t == 0 else None, k, k + 2)
                        yield

            def evac(dve, s, i, t):
                dve.wait_ge(*tile_done(s, i, t, 0))
                dst = [vT[:, 0, :], vT[:, 1, :]] + [xq[:, x, :] for x in range(4)] + [gs[:, 0, :], gs[:, 1, :]]
                dve.tensor_tensor(dst[t], tile(s, t, 0), R[:, :], ALU.mult).then_inc(*taken(s, t, 0))

            def prep_tensor_a(pe, h):
                tp.turn()
                pe.wait_ge(*ve.at("y gated 1", h, 1))
                for x in range(4):
                    pe.wait_ge(*ap_.at(f"square {x}", h))
                    pe.matmul(wbank(x), halves, rr[:, x, :], start=True, stop=True).then_inc(*tp.done(f"sum {x}"))

            def prep_tensor_b(pe, h):
                for x in range(4):
                    pe.wait_ge(*vp.at(f"normed {x}", h))
                    pe.matmul(wbank(x), rot, xq[:, x, :], start=True, stop=True).then_inc(*tp.done(f"rotated {x}"))

            def prep_scalar(act, s, i, h):
                ap_.turn()
                for x in range(4):
                    act.wait_ge(*tile_taken(s, i, 2 + x, 0))
                    if x == 0:
                        act.wait_ge(*vp.at("rope 3", h, 1))
                    act.activation(rr[:, x, :], xq[:, x, :], ACT.Square).then_inc(*ap_.done(f"square {x}"))
                for x in range(4):
                    act.wait_ge(*tp.at(f"sum {x}", h))
                    act.activation(rr[:, x, :], wbank(x), ACT.Ln, scale=1.0 / 64, bias=bias[:, 0:1])\
                       .then_inc(*ap_.done(f"ln {x}"))
                for x in range(4):
                    act.wait_ge(*ap_.at(f"ln {x}", h))
                    act.activation(rr[:, x, :], rr[:, x, :], ACT.Exp, scale=-0.5).then_inc(*ap_.done(f"1/rms {x}"))
                for x in range(2):
                    act.wait_ge(*tile_taken(s, i, 6 + x, 0))
                act.activation(gs[:, :, :], gs[:, :, :], ACT.Silu).then_inc(*ap_.done("silu"))

            def prep_vector_a(dve, h):
                vp.turn()
                for x in range(4):
                    dve.wait_ge(*ap_.at(f"1/rms {x}", h))
                    dve.scalar_tensor_tensor(out=xq[:, x, :], in0=xq[:, x, :], scalar=(wk, wq)[x // 2],
                                             in1=rr[:, x, :], op0=ALU.mult, op1=ALU.mult)\
                       .then_inc(*vp.done(f"normed {x}"))

            def prep_vector_b(dve, h):
                for x in range(4):
                    if x == 0:
                        dve.wait_ge(*vp.at("normed 3", h))
                    dve.tensor_tensor(rr[:, x, :], xq[:, x, :], cosT[:, :], ALU.mult).then_inc(*vp.done(f"cos {x}"))
                    dve.wait_ge(*tp.at(f"rotated {x}", h))
                    dve.wait_ge(*vp.at(f"cos {x}", h))
                    dve.tensor_tensor(xq[:, x, :], wbank(x), sinT[:, :], ALU.mult).then_inc(*vp.done(f"sin {x}"))
                    dve.wait_ge(*vp.at(f"sin {x}", h))
                    if x < 2:
                        last = dve.tensor_tensor(kn[:, x, :], rr[:, x, :], xq[:, x, :], ALU.add)
                    else:
                        for m in range(2):
                            r = slice(64 * m, 64 * m + 64)
                            last = dve.tensor_tensor(qz[r, x - 2, m, :], rr[r, x, :], xq[r, x, :], ALU.add)
                            if m == 0:
                                last.then_inc(*vp.done(f"rope a {x}"))
                    last.then_inc(*vp.done(f"rope {x}"))

            def work_tensor(pe, i, more):
                te.turn()
                pe.wait_ge(*vp.at("rope 3", i))
                for cc in range(NCH):
                    for d in range(2):
                        at = (cc % 2) * 2 * P + d * P
                        last = pe.transpose(wbank(cc // 2)[:, at:at + P], vT[:, d, cc * P:(cc + 1) * P], ident)
                last.then_inc(*te.done("v tokens"))
                for x, (hd, t, m) in enumerate(X):
                    b, w = x % 4, (t + 1) * P
                    if x < 2:
                        pe.wait_ge(*ae.at(f"v {x}", i))
                    elif x >= 4:
                        pe.wait_ge(*ae.at(f"exp {x - 4}", i))
                    pe.matmul(wbank(b)[:, 0:w], qz[:, hd, m, t * P:w], kn[:, hd, 0:w], start=True, stop=False)
                    pe.matmul(wbank(b)[:, t * P:w], ident, allowed, start=False, stop=True)\
                      .then_inc(*te.done(f"scores {x}"))
                    more()
                for hd in range(2):
                    for t in range(NCH):
                        b = t % 3
                        if t == 3:
                            pe.wait_ge(*ve.at(f"p transposed {hd} 0", i))
                        elif hd:
                            pe.wait_ge(*ve.at("p transposed 0 3", i))
                            if t == 2:
                                pe.wait_ge(*ae.at("o ln 0", i))
                        elif t == 0:
                            pe.wait_ge(*ae.at("exp 15", i))
                        for u in range(t, NCH):
                            if t == 0 and hd == 0:
                                pe.wait_ge(*ve.at(f"p {2 * u + 1}", i))
                            a = off_q[u] + t * P
                            last = pe.transpose(wbank(b)[:, (u - t) * P:(u - t + 1) * P],
                                                prob[:, hd, a:a + P], ident)
                        last.then_inc(*te.done(f"p transposed {hd} {t}"))
                    more()
                    more()
                    for t in range(NCH):
                        pe.wait_ge(*ve.at(f"p transposed {hd} {t}", i))
                        last = pe.matmul(wbank(3)[:, t * P:], vt[:, t, hd * P:(hd + 1) * P],
                                         pT[:, off_k[t]:off_k[t] + (NCH - t) * P], start=t == 0, stop=t == NCH - 1)
                    last.then_inc(*te.done(f"o {hd}"))
                    more()
                    pe.wait_ge(*ae.at(f"o square {hd}", i))
                    pe.matmul(wbank(2), ones, yf[:, hd, :], start=True, stop=True).then_inc(*te.done(f"o sum {hd}"))
                    more()

            def work_scalar(act, i, after):
                ae.turn()
                act.wait_ge(*te.at("v tokens", i))
                for x in range(2):
                    act.activation(vt[:, 2 * x:2 * x + 2, :], wbank(x).rearrange("p (c v) -> p c v", c=2), ACT.Copy)\
                       .then_inc(*ae.done(f"v {x}"))
                for x, (hd, t, m) in enumerate(X):
                    w = (t + 1) * P
                    dst = p1[:, t % 2, 0:w] if m else prob[:, hd, off_q[t]:off_q[t] + w]
                    act.wait_ge(*ve.at(f"max {x}", i))
                    act.activation(dst, wbank(x % 4)[:, 0:w], ACT.Exp, scale=SCALE,
                                   bias=nmx[:, x:x + 1], accum_out=rs[:, x:x + 1]).then_inc(*ae.done(f"exp {x}"))
                    if x in (5, 9, 13):
                        after((x - 5) // 4)
                after(3)
                for hd in range(2):
                    act.wait_ge(*te.at(f"o {hd}", i))
                    act.activation(yf[:, hd, :], wbank(3), ACT.Square).then_inc(*ae.done(f"o square {hd}"))
                    act.wait_ge(*te.at(f"o sum {hd}", i))
                    act.activation(ro, wbank(2), ACT.Ln, scale=1.0 / P, bias=bias[:, 0:1])\
                       .then_inc(*ae.done(f"o ln {hd}"))
                    act.wait_ge(*ae.at(f"o ln {hd}", i))
                    act.activation(ro, ro, ACT.Exp, scale=-0.5).then_inc(*ae.done(f"1/rms o {hd}"))
                for j in range(4, 8):
                    after(j)

            ro = sq[:, 0, :]

            def work_vector(dve, i, evac):
                ve.turn()

                def normalize(x):
                    hd, t, m = X[x]
                    w = (t + 1) * P
                    s = slice(off_q[t], off_q[t] + w)
                    dve.wait_ge(*ae.at(f"exp {x}", i))
                    dve.reciprocal(ri[:, x:x + 1], rs[:, x:x + 1]).then_inc(*ve.done(f"1/sum {x}"))
                    dve.wait_ge(*ve.at(f"1/sum {x}", i))
                    if m == 0:
                        dve.tensor_scalar(prob[:, hd, s], prob[:, hd, s], ri[:, x:x + 1], None, ALU.mult)\
                           .then_inc(*ve.done(f"p {x}"))
                    else:
                        dve.tensor_scalar(ri[:, x:x + 1], ri[:, x:x + 1], lam[:, 6:7], None, ALU.mult)\
                           .then_inc(*ve.done(f"lam/sum {x}"))
                        dve.wait_ge(*ve.at(f"lam/sum {x}", i))
                        dve.scalar_tensor_tensor(out=prob[:, hd, s], in0=p1[:, t % 2, 0:w], scalar=ri[:, x:x + 1],
                                                 in1=prob[:, hd, s], op0=ALU.mult, op1=ALU.add)\
                           .then_inc(*ve.done(f"p {x}"))
                for x, (hd, t, m) in enumerate(X):
                    w = (t + 1) * P
                    dve.wait_ge(*te.at(f"scores {x}", i))
                    dve.reduce_max(mxs[:, x:x + 1], wbank(x % 4)[:, 0:w], AX.X).then_inc(*ve.done(f"max raw {x}"))
                    dve.wait_ge(*ve.at(f"max raw {x}", i))
                    dve.tensor_scalar(nmx[:, x:x + 1], mxs[:, x:x + 1], -SCALE, None, ALU.mult)\
                       .then_inc(*ve.done(f"max {x}"))
                    if x:
                        normalize(x - 1)
                    if x % 4 == 3:
                        evac(x // 4)
                normalize(15)
                for hd in range(2):
                    for t in range(NCH):
                        w = (NCH - t) * P
                        dve.wait_ge(*te.at(f"p transposed {hd} {t}", i))
                        dve.tensor_copy(pT[:, off_k[t]:off_k[t] + w], wbank(t % 3)[:, 0:w])\
                           .then_inc(*ve.done(f"p transposed {hd} {t}"))
                    if hd == 0:
                        dve.wait_ge(*ap_.at("silu", i))
                    dve.wait_ge(*te.at(f"o sum {hd}", i))
                    dve.scalar_tensor_tensor(out=yf[:, hd, :], in0=wbank(3), scalar=lam[:, 4:5], in1=gs[:, hd, :],
                                             op0=ALU.mult, op1=ALU.mult).then_inc(*ve.done(f"y gated {hd}"))
                    dve.wait_ge(*ve.at(f"y gated {hd}", i))
                    dve.wait_ge(*ae.at(f"1/rms o {hd}", i))
                    dve.tensor_tensor(yf[:, hd, :], yf[:, hd, :], ro, ALU.mult).then_inc(*ve.done(f"y {hd}"))
                    dve.wait_ge(*ve.at(f"y {hd}", i))
                    dve.tensor_copy(yh[:, hd, :], yf[:, hd, :]).then_inc(*ve.done(f"y hi {hd}"))
                    dve.wait_ge(*ve.at(f"y hi {hd}", i))
                    dve.tensor_tensor(yl[:, hd, :], yf[:, hd, :], yh[:, hd, :].bitcast(F32), ALU.subtract)\
                       .then_inc(*ve.done(f"y lo {hd}"))
                for t in range(4, 8):
                    evac(t)

            def out_half(pe, s, i, h, j):
                for m in range(4):
                    product(pe, s, i, j, m, yh, yl, [ve.at(f"y lo {k}", h) for k in range(2)])

            def tensor(pe):
                tables_tensor(pe)
                for _ in in_pieces(pe, first_sec, 0, operand_waits(nv)):
                    pass
                prep_tensor_a(pe, 0)
                prep_tensor_b(pe, 0)

                def turn(i, last):
                    rest = in_pieces(pe, sec, i)
                    work_tensor(pe, i, lambda: next(rest, None))
                    for _ in rest:
                        pass
                    prep_tensor_a(pe, i + 1)
                    out_half(pe, sec, i, i, 8)
                    prep_tensor_b(pe, i + 1)
                    out_half(pe, sec, i, i, 9)
                loop(pe, PAIRS - 1, turn)
                work_tensor(pe, PAIRS - 1, lambda: None)
                for j in range(2):
                    out_half(pe, last_sec, 0, PAIRS - 1, j)

            def scalar(act):
                tables_scalar(act)
                for j in range(8):
                    hi_after(act, first_sec, 0, j, True)
                prep_scalar(act, first_sec, 0, 0)

                def turn(i, last):
                    work_scalar(act, i, lambda j: hi_after(act, sec, i, j, last))
                    prep_scalar(act, sec, i, i + 1)
                    for j in (8, 9):
                        hi_after(act, sec, i, j, last)
                loop(act, PAIRS - 1, turn)
                work_scalar(act, PAIRS - 1, lambda j: None)
                for j in (0, 1):
                    hi_after(act, last_sec, 0, j, True)

            def vector(dve):
                tables_vector(dve)
                for t in range(8):
                    evac(dve, first_sec, 0, t)
                prep_vector_a(dve, 0)
                prep_vector_b(dve, 0)

                def turn(i, last):
                    work_vector(dve, i, lambda t: evac(dve, sec, i, t))
                    prep_vector_a(dve, i + 1)
                    add_to_x(dve, sec, i, 8, range(0, 4))
                    prep_vector_b(dve, i + 1)
                    add_to_x(dve, sec, i, 9, range(4, 8))
                loop(dve, PAIRS - 1, turn)
                work_vector(dve, PAIRS - 1, lambda t: None)
                for j in (0, 1):
                    add_to_x(dve, last_sec, 0, j, range(4 * j, 4 * j + 4))

            def tables(act):
                act.wait_ge(*x_ready_before)
                act.dma_start(pos_i, T["positions_2"].to_broadcast([P, SEQ])).then_inc(pos_in, 16)
                act.dma_start(mk[:, :, :], T["odd_masks"].rearrange("p (k n) -> p k n", k=3)).then_inc(pos_in, 16)

            def sync(sp):
                for s in (first_sec, sec, last_sec):
                    load_slots(s)(sp)

            def gpsimd(pool):
                for s in (first_sec, sec, last_sec):
                    split_slots(s)(pool)

            x_ready.append(tile_taken(last_sec, 0, 1, 3))
            me = {"sync": sync, "gpsimd": gpsimd, "scalar": scalar, "tensor": tensor, "vector": vector,
                  "steps": {"scalar": [ab, ap_, ae], "tensor": [tb, tp, te], "vector": [vbs, vp, ve]}}
            return merge({"scalar": tables}, nv, me)

        STAGE = {"load": load_x, "pool": pool_layer, "gdn": gdn_layer, "mla": mla_layer, "even": even_layer, "odd": odd_layer,
                
                 "final": final_norm, "store": store_x}
        stages = []
        small = []

        small.append((cst[:, :], T["consts"]))
        small.append((par[:, :], T["params"]))

        for n, (kind, j) in enumerate(plan):
            with ExitStack() as mine:
                area[0] = mine
                stages.append(STAGE[kind](n, j))
            area[0] = top

        def credit(eng, engine):
            for st in stages:
                for s in st.get("steps", {}).get(engine, []):
                    eng.sem_inc(s.sem, s.counts.get("per turn", 1))

        block = top.enter_context(nc.Block())

        @block.sync
        def _(sp):
            for dst, src in small:
                sp.dma_start(dst, src).then_inc(consts_in, 16)
            for st in stages:
                if "sync" in st:
                    st["sync"](sp)

        @block.gpsimd
        def _(pool):
            for q in range(RING):
                pool.sem_inc(lo_ready[q], 1)
            for k, value in enumerate(BIASES):
                pool.memset(bias[:, k:k + 1], value).then_inc(consts_in, 1)
            credit(pool, "gpsimd")
            for st in stages:
                if "gpsimd" in st:
                    st["gpsimd"](pool)

        @block.scalar
        def _(act):
            credit(act, "scalar")
            act.wait_ge(consts_in, 16 * len(small) + len(BIASES))
            for first in W.at_start:
                slot_hi(act, *first)
            for st in stages:
                if "scalar" in st:
                    st["scalar"](act)

        @block.vector
        def _(dve):
            for b in range(BANKS):
                dve.sem_inc(bank_taken[b], 1)
            credit(dve, "vector")
            dve.wait_ge(consts_in, 16 * len(small) + len(BIASES))
            for st in stages:
                if "vector" in st:
                    st["vector"](dve)

        @block.tensor
        def _(pe):
            for q in range(RING):
                pe.sem_inc(slot_used[q], 1)
            credit(pe, "tensor")
            pe.wait_ge(consts_in, 16 * len(small) + len(BIASES))
            for st in stages:
                if "tensor" in st:
                    st["tensor"](pe)


MLA_IN = [(4, 2)] * 2 + [(6, 1)] * 3 + [(8, 1)] * 2
SLOTS = {
    "pool": [("pool", 4, [(8, 1)] * 8 + [(4, 2)] * 6)],
    "gdn": [("gdn_ba", 1, [(8, 1)]), ("gdn_first", 1, [(8, 1)] * 6), ("gdn", 7, [(8, 1)] * 6 + [(2, 4)] * 2),
            ("gdn_last", 1, [(2, 4)] * 2)],
    "mla": [("mla_c", 1, [(8, 1)] * 11), ("mla_first", 1, MLA_IN), ("mla", 7, MLA_IN + [(2, 4)] * 2),
            ("mla_last", 1, [(2, 4)] * 2)],
    "even": [("ev_dt", 1, [(8, 1)]), ("ev_glu", 4, [(8, 1)] * 4), ("ev_first", 1, [(8, 1)] * 6),
             ("ev_ssd", 3, [(8, 1)] * 6 + [(2, 4)] * 2), ("ev_last", 1, [(2, 4)] * 2),
             ("ev_zfirst", 1, [(8, 1)] * 2), ("ev_z", 3, [(8, 1)] * 2 + [(2, 4)] * 2),
             ("ev_zlast", 1, [(2, 4)] * 2)],
    "odd": [("odd_first", 1, [(8, 1)] * 8), ("odd", 3, [(8, 1)] * 8 + [(2, 4)] * 2),
            ("odd_last", 1, [(2, 4)] * 2)],
}


def tiles(w, n=P):
    for c in range(0, w.shape[1], n):
        yield w[:, c:c + n]


def slot_sources(kind, l, A):
    if kind == "pool":
        w_in, w_grp, w_out = A["pool_w_in"][l], A["pool_w_grp"][l], A["pool_w_out"][l]
        for g in range(4):
            yield from tiles(w_in[:, g * 512:(g + 1) * 512])
            yield from tiles(w_in[:, 2048 + g * 512:2048 + (g + 1) * 512])
            yield from tiles(w_grp[g], 256)
            yield from tiles(w_out[g * 512:(g + 1) * 512], 256)
    if kind == "gdn":
        w, out = A["gdn_w_in"][l], A["gdn_w_out"][l]

        def head(h):
            yield w[:, h * 128:h * 128 + 128]
            yield w[:, 1024 + h * 128:1152 + h * 128]
            yield from tiles(w[:, 2048 + h * 256:2304 + h * 256])
            yield from tiles(w[:, 4096 + h * 256:4352 + h * 256])

        ba = np.zeros((D, P), np.float32)
        ba[:, 0:8], ba[:, 32:40] = w[:, 6144:6152], w[:, 6152:6160]
        yield ba
        yield from head(0)
        for h in range(7):
            yield from head(h + 1)
            yield from tiles(out[h * 256:(h + 1) * 256], 512)
        yield from tiles(out[7 * 256:], 512)
    if kind == "mla":
        w, uq, ukv, out = A["mla_w_in"][l], A["mla_w_uq"][l], A["mla_w_ukv"][l], A["mla_w_out"][l]

        def pair(t):
            a, b = 2 * t, 2 * t + 1
            for c in (128, 0):
                yield np.concatenate([ukv[:, h * 256 + c:h * 256 + c + 128] for h in (a, b)], axis=1)
            for h in (a, b):
                yield uq[:, h * 192:h * 192 + 128]
            yield np.concatenate([uq[:, h * 192 + 128:h * 192 + 192] for h in (a, b)], axis=1)
            yield from tiles(w[:, 1344 + t * 256:1344 + (t + 1) * 256])

        yield from tiles(w[:, 768:1280])
        yield np.concatenate([w[:, 1280:1344]] * 2, axis=1)
        yield from tiles(w[:, 0:768])
        yield from pair(0)
        for t in range(7):
            yield from pair(t + 1)
            yield from tiles(out[t * 256:(t + 1) * 256], 512)
        yield from tiles(out[7 * 256:], 512)
    if kind == "even":
        w, out = A["a_w_in_2"][l], A["a_w_out_2"][l]

        def group(g):
            yield from tiles(w[:, 1024 + g * 256:1024 + (g + 1) * 256])
            yield w[:, 2048 + g * 128:2048 + (g + 1) * 128]
            yield w[:, 2560 + g * 128:2560 + (g + 1) * 128]
            yield from tiles(w[:, g * 256:(g + 1) * 256])

        yield w[:, 3072:3200]
        for t in range(8):
            yield w[:, 3088 + t * 128:3088 + (t + 1) * 128]
            yield w[:, 4112 + t * 128:4112 + (t + 1) * 128]
        yield from group(0)
        for g in range(4):
            if g < 3:
                yield from group(g + 1)
            yield from tiles(out[g * 256:(g + 1) * 256], 512)
        yield from tiles(w[:, 5136:5136 + 256])
        for g in range(4):
            if g < 3:
                yield from tiles(w[:, 5136 + (g + 1) * 256:5136 + (g + 2) * 256])
            yield from tiles(out[1024 + g * 256:1024 + (g + 1) * 256], 512)
    if kind == "odd":
        w, out = A["c_w_in_2"][l], A["c_w_out_2"][l]

        def heads(t):
            for c in (2048, 1024, 0, 3072):
                yield from tiles(w[:, c + t * 256:c + (t + 1) * 256])

        yield from heads(0)
        for t in range(3):
            yield from heads(t + 1)
            yield from tiles(out[t * 256:(t + 1) * 256], 512)
        yield from tiles(out[3 * 256:], 512)


def lay_out_weights(layers, A):
    seen, slots = {}, []
    for kind in layers:
        l = seen[kind] = seen.get(kind, -1) + 1
        shapes = [s for _, iters, items in SLOTS.get(kind, []) for _ in range(iters) for s in items]
        parts = list(slot_sources(kind, l, A)) if shapes else []
        assert len(parts) == len(shapes)
        for (nk, nm), w in zip(shapes, parts):
            assert w.shape == (nk * P, nm * P), (kind, w.shape, nk, nm)
            slot = np.zeros((P, SLOT), np.float32)
            slot[:, :nk * nm * P] = w.reshape(nk, P, nm * P).transpose(1, 0, 2).reshape(P, -1)
            slots.append(slot)
    return np.stack(slots) if slots else np.zeros((1, P, SLOT), np.float32)


def columns(v):
    v = np.asarray(v, np.float32)
    lead = int(np.prod(v.shape[:-1]))
    return v.reshape(lead, -1, P).transpose(2, 0, 1).reshape(P, -1)


def small_parameters(A):
    out = {}
    for k in range(4):
        out[f"norm_g{k}"] = columns(A["norm_g"][k])
    for l in range(2):
        out[f"pool_scale{l}"] = columns(A["pool_scale"][l])
    out["final_g"] = columns(A["final_g"])
    taps = A["gdn_conv"][0].reshape(4, 32, P)
    out["gdn_conv"] = np.concatenate(
        [taps[:, t].T for h in range(8) for t in (h, 8 + h, 16 + 2 * h, 17 + 2 * h)], axis=1)
    out["gdn_norm_g"] = columns(A["gdn_norm_g"][0])
    out["mla_q_norm_g"] = columns(A["mla_q_norm_g"][0])
    out["mla_kv_norm_g"] = columns(A["mla_kv_norm_g"][0])
    r = np.arange(P)
    out["mla_inv"] = (10000.0 ** (-(r % 32) / 32.0)).astype(np.float32).reshape(P, 1)
    out["c_norm_w"] = columns(A["c_norm_w_2"][0])
    out["odd_inv"] = np.where(r % 64 < 16, 500000.0 ** (-2.0 * (r % 8) / 16.0), 0.0).astype(np.float32).reshape(P, 1)
    for name in ("c_q_norm_w", "c_k_norm_w"):
        out[name] = np.concatenate([A[name + "_2"][0]] * 2).reshape(P, 1)
    out["c_subln_w"] = columns(A["c_subln_w_2"][0])
    out["c_lams"] = np.zeros((P, 4), np.float32)
    for k, name in enumerate(("c_lq1_2", "c_lq2_2", "c_lk1_2", "c_lk2_2")):
        out["c_lams"][0:64, k] = A[name][0]
    out["a_norm_w"] = columns(A["a_norm_w_2"][0])
    for name in ("a_dt_bias", "a_a_log"):
        out[name] = np.zeros((P, 1), np.float32)
        out[name][0:16, 0] = A[name + "_2"][0]
    taps = np.concatenate([A["a_conv_w_2"][0], A["a_conv_b_2"][0][None]]).reshape(5, 16, P)
    out["a_conv"] = np.concatenate(
        [taps[:, t].T for g in range(4) for t in (2 * g, 2 * g + 1, 8 + g, 12 + g)], axis=1)
    taps = np.concatenate([A["a_dw_w_2"][0], A["a_dw_b_2"][0][None]]).reshape(32, KD, P)
    out["a_dw"] = np.concatenate([taps[:, t].T for t in range(KD)], axis=1)
    out["a_d_skip"] = columns(np.repeat(A["a_d_skip_2"][0], 64))
    for name in ("a_ssd_norm_w", "a_ln_w", "a_ln_b"):
        out[name] = columns(A[name + "_2"][0])
    for name in ("gdn_dt_bias", "gdn_a_log"):
        out[name] = np.zeros((P, 1), np.float32)
        out[name][32:40, 0] = A[name][0]
    return out


PARAMS = {}


def lay_out_parameters(A):
    at, parts = 0, small_parameters(A)
    for name, v in parts.items():
        PARAMS[name] = (at, at + v.shape[1])
        at += v.shape[1]
    PARAMS["end"] = (at, at)
    return np.concatenate(list(parts.values()), axis=1)


LAYERS = ("load", "pool", "gdn", "mla", "pool", "final", "even", "odd", "store")
BIASES = (EPS, EPS * 128, math.pi / 2, 1e-5)
GDN_MASKS = ("upper", "-strict lower", "blocks 16", "join 16", "join 32", "join 64")


def constants():
    p, x = np.arange(P)[:, None], np.arange(P)[None, :]
    c = {"identity": p == x, "ones": p + x >= 0, "upper": x >= p, "-strict lower": -1.0 * (x < p),
         "blocks 16": p // 16 == x // 16}
    for s in (16, 32, 64):
        c[f"join {s}"] = (p // (2 * s) == x // (2 * s)) & (p // s % 2 == 0) & (x // s % 2 == 1)
    rot = np.zeros((P, P), np.float32)
    for m in range(P):
        if m % 64 < 32:
            rot[m + 32, m] = -1.0
        else:
            rot[m - 32, m] = 1.0
    orot = np.zeros((P, P), np.float32)
    for m in range(P):
        if m % 64 < 8:
            orot[m + 8, m] = -1.0
        elif m % 64 < 16:
            orot[m - 8, m] = 1.0
    t = np.arange(SEQ)
    rcnt = np.stack([1.0 / np.minimum(t + 1, w) for w in WINDOWS]).astype(np.float32)
    odd_masks = [orot, np.where((x >= 64) & (p < 64), NEG, 0.0), p // 64 == x // 64]
    return {"odd_masks": np.concatenate([m.astype(np.float32) for m in odd_masks], axis=1),
            "mla_masks": np.concatenate([rot, np.where(x > p, NEG, 0.0).astype(np.float32)], axis=1),
            "consts": np.concatenate([c[k].astype(np.float32) for k in ("identity", "ones")], axis=1),
            "gdn_masks": np.concatenate([c[k].astype(np.float32) for k in GDN_MASKS], axis=1),
            "rcnt": np.ascontiguousarray(np.broadcast_to(rcnt.reshape(1, -1), (P, 4 * SEQ)))}


def kernel(**inputs):
    from concourse import bacc, mybir
    from concourse.bass_utils import run_bass_kernel_spmd

    A = {name: np.asarray(a) for name, a in inputs.items()}
    arrays = {"x": A["x"], "positions": A["positions"], "positions_2": A["positions_2"], "weights": lay_out_weights(LAYERS, A),
              "params": lay_out_parameters(A), **constants()}
    arrays = {name: np.ascontiguousarray(a) for name, a in arrays.items()}
    counts = {}
    for _ in range(2):
        nc = bacc.Bacc("TRN2", target_bir_lowering=False, num_devices=1)
        T = {name: nc.dram_tensor(f"{name}_dram", a.shape, mybir.dt.from_np(a.dtype), kind="ExternalInput").ap()
             for name, a in arrays.items()}
        out = nc.dram_tensor("out_dram", (1, SEQ, D), mybir.dt.float32, kind="ExternalOutput").ap()
        program(nc, T, out, counts, LAYERS)
    r = run_bass_kernel_spmd(nc, [{f"{name}_dram": a for name, a in arrays.items()}], core_ids=[0])
    return r.results[0]["out_dram"]
```

```python
import math
from contextlib import ExitStack

import numpy as np

SEQ, D = 512, 1024
P = 128
KD = D // P
EPS = 1e-6
RING = 4
BANKS = 4
SLOT = 1024
WINDOWS = (2, 4, 8, 16)
PAD = max(WINDOWS)
NCH = SEQ // P
NEG = -3.0e37
ROUND = 1.5 * 2.0 ** 23
TWO_PI = (6.28125, 0.0019350051879882812, 3.0199159795074593e-07)
PI_BELOW = 3.1415925


def ring_positions(n):
    short = {1: [3], 2: [2, 3], 5: [0, 1, 2, 3, 1]}
    if n in short:
        return short[n]
    threes = (-n) % 4
    return (n - 3 * threes) // 4 * [0, 1, 2, 3] + threes * [0, 1, 2]


class Stream:

    def __init__(self, sections):
        self.sec = {}
        slots, banks, tiles, first, next_bank = [0] * RING, [0] * BANKS, 0, 0, 0
        for name, iters, items in sections:
            s = {"iters": iters, "items": items, "slots0": list(slots), "first": first,
                 "banks0": list(banks), "tiles0": tiles}
            first += iters * len(items)
            ds, db, dt = [0] * RING, [0] * BANKS, 0
            s["slot"], s["tile"] = [], []
            t = next_bank if iters == 1 else 0
            for j, (_, nm) in enumerate(items):
                pos = ring_positions(len(items))[j]
                s["slot"].append((pos, ds[pos]))
                ds[pos] += 1
                row = []
                for m in range(nm):
                    b = t % BANKS
                    last = m == nm - 1
                    row.append((b, db[b], None if last else dt + 1))
                    db[b] += 1
                    dt += not last
                    t += 1
                s["tile"].append(row)
            s["per"] = (ds, db, dt)
            next_bank = t % BANKS
            for q in range(RING):
                slots[q] += iters * ds[q]
            for b in range(BANKS):
                banks[b] += iters * db[b]
            tiles += iters * dt
            self.sec[name] = s
        self.plan_ahead()

    def pos(self, sec, j):
        return self.sec[sec]["slot"][j][0]

    def uses(self, sec, i, j):
        s = self.sec[sec]
        pos, before = s["slot"][j]
        return s["slots0"][pos] + before + i * s["per"][0][pos]

    def bank(self, sec, j, m):
        return self.sec[sec]["tile"][j][m][0]

    def bank_uses(self, sec, i, j, m):
        s = self.sec[sec]
        b, before, _ = s["tile"][j][m]
        return s["banks0"][b] + before + i * s["per"][1][b]

    def tiles(self, sec, i, j, m):
        s = self.sec[sec]
        _, _, through = s["tile"][j][m]
        return None if through is None else s["tiles0"] + through + i * s["per"][2]

    def plan_ahead(self):
        flat = [(name, i, j) for name, s in self.sec.items() for i in range(s["iters"])
                for j in range(len(s["items"]))]
        held, latest = {}, None
        self.at_start, self.after = [], {x: [] for x in flat}
        for x in flat:
            q = self.pos(x[0], x[2])
            if q in held and (latest is None or flat.index(held[q]) > flat.index(latest)):
                latest = held[q]
            (self.at_start if latest is None else self.after[latest]).append(x)
            held[q] = x
        for name, s in self.sec.items():
            for i in range(1, s["iters"] - 1):
                for j in range(len(s["items"])):
                    a, b = self.after[name, 0, j], self.after[name, i, j]
                    assert [(x[0], x[1], x[2]) for x in a] == [(x[0], x[1] - i, x[2]) for x in b], (name, i, j)

    def ahead(self, sec, i, j, last):
        if last:
            return self.after[sec, self.sec[sec]["iters"] - 1, j]
        return [(s, i + di, jj) for s, di, jj in self.after[sec, 0, j]]


class Steps:

    def __init__(self, sem, counts):
        self.sem, self.counts, self.n = sem, counts, 0

    def turn(self):
        self.n = 0

    def done(self, name):
        self.n += 1
        assert self.counts.setdefault(name, self.n) == self.n, name
        self.counts["per turn"] = max(self.counts.get("per turn", 0), self.n)
        return self.sem, 1

    def at(self, name, i=0, ago=0):
        per = self.counts.get("per turn", 1)
        return self.sem, self.counts.get(name, 1) + (i - ago + 1) * per


def program(nc, T, out, counts, layers):
    from concourse import mybir
    import concourse.bass as bass

    F32, F32R, BF16, I32 = mybir.dt.float32, mybir.dt.float32r, mybir.dt.bfloat16, mybir.dt.int32
    ALU = mybir.AluOpType
    ACT = mybir.ActivationFunctionType
    AX = mybir.AxisListType
    ds = bass.ds

    kinds = {"pool": 0, "gdn": 0, "mla": 0, "even": 0, "odd": 0}
    plan = []
    for kind in layers:
        plan.append((kind, kinds.get(kind, 0)))
        if kind in kinds:
            kinds[kind] += 1

    SECTIONS = []
    for n, (kind, _) in enumerate(plan):
        SECTIONS += [(f"{name}{n}", iters, items) for name, iters, items in SLOTS.get(kind, [])]
    W = Stream(SECTIONS)

    top = ExitStack()
    with top:
        area = [top]

        def sb(name, shape, dt=F32):
            return area[0].enter_context(nc.sbuf_tensor(name, shape, dt))

        def sem(name):
            return top.enter_context(nc.semaphore(name))

        def steps(section, *engines):
            return [Steps(sem(f"{section}_{e}"), counts.setdefault((section, e), {})) for e in engines]

        xT = sb("xT", [P, KD, SEQ])
        xh = sb("xh", [P, KD, SEQ], F32R)
        xl = sb("xl", [P, KD, SEQ], F32R)
        raw = sb("raw", [P, RING, SLOT])
        whi = sb("whi", [P, RING, SLOT], F32R)
        wlo = sb("wlo", [P, RING, SLOT], F32R)
        R = sb("R", [P, SEQ])
        Rt = sb("Rt", [P, SEQ])
        sq = sb("sq", [P, 2, SEQ])
        cst = sb("cst", [P, 2 * P])
        ident = cst[:, 0:P]
        ones = cst[:, P:2 * P]
        bias = sb("bias", [P, len(BIASES)])
        par = sb("par", [P, PARAMS["end"][1]])
        psum = top.enter_context(nc.psum_tensor("psum", [P, 8, SEQ], F32))

        def gbank(b):
            return psum[:, b, :]

        def wbank(b):
            return psum[:, BANKS + b, :]

        raw_landed = [sem(f"raw_landed{q}") for q in range(RING)]
        hi_ready = [sem(f"hi_ready{q}") for q in range(RING)]
        lo_ready = [sem(f"lo_ready{q}") for q in range(RING)]
        slot_used = [sem(f"slot_used{q}") for q in range(RING)]
        tile_ready = sem("tile_ready")
        bank_taken = [sem(f"bank_taken{b}") for b in range(BANKS)]
        consts_in = sem("consts_in")
        out_stored = sem("out_stored")

        def load_slot(sp, sec, i, j):
            q = W.pos(sec, j)
            nk, nm = W.sec[sec]["items"][j]
            n = nk * nm * P
            sp.wait_ge(lo_ready[q], W.uses(sec, i, j) + 1)
            s = W.sec[sec]
            src = T["weights"][s["first"] + j] if isinstance(i, int) and i == 0 and s["iters"] == 1 else \
                T["weights"][ds(i * len(s["items"]) + (s["first"] + j), 1)].rearrange("a p n -> p (a n)")
            sp.dma_start(raw[:, q, 0:n], src[:, 0:n]).then_inc(raw_landed[q], 16)

        def load_slots(sec):
            def sync(sp):
                s = W.sec[sec]
                if s["iters"] == 1:
                    for j in range(len(s["items"])):
                        load_slot(sp, sec, 0, j)
                else:
                    with sp.Fori(0, s["iters"]) as i:
                        for j in range(len(s["items"])):
                            load_slot(sp, sec, i, j)
            return sync

        def split_slots(sec):
            def gpsimd(pool):
                s = W.sec[sec]
                if s["iters"] == 1:
                    for j in range(len(s["items"])):
                        slot_lo(pool, sec, 0, j)
                else:
                    with pool.Fori(0, s["iters"]) as i:
                        for j in range(len(s["items"])):
                            slot_lo(pool, sec, i, j)
            return gpsimd

        def slot_hi(act, sec, i, j):
            q = W.pos(sec, j)
            nk, nm = W.sec[sec]["items"][j]
            act.wait_ge(raw_landed[q], W.uses(sec, i, j) * 16 + 16)
            act.wait_ge(slot_used[q], W.uses(sec, i, j) + 1)
            act.activation(whi[:, q, 0:nk * nm * P], raw[:, q, 0:nk * nm * P], ACT.Copy).then_inc(hi_ready[q], 1)

        def hi_after(act, sec, i, j, last):
            for nxt in W.ahead(sec, i, j, last):
                slot_hi(act, *nxt)

        def slot_lo(pool, sec, i, j):
            q = W.pos(sec, j)
            nk, nm = W.sec[sec]["items"][j]
            n = nk * nm * P
            pool.wait_ge(hi_ready[q], W.uses(sec, i, j) + 1)
            pool.tensor_tensor(wlo[:, q, 0:n], raw[:, q, 0:n], whi[:, q, 0:n].bitcast(F32),
                               ALU.subtract).then_inc(lo_ready[q], 1)

        def product(pe, sec, i, j, m, hi, lo, waits=None, k0=0, k1=None, between=None):
            q = W.pos(sec, j)
            nk, nm = W.sec[sec]["items"][j]
            b = W.bank(sec, j, m)
            k1 = nk if k1 is None else k1
            if m == k0 == 0:
                pe.wait_ge(lo_ready[q], W.uses(sec, i, j) + 2)
            if k0 == 0:
                pe.wait_ge(bank_taken[b], W.bank_uses(sec, i, j, m) + 1)
            for k in range(k0, k1):
                if waits and waits[k]:
                    pe.wait_ge(*waits[k])
                c = (k * nm + m) * P
                pe.matmul(gbank(b), whi[:, q, c:c + P], hi[:, k, :], start=k == 0, stop=False)
                pe.matmul(gbank(b), whi[:, q, c:c + P], lo[:, k, :], start=False, stop=False)
                done = pe.matmul(gbank(b), wlo[:, q, c:c + P], hi[:, k, :], start=False, stop=k == nk - 1)
                if k == nk - 1:
                    done.then_inc(*((slot_used[q], 1) if m == nm - 1 else (tile_ready, 1)))
                if between:
                    between(k)

        def tile_done(sec, i, j, m):
            n = W.tiles(sec, i, j, m)
            if n is None:
                return slot_used[W.pos(sec, j)], W.uses(sec, i, j) + 2
            return tile_ready, n

        def tile_taken(sec, i, j, m):
            return bank_taken[W.bank(sec, j, m)], W.bank_uses(sec, i, j, m) + 2

        def taken(sec, j, m):
            return bank_taken[W.bank(sec, j, m)], 1

        def tile(sec, j, m):
            return gbank(W.bank(sec, j, m))

        def loop(eng, n, body, first=False):
            if first:
                body(0, False)
            if n > 1:
                with eng.Fori(int(first), n - 1) as i:
                    body(i, False)
            body(n - 1, True)

        def param(name):
            c0, c1 = PARAMS[name]
            return par[:, c0:c1]

        x_ready = []

        def load_x(n, j):
            xin = sb("xin", [P, NCH, D])
            BLOCKS = 4
            x_landed = [sem(f"x_landed{b}") for b in range(BLOCKS)]
            te, ve = steps("load_x", "tensor", "vector")

            def sync(sp):
                for b in range(BLOCKS):
                    c = slice(b * D // BLOCKS, (b + 1) * D // BLOCKS)
                    sp.dma_start(xin[:, :, c], T["x"][0].rearrange("(t p) d -> p t d", p=P)[:, :, c])\
                      .then_inc(x_landed[b], 16)

            def tensor(pe):
                for k in range(KD):
                    pe.wait_ge(x_landed[k * BLOCKS // KD], 16)
                    if k >= BANKS:
                        pe.wait_ge(*ve.at(f"x {k - BANKS}"))
                    for t in range(NCH):
                        last = pe.transpose(wbank(k % BANKS)[:, t * P:(t + 1) * P],
                                            xin[:, t, k * P:(k + 1) * P], ident)
                    last.then_inc(*te.done(f"x {k}"))

            def vector(dve):
                for k in range(KD):
                    dve.wait_ge(*te.at(f"x {k}"))
                    dve.tensor_copy(xT[:, k, :], wbank(k % BANKS)).then_inc(*ve.done(f"x {k}"))

            x_ready.append(ve.at(f"x {KD - 1}"))
            return {"sync": sync, "tensor": tensor, "vector": vector, "steps": {"tensor": [te], "vector": [ve]}}

        def norm(n, gain):
            ae, te, ve = steps(f"norm{n}", "scalar", "tensor", "vector")
            before = x_ready[-1]

            def scalar(act):
                act.wait_ge(*before)
                for k in range(KD):
                    if k >= 2:
                        act.wait_ge(*te.at(f"sum {k - 2}"))
                    act.activation(sq[:, k % 2, :], xT[:, k, :], ACT.Square).then_inc(*ae.done(f"square {k}"))
                act.wait_ge(*te.at(f"sum {KD - 1}"))
                act.activation(Rt[:, :], wbank(0), ACT.Ln, bias=bias[:, 0:1], scale=1.0 / D)\
                   .then_inc(*ae.done("ln"))
                act.wait_ge(*ae.at("ln"))
                act.activation(R[:, :], Rt[:, :], ACT.Exp, scale=-0.5).then_inc(*ae.done("R"))

            def sum_squares(pe, k):
                pe.wait_ge(*ae.at(f"square {k}"))
                pe.matmul(wbank(0), ones, sq[:, k % 2, :], start=k == 0, stop=k == KD - 1)\
                  .then_inc(*te.done(f"sum {k}"))

            def first_product(pe, sec, i, j):
                product(pe, sec, i, j, 0, xh, xl, [ve.at(f"lo {k}") for k in range(KD)],
                        between=lambda k: sum_squares(pe, k))

            def vector(dve):
                dve.wait_ge(*before)
                for k in range(KD):
                    dve.tensor_scalar(xh[:, k, :], xT[:, k, :], gain[:, k:k + 1], None, ALU.mult)\
                       .then_inc(*ve.done(f"hi {k}"))
                    dve.wait_ge(*ve.at(f"hi {k}"))
                    dve.scalar_tensor_tensor(out=xl[:, k, :], in0=xT[:, k, :], scalar=gain[:, k:k + 1],
                                             in1=xh[:, k, :].bitcast(F32), op0=ALU.mult, op1=ALU.subtract)\
                       .then_inc(*ve.done(f"lo {k}"))
                dve.wait_ge(*ae.at("R"))

            return {"scalar": scalar, "vector": vector, "steps": {"scalar": [ae], "tensor": [te], "vector": [ve]},
                    "first product": first_product}

        def two_norms(n, gain1, gain2):
            ae, te, ve = steps(f"norms{n}", "scalar", "tensor", "vector")
            gains = sb("gains", [P, KD])
            before = x_ready[-1]

            def scalar(act):
                act.wait_ge(*before)
                for k in range(2 * KD):
                    if k >= 2:
                        act.wait_ge(*te.at(f"sum {k - 2}"))
                    if k == KD:
                        act.wait_ge(*te.at(f"sum {KD - 1}"))
                        act.activation(Rt[:, :], wbank(0), ACT.Ln, bias=bias[:, 0:1], scale=1.0 / D)\
                           .then_inc(*ae.done("ln 1"))
                        act.wait_ge(*ae.at("ln 1"))
                        act.activation(R[:, :], Rt[:, :], ACT.Exp, scale=-0.5).then_inc(*ae.done("R 1"))
                    if k >= KD:
                        act.wait_ge(*ve.at(f"x {k - KD}"))
                    act.activation(sq[:, k % 2, :], xT[:, k % KD, :], ACT.Square).then_inc(*ae.done(f"square {k}"))
                act.wait_ge(*te.at(f"sum {2 * KD - 1}"))
                act.activation(Rt[:, :], wbank(0), ACT.Ln, bias=bias[:, 0:1], scale=1.0 / D)\
                   .then_inc(*ae.done("ln 2"))
                act.wait_ge(*ae.at("ln 2"))
                act.activation(Rt[:, :], Rt[:, :], ACT.Exp, scale=-0.5).then_inc(*ae.done("R 2"))

            def sum_squares(pe, k):
                pe.wait_ge(*ae.at(f"square {k}"))
                pe.matmul(wbank(0), ones, sq[:, k % 2, :], start=k % KD == 0, stop=k % KD == KD - 1)\
                  .then_inc(*te.done(f"sum {k}"))

            def first_product(pe, sec, i, j):
                product(pe, sec, i, j, 0, xh, xl, [ve.at(f"lo {k}") for k in range(KD)],
                        between=lambda k: sum_squares(pe, k))

            def vector(dve):
                dve.wait_ge(*before)
                dve.tensor_tensor(gains[:, :], gain1, gain2, ALU.mult).then_inc(*ve.done("gains"))
                dve.wait_ge(*ve.at("gains"))
                for k in range(KD):
                    dve.tensor_scalar(xh[:, k, :], xT[:, k, :], gains[:, k:k + 1], None, ALU.mult)\
                       .then_inc(*ve.done(f"hi {k}"))
                    dve.wait_ge(*ve.at(f"hi {k}"))
                    dve.scalar_tensor_tensor(out=xl[:, k, :], in0=xT[:, k, :], scalar=gains[:, k:k + 1],
                                             in1=xh[:, k, :].bitcast(F32), op0=ALU.mult, op1=ALU.subtract)\
                       .then_inc(*ve.done(f"lo {k}"))
                dve.wait_ge(*ae.at("R 1"))
                dve.wait_ge(*ve.at(f"lo {KD - 1}"))
                for k in range(KD):
                    dve.scalar_tensor_tensor(out=xT[:, k, :], in0=xT[:, k, :], scalar=gain1[:, k:k + 1], in1=R[:, :],
                                             op0=ALU.mult, op1=ALU.mult).then_inc(*ve.done(f"x {k}"))
                dve.wait_ge(*ae.at("R 2"))
                dve.wait_ge(*ve.at(f"x {KD - 1}"))
                dve.tensor_tensor(R[:, :], R[:, :], Rt[:, :], ALU.mult).then_inc(*ve.done("R"))
                dve.wait_ge(*ve.at("R"))

            return {"scalar": scalar, "vector": vector, "steps": {"scalar": [ae], "tensor": [te], "vector": [ve]},
                    "first product": first_product,
                    "second sum": lambda pe, k: sum_squares(pe, KD + k)}

        def add_to_x(dve, sec, i, j, tiles):
            for m, t in enumerate(tiles):
                add_tile(dve, sec, i, j, m, t)

        def add_tile(dve, sec, i, j, m, t):
            dve.wait_ge(*tile_done(sec, i, j, m))
            dve.tensor_tensor(xT[:, t, :], tile(sec, j, m), xT[:, t, :], ALU.add).then_inc(*taken(sec, j, m))

        def merge(*parts):
            out = {"steps": {}}
            for e in ("sync", "gpsimd", "scalar", "vector", "tensor"):
                fs = [p[e] for p in parts if e in p]
                if fs:
                    out[e] = (lambda fs: lambda eng: [f(eng) for f in fs] and None)(fs)
                ss = [s for p in parts for s in p.get("steps", {}).get(e, [])]
                if ss:
                    out["steps"][e] = ss
            return out

        def pool_layer(n, l):
            nv = norm(n, param(f"norm_g{(0, 3)[l]}"))
            sec = f"pool{n}"
            G = D * 2 // 4 // P
            u = sb(f"pool_u{n}", [P, G, SEQ])
            cum = sb(f"pool_cum{n}", [P, 2, PAD + SEQ])
            d = sb(f"pool_d{n}", [P, 2, SEQ])
            ph = sb(f"pool_ph{n}", [P, G, SEQ], F32R)
            pl = sb(f"pool_pl{n}", [P, G, SEQ], F32R)
            yh = sb(f"pool_yh{n}", [P, G, SEQ], F32R)
            yl = sb(f"pool_yl{n}", [P, G, SEQ], F32R)
            g = sb(f"pool_g{n}", [P, G, SEQ])
            rcnt = sb(f"pool_rcnt{n}", [P, 4, SEQ])
            onesrow = sb(f"pool_onesrow{n}", [P, SEQ])
            scale = param(f"pool_scale{l}")
            tables_in = sem(f"pool_tables_in{n}")
            ae, te, ve = steps(sec, "scalar", "tensor", "vector")

            def tables(act):
                act.wait_ge(*x_ready_before)
                act.dma_start(rcnt[:, :, :], T["rcnt"].rearrange("p (w s) -> p w s", w=4)).then_inc(tables_in, 16)

            def sync(sp):
                load_slots(sec)(sp)

            def scalar(act):
                def turn(i, last):
                    ae.turn()
                    for j in range(8):
                        hi_after(act, sec, i, j, last)
                    for m in range(G):
                        act.wait_ge(*tile_taken(sec, i, 4 + m, 0))
                        act.activation(g[:, m, :], g[:, m, :], ACT.Silu).then_inc(*ae.done(f"silu {m}"))
                    for j in range(8, 14):
                        hi_after(act, sec, i, j, last)
                loop(act, 4, turn)

            def tensor(pe):
                def turn(i, last):
                    te.turn()
                    for j in range(8):
                        if j == 0 and isinstance(i, int) and i == 0:
                            nv["first product"](pe, sec, i, j)
                        else:
                            product(pe, sec, i, j, 0, xh, xl)
                    for m in range(G):
                        product(pe, sec, i, 8 + m // 2, m % 2, ph, pl, [ve.at(f"p lo {k}", i) for k in range(G)])
                    for m in range(KD):
                        product(pe, sec, i, 10 + m // 2, m % 2, yh, yl, [ve.at(f"y lo {k}", i) for k in range(G)])
                loop(pe, 4, turn, first=True)

            def vector(dve):
                dve.wait_ge(tables_in, 16)
                dve.memset(cum[:, :, 0:PAD], 0.0).then_inc(tables_in, 1)
                dve.memset(onesrow[:, :], 1.0).then_inc(tables_in, 1)
                dve.wait_ge(tables_in, 18)

                def turn(i, last):
                    ve.turn()
                    shift = WINDOWS[3] if last else None
                    for m in range(G):
                        dve.wait_ge(*tile_done(sec, i, m, 0))
                        dve.tensor_tensor(u[:, m, :], tile(sec, m, 0), R[:, :], ALU.mult)\
                           .then_inc(*taken(sec, m, 0))
                    for m in range(G):
                        b = m % 2
                        dve.wait_ge(*tile_taken(sec, i, m, 0))
                        dve.tensor_tensor_scan(cum[:, b, PAD:], onesrow[:, :], u[:, m, :], 0.0,
                                               ALU.mult, ALU.add).then_inc(*ve.done(f"cum {m}"))
                        dve.wait_ge(*ve.at(f"cum {m}", i))
                        back = cum[:, b, PAD - shift:PAD - shift + SEQ] if last else \
                            cum[:, b, ds(PAD - 2 - i * i - i, SEQ)]
                        dve.tensor_tensor(d[:, b, :], cum[:, b, PAD:], back, ALU.subtract)\
                           .then_inc(*ve.done(f"window {m}"))
                        dve.wait_ge(*ve.at(f"window {m}", i))
                        dve.tensor_tensor(d[:, b, :], d[:, b, :], rcnt[:, 3 if last else ds(i, 1), :], ALU.mult)\
                           .then_inc(*ve.done(f"mean {m}"))
                        dve.wait_ge(*ve.at(f"mean {m}", i))
                        dve.tensor_tensor(u[:, m, :], d[:, b, :], u[:, m, :], ALU.subtract)\
                           .then_inc(*ve.done(f"p {m}"))
                        dve.wait_ge(*ve.at(f"p {m}", i))
                        dve.tensor_copy(ph[:, m, :], u[:, m, :]).then_inc(*ve.done(f"p hi {m}"))
                        dve.wait_ge(*ve.at(f"p hi {m}", i))
                        dve.tensor_tensor(pl[:, m, :], u[:, m, :], ph[:, m, :].bitcast(F32), ALU.subtract)\
                           .then_inc(*ve.done(f"p lo {m}"))
                    for m in range(G):
                        dve.wait_ge(*tile_done(sec, i, 4 + m, 0))
                        dve.tensor_tensor(g[:, m, :], tile(sec, 4 + m, 0), R[:, :], ALU.mult)\
                           .then_inc(*taken(sec, 4 + m, 0))
                    for m in range(G):
                        dve.wait_ge(*ae.at(f"silu {m}", i))
                        dve.wait_ge(*tile_done(sec, i, 8 + m // 2, m % 2))
                        dve.scalar_tensor_tensor(out=u[:, m, :], in0=tile(sec, 8 + m // 2, m % 2),
                                                 scalar=scale[:, 12 + m:13 + m] if last else
                                                 scale[:, ds(i * G + m, 1)],
                                                 in1=g[:, m, :], op0=ALU.mult, op1=ALU.mult)\
                           .then_inc(*taken(sec, 8 + m // 2, m % 2))
                        dve.wait_ge(*tile_taken(sec, i, 8 + m // 2, m % 2))
                        dve.tensor_copy(yh[:, m, :], u[:, m, :]).then_inc(*ve.done(f"y hi {m}"))
                        dve.wait_ge(*ve.at(f"y hi {m}", i))
                        dve.tensor_tensor(yl[:, m, :], u[:, m, :], yh[:, m, :].bitcast(F32), ALU.subtract)\
                           .then_inc(*ve.done(f"y lo {m}"))
                    for j in range(4):
                        add_to_x(dve, sec, i, 10 + j, (2 * j, 2 * j + 1))
                loop(dve, 4, turn)

            x_ready_before = x_ready[-1]
            x_ready.append(tile_taken(sec, 3, 13, 1))
            me = {"sync": sync, "gpsimd": split_slots(sec), "scalar": scalar, "tensor": tensor, "vector": vector,
                  "steps": {"scalar": [ae], "tensor": [te], "vector": [ve]}}
            return merge({"scalar": tables}, nv, me)

        def store_x(n, l):
            y = sb("y", [P, 2, D])
            te, ve = steps("store_x", "tensor", "vector")
            before = x_ready[-1]

            def tensor(pe):
                pe.wait_ge(*before)
                for t in range(NCH):
                    for h in range(2):
                        b = (2 * t + h) % BANKS
                        if 2 * t + h >= BANKS:
                            pe.wait_ge(*ve.at(f"y {t - 2} {h}"))
                        for k in range(4):
                            last = pe.transpose(wbank(b)[:, k * P:(k + 1) * P],
                                                xT[:, 4 * h + k, t * P:(t + 1) * P], ident)
                        last.then_inc(*te.done(f"y {t} {h}"))

            def vector(dve):
                for t in range(NCH):
                    if t >= 2:
                        dve.wait_ge(out_stored, 16 * (t - 1))
                    for h in range(2):
                        dve.wait_ge(*te.at(f"y {t} {h}"))
                        dve.tensor_copy(y[:, t % 2, h * 512:(h + 1) * 512], wbank((2 * t + h) % BANKS))\
                           .then_inc(*ve.done(f"y {t} {h}"))

            def sync(sp):
                for t in range(NCH):
                    sp.wait_ge(*ve.at(f"y {t} 1"))
                    if t:
                        sp.wait_ge(out_stored, 16 * t)
                    sp.dma_start(out[0, t * P:(t + 1) * P, :], y[:, t % 2, :]).then_inc(out_stored, 16)
                sp.wait_ge(out_stored, 16 * NCH)

            return {"sync": sync, "tensor": tensor, "vector": vector, "steps": {"tensor": [te], "vector": [ve]}}

        def even_layer(n, l):
            nv = two_norms(n, param("final_g"), param("a_norm_w"))
            sections = [f"ev_{s}{n}" for s in ("dt", "first", "glu", "ssd", "last", "out")]
            dt_sec, first_sec, glu_sec, sec, last_sec, out_sec = sections
            GROUPS, HG, H, TAPS = 4, 4, 16, 31
            PADU = TAPS - 1
            ue = sb("e_ue", [P, PADU + SEQ])
            uk = sb("e_uk", [P, GROUPS, PADU + SEQ])
            conv31 = sb("e_c", [P, KD, SEQ])
            pre = sb("e_pre", [P, 4, 3 + SEQ])
            stg = sb("e_stg", [P, 4, SEQ])
            gp = sb("e_gp", [P, 2, SEQ])
            Gm = sq[0:16, :, :]
            xds = sb("e_xd", [P, 2, NCH, 2 * P])
            xd, xw = xds[:, 0, :, :], xds[:, 1, :, :]
            btok = sb("e_btok", [P, NCH, P])
            cbm = sb("e_cbm", [P, NCH, P])
            HS = sb("e_HS", [P, 3, 2 * P])
            yh = sb("e_yh", [P, 2, SEQ], F32R)
            yl = sb("e_yl", [P, 2, SEQ], F32R)
            zs = sb("e_zs", [P, KD, SEQ])
            Q = sb("e_Q", [P, SEQ])
            gcol = sb("e_gcol", [P, 3, NCH, H])
            ecl = sb("e_ecl", [P, H, NCH])
            small_ = sb("e_small", [P, 3 * 64])
            mU = sb("e_mU", [P, P])
            wt = sb("e_wt", [P, 32])
            yf = xds[:, :, :, :].rearrange("p a c v -> p (a c v)")[:, 0:2 * SEQ].rearrange("p (d s) -> p d s", d=2)
            glu = xds[:, :, :, :].rearrange("p a c v -> p (a c v)").rearrange("p (d s) -> p d s", d=4)
            acc = sb("e_acc", [P, SEQ])
            whole = area[0]
            with ExitStack() as until_ssd_ends:
                area[0] = until_ssd_ends
                ecs = sb("e_ecs", [P, 2, SEQ])
                Dd = sb("e_D", [P, 2, SEQ])
            area[0] = whole
            ohs, ols = [yh, sb("e_yh2", [P, 2, SEQ], F32R)], [yl, sb("e_yl2", [P, 2, SEQ], F32R)]
            tmp = [conv31[:, x, :] for x in range(6)]
            dtb, alog = param("a_dt_bias"), param("a_a_log")
            conv, dw = param("a_conv"), param("a_dw")
            dskip, snw = param("a_d_skip"), param("a_ssd_norm_w")
            lnw, lnb = param("a_ln_w"), param("a_ln_b")
            mask_in = sem("even_mask_in")
            ab, tb, vbs = steps(f"ev_dt{n}", "scalar", "tensor", "vector")
            ag, vg = steps(f"ev_glu{n}", "scalar", "vector")
            ap_, vp = steps(f"ev_prep{n}", "scalar", "vector")
            ae, te, ve = steps(sec, "scalar", "tensor", "vector")
            al, tl, vl = steps(f"ev_ln{n}", "scalar", "tensor", "vector")
            az, vz = steps(f"ev_z{n}", "scalar", "vector")
            x_ready_before = x_ready[-1]
            h16 = slice(0, 16)
            cs16 = slice(32, 48)

            def chunks(ap):
                return ap.rearrange("p (c n) -> p c n", c=NCH)

            def at(ap, i, per, k=0, w=1):
                return ap[:, ds(i * per + k, w)] if not isinstance(i, int) else ap[:, i * per + k:i * per + k + w]

            def dt_take(dve):
                dve.wait_ge(*tile_done(dt_sec, 0, 0, 0))
                dve.tensor_tensor(tmp[0], tile(dt_sec, 0, 0), R[:, :], ALU.mult).then_inc(*taken(dt_sec, 0, 0))
                dve.memset(Q[:, :], 0.0).then_inc(*vbs.done("Q zero"))
                dve.memset(ue[:, 0:PADU], 0.0).then_inc(*vbs.done("pad of ue"))
                dve.memset(uk[:, :, 0:PADU], 0.0).then_inc(*vbs.done("pads of uk"))
                dve.wait_ge(*vbs.at("pads of uk"))

            def dt_vector(dve):
                q = tmp[0][h16]
                dve.wait_ge(*tile_taken(dt_sec, 0, 0, 0))
                dve.tensor_scalar(tmp[1][h16], q, dtb[h16], None, ALU.add).then_inc(*vbs.done("z"))
                dve.wait_ge(*ab.at("exp z"))
                dve.tensor_scalar(tmp[3][h16], tmp[2][h16], 1.0, None, ALU.add).then_inc(*vbs.done("u"))
                dve.wait_ge(*vbs.at("u"))
                dve.tensor_scalar(tmp[4][h16], tmp[3][h16], -1.0, None, ALU.add).then_inc(*vbs.done("u-1"))
                dve.wait_ge(*vbs.at("u-1"))
                dve.tensor_scalar(tmp[5][h16], tmp[4][h16], 0.0, None, ALU.is_equal).then_inc(*vbs.done("is 0"))
                dve.wait_ge(*vbs.at("is 0"))
                dve.tensor_tensor(tmp[4][h16], tmp[4][h16], tmp[5][h16], ALU.add).then_inc(*vbs.done("den"))
                dve.wait_ge(*vbs.at("den"))
                dve.reciprocal(tmp[4][h16], tmp[4][h16]).then_inc(*vbs.done("1/den"))
                dve.wait_ge(*ab.at("ln u"))
                dve.wait_ge(*vbs.at("1/den"))
                dve.tensor_tensor(tmp[3][h16], tmp[3][h16], tmp[4][h16], ALU.mult).then_inc(*vbs.done("ln/den"))
                dve.wait_ge(*vbs.at("ln/den"))
                dve.tensor_tensor(tmp[3][h16], tmp[3][h16], tmp[5][h16], ALU.add).then_inc(*vbs.done("ratio"))
                dve.wait_ge(*vbs.at("ratio"))
                dve.tensor_tensor(tmp[3][h16], tmp[3][h16], tmp[2][h16], ALU.mult).then_inc(*vbs.done("log1p"))
                dve.wait_ge(*vbs.at("log1p"))
                dve.scalar_tensor_tensor(out=Q[h16, :], in0=tmp[1][h16], scalar=0.0, in1=tmp[3][h16], op0=ALU.max,
                                         op1=ALU.add).then_inc(*vbs.done("dt"))
                dve.wait_ge(*vbs.at("dt"))
                dve.wait_ge(*ab.at("exp a"))
                dve.tensor_scalar(tmp[3][cs16], Q[h16, :], small_[h16, 0:1], -1.0, ALU.mult, ALU.mult)\
                   .then_inc(*vbs.done("da"))
                dve.memset(tmp[5], 1.0).then_inc(*vbs.done("ones"))
                dve.wait_ge(*vbs.at("ones"))
                for c in range(NCH):
                    s = slice(c * P, (c + 1) * P)
                    dve.tensor_tensor_scan(Q[cs16, s], tmp[5][cs16, s], tmp[3][cs16, s], 0.0, ALU.mult, ALU.add)\
                       .then_inc(*vbs.done(f"cumsum {c}"))
                for c in range(NCH):
                    s = slice(c * P, (c + 1) * P)
                    dve.wait_ge(*vbs.at(f"cumsum {c}"))
                    dve.tensor_scalar(tmp[4][cs16, s], Q[cs16, s], Q[cs16, c * P + P - 1:(c + 1) * P], None,
                                      ALU.subtract).then_inc(*vbs.done(f"cs-last {c}"))
                dve.tensor_copy(small_[h16, 64:68], Q[cs16, P - 1::P]).then_inc(*vbs.done("last"))
                dve.wait_ge(*vbs.at("last"))
                dve.tensor_tensor(small_[h16, 128:192].rearrange("p (h c) -> p h c", c=NCH),
                                  ident[h16, 0:16].unsqueeze(2).to_broadcast([16, H, NCH]),
                                  small_[h16, 64:68].unsqueeze(1).to_broadcast([16, H, NCH]), ALU.mult)\
                   .then_inc(*vbs.done("last diagonal"))
                dve.wait_ge(*ab.at("exp last-cs"))
                dve.tensor_tensor(Q[64:80, :], Q[h16, :], tmp[1][h16], ALU.mult).then_inc(*vbs.done("dt exp"))
                dve.wait_ge(*tb.at("columns"))
                dve.tensor_copy(gcol[:, :, :, :],
                                wbank(0).rearrange("p (c q h) -> p q c h", c=NCH, q=4)[:, 0:3, :, 0:H])\
                   .then_inc(*vbs.done("columns"))
                dve.memset(pre[:, :, 0:3], 0.0).then_inc(*vbs.done("pads"))
                dve.wait_ge(*vbs.at("pads"))
                dve.wait_ge(mask_in, 16)

            def dt_scalar(act):
                act.wait_ge(*vbs.at("z"))
                act.activation(tmp[2][h16], tmp[1][h16], ACT.Abs).then_inc(*ab.done("abs z"))
                act.wait_ge(*ab.at("abs z"))
                act.activation(tmp[2][h16], tmp[2][h16], ACT.Exp, scale=-1.0).then_inc(*ab.done("exp z"))
                act.activation(small_[h16, 0:1], alog[h16], ACT.Exp).then_inc(*ab.done("exp a"))
                act.wait_ge(*vbs.at("u-1"))
                act.activation(tmp[3][h16], tmp[3][h16], ACT.Ln).then_inc(*ab.done("ln u"))
                for j in range(3):
                    hi_after(act, first_sec, 0, j, True)
                act.wait_ge(*vbs.at("cs-last 3"))
                act.activation(tmp[1][h16], tmp[4][cs16], ACT.Exp, scale=-1.0).then_inc(*ab.done("exp last-cs"))
                act.wait_ge(*tb.at("last"))
                act.activation(ecl[:, :, :], wbank(1)[:, 0:64].rearrange("p (h c) -> p h c", c=NCH), ACT.Exp)\
                   .then_inc(*ab.done("exp last"))

            def dt_tensor(pe):
                pe.wait_ge(*vbs.at("last diagonal"))
                pe.matmul(wbank(1)[:, 0:64], ones[h16, :], small_[h16, 128:192], start=True, stop=True)\
                  .then_inc(*tb.done("last"))
                pe.wait_ge(*vbs.at("dt exp"))
                for c in range(NCH):
                    last = pe.transpose(wbank(0)[:, c * P:(c + 1) * P], Q[:, c * P:(c + 1) * P], ident)
                last.then_inc(*tb.done("columns"))

            def taps(dve, st, i, source, k0, k1, x=0):
                for k in range(k0, k1):
                    out = acc[:, :] if k < TAPS - 1 else channel(conv31[:, :, :], i, 2, x)
                    if k == 0:
                        dve.tensor_scalar(acc[:, :], source[:, 0:SEQ], wt[:, 0:1], wt[:, TAPS:TAPS + 1],
                                          ALU.mult, ALU.add).then_inc(*st.done("tap 0"))
                    else:
                        dve.wait_ge(*st.at(f"tap {k - 1}", i))
                        dve.scalar_tensor_tensor(out=out, in0=source[:, k:k + SEQ], scalar=wt[:, k:k + 1],
                                                 in1=acc[:, :], op0=ALU.mult, op1=ALU.add)\
                           .then_inc(*st.done(f"tap {k}"))

            def channel(ap, i, per, k):
                return ap[:, i * per + k, :] if isinstance(i, int) else ap[:, ds(i * per + k, 1), :]\
                    .rearrange("p a s -> p (a s)")

            def glu_vector(dve, i):
                vg.turn()
                dve.tensor_copy(wt[:, :], at(dw, i, 64, 0, 32)).then_inc(*vg.done("taps"))
                for x in range(2):
                    for j in (2 * x, 2 * x + 1):
                        dve.wait_ge(*tile_done(glu_sec, i, j, 0))
                        dve.tensor_tensor(glu[:, j, :], tile(glu_sec, j, 0), R[:, :], ALU.mult)\
                           .then_inc(*taken(glu_sec, j, 0))
                    if x == 0:
                        dve.wait_ge(*ag.at("sigmoid 0", i))
                        dve.tensor_tensor(ue[:, PADU:], glu[:, 0, :], glu[:, 1, :], ALU.mult).then_inc(*vg.done("u 0"))
                        dve.wait_ge(*vg.at("u 0", i))
                        taps(dve, vg, i, ue, 0, 15)
                taps(dve, vg, i, ue, 15, 18)
                dve.wait_ge(*ag.at("sigmoid 1", i))
                dve.tensor_tensor(channel(uk[:, :, PADU:], i, 1, 0), glu[:, 2, :], glu[:, 3, :], ALU.mult)\
                   .then_inc(*vg.done("u 1"))
                taps(dve, vg, i, ue, 18, 22)
                for x in range(2):
                    dve.wait_ge(*tile_done(glu_sec, i, 4 + x, 0))
                    dve.tensor_tensor(channel(zs[:, :, :], i, 2, x), tile(glu_sec, 4 + x, 0), R[:, :], ALU.mult)\
                       .then_inc(*taken(glu_sec, 4 + x, 0))
                    taps(dve, vg, i, ue, 22 + 4 * x, 26 + 4 * x)
                taps(dve, vg, i, ue, 30, TAPS)
                dve.wait_ge(*vg.at(f"tap {TAPS - 1}", i))

            def glu_scalar(act, i, last):
                ag.turn()
                for x in range(2):
                    hi_after(act, glu_sec, i, 2 * x, last)
                    hi_after(act, glu_sec, i, 2 * x + 1, last)
                    act.wait_ge(*tile_taken(glu_sec, i, 2 * x + 1, 0))
                    act.activation(glu[:, 2 * x + 1, :], glu[:, 2 * x + 1, :], ACT.Sigmoid)\
                       .then_inc(*ag.done(f"sigmoid {x}"))
                for j in (4, 5):
                    hi_after(act, glu_sec, i, j, last)
                for x in range(2):
                    act.wait_ge(*tile_taken(glu_sec, i, 4 + x, 0))
                    act.activation(channel(zs[:, :, :], i, 2, x), channel(zs[:, :, :], i, 2, x), ACT.Silu)\
                       .then_inc(*ag.done(f"silu z {x}"))

            def in_pieces(pe, s, i):
                for t in range(6):
                    for k in range(0, KD, 2):
                        product(pe, s, i, t, 0, xh, xl, None, k, k + 2)
                        yield

            def evac(dve, s, i, t):
                dve.wait_ge(*tile_done(s, i, t, 0))
                dst = pre[:, t, 3:] if t < 4 else gp[:, t - 4, :]
                dve.tensor_tensor(dst, tile(s, t, 0), R[:, :], ALU.mult).then_inc(*taken(s, t, 0))

            def prep_vector(dve, s, i, h, adds=None):
                vp.turn()
                dve.wait_ge(*tile_taken(s, i, 3, 0))
                dve.wait_ge(*te.at("y 3", h, 1))
                for x in (2, 3, 0, 1):
                    for tap in range(4):
                        w = at(conv, h, 20, x * 5 + tap)
                        if tap == 0:
                            dve.tensor_scalar(stg[:, x, :], pre[:, x, 0:SEQ], w, None, ALU.mult)\
                               .then_inc(*vp.done(f"tap {tap} {x}"))
                        else:
                            dve.wait_ge(*vp.at(f"tap {tap - 1} {x}", h))
                            dve.scalar_tensor_tensor(out=stg[:, x, :], in0=pre[:, x, tap:tap + SEQ], scalar=w,
                                                     in1=stg[:, x, :], op0=ALU.mult, op1=ALU.add)\
                               .then_inc(*vp.done(f"tap {tap} {x}"))
                        if adds and tap % 2:
                            adds(((x + 2) % 4) * 2 + tap // 2)

            def prep_scalar(act, s, i, h):
                ap_.turn()
                for x in (2, 3, 0, 1):
                    act.wait_ge(*vp.at(f"tap 3 {x}", h))
                    act.activation(stg[:, x, :], stg[:, x, :], ACT.Silu, bias=at(conv, h, 20, x * 5 + 4))\
                       .then_inc(*ap_.done(f"silu {x}"))
                act.wait_ge(*ve.at("y z 1", h, 1))
                act.wait_ge(*tile_taken(s, i, 5, 0))
                act.activation(gp[:, :, :], gp[:, :, :], ACT.Silu).then_inc(*ap_.done("silu z"))

            def work_tensor(pe, i, more):
                te.turn()
                pe.wait_ge(*ap_.at("silu 2", i))
                pe.wait_ge(*ve.at("y skip 1", i, 1))
                for c in range(NCH):
                    last = pe.transpose(wbank(2)[:, c * P:(c + 1) * P], stg[:, 2, c * P:(c + 1) * P], ident)
                last.then_inc(*te.done("B tokens"))
                pe.wait_ge(*ap_.at("silu 3", i))
                for c in range(NCH):
                    s = slice(c * P, (c + 1) * P)
                    last = pe.matmul(wbank(3)[:, s], stg[:, 2, s], stg[:, 3, s], start=True, stop=True)
                last.then_inc(*te.done("cb"))
                pe.wait_ge(*ap_.at("silu 1", i))
                pe.wait_ge(*ae.at("ln y", i, 1))
                for c in range(NCH):
                    for d in range(2):
                        a = (c % 2) * 2 * P + d * P
                        last = pe.transpose(wbank(c // 2)[:, a:a + P], stg[:, d, c * P:(c + 1) * P], ident)
                last.then_inc(*te.done("x tokens"))
                more()
                more()
                for c in range(3):
                    b = 2 + c % 2
                    if c == 0:
                        pe.wait_ge(*ae.at("B tokens", i))
                        pe.wait_ge(*ve.at("x w 1", i))
                    elif c == 2:
                        pe.wait_ge(*ve.at("state 0", i))
                    pe.matmul(wbank(b)[:, 0:2 * P], btok[:, c, :], xw[:, c, :], start=True, stop=True)\
                      .then_inc(*te.done(f"state {c}"))
                    more()
                pe.wait_ge(*ve.at("x dt 1", i))
                for h in range(HG):
                    if h >= 2:
                        pe.wait_ge(*ve.at(f"row {h}", i))
                    pe.matmul(wbank(h % 2), ones[h16, :], Gm[:, h % 2, :], start=True, stop=True)\
                      .then_inc(*te.done(f"cs row {h}"))
                    more()
                    if h:
                        y_head(pe, i, h - 1)
                        more()
                        more()
                y_head(pe, i, HG - 1)
                for _ in range(4):
                    more()
                for d in range(2):
                    pe.wait_ge(*ae.at(f"y square {d}", i))
                    pe.matmul(wbank(0), ones, ecs[:, d, :], start=d == 0, stop=d == 1).then_inc(*te.done(f"y sum {d}"))

            def y_head(pe, i, h):
                b, r = 2 + h // 2, slice(64 * (h % 2), 64 * (h % 2) + 64)
                hc = slice(64 * h, 64 * h + 64)
                pe.wait_ge(*ve.at(f"M {h}", i))
                for c in range(NCH):
                    s = slice(c * P, (c + 1) * P)
                    if c:
                        pe.matmul(wbank(b)[r, s], HS[:, c - 1, hc], ecs[:, h % 2, s], start=True, stop=False)
                    last = pe.matmul(wbank(b)[r, s], xd[:, c, hc], Dd[:, h % 2, s], start=c == 0, stop=True)
                last.then_inc(*te.done(f"y {h}"))

            def work_scalar(act, i, between):
                ae.turn()
                act.wait_ge(*te.at("B tokens", i))
                act.activation(btok[:, :, :], chunks(wbank(2)), ACT.Copy).then_inc(*ae.done("B tokens"))
                for h in range(HG):
                    act.wait_ge(*te.at(f"cs row {h}", i))
                    act.activation(ecs[:, h % 2, :], wbank(h % 2), ACT.Exp).then_inc(*ae.done(f"exp cs {h}"))
                    for c in range(NCH):
                        s = slice(c * P, (c + 1) * P)
                        last = act.activation(Dd[:, h % 2, s], wbank(h % 2)[:, s], ACT.Relu, scale=-1.0,
                                              bias=at(gcol[:, 1, c, :], i, 4, h))
                    last.then_inc(*ae.done(f"d {h}"))
                    act.wait_ge(*ae.at(f"d {h}", i))
                    act.activation(Dd[:, h % 2, :], Dd[:, h % 2, :], ACT.Exp, scale=-1.0)\
                       .then_inc(*ae.done(f"exp d {h}"))
                    between(h)
                for d in range(2):
                    act.wait_ge(*ve.at(f"y z {d}", i))
                    act.activation(ecs[:, d, :], yf[:, d, :], ACT.Square).then_inc(*ae.done(f"y square {d}"))
                act.wait_ge(*te.at("y sum 1", i))
                act.activation(Rt[:, :], wbank(0), ACT.Ln, scale=1.0 / (2 * P), bias=bias[:, 0:1])\
                   .then_inc(*ae.done("ln y"))
                act.wait_ge(*ae.at("ln y", i))
                act.activation(Rt[:, :], Rt[:, :], ACT.Exp, scale=-0.5).then_inc(*ae.done("1/rms y"))
                between(4)
                between(5)

            def work_vector(dve, i, evac):
                ve.turn()
                csc = slice(4 * i, 4 * i + 4) if isinstance(i, int) else ds(i * 4, 4)

                def row(h):
                    sel = ident[cs16, 32 + 4 * i + h:33 + 4 * i + h] if isinstance(i, int) else \
                        ident[cs16, ds(i * 4 + (32 + h), 1)]
                    if h >= 2:
                        dve.wait_ge(*te.at(f"cs row {h - 2}", i))
                    dve.tensor_scalar(Gm[:, h % 2, :], Q[cs16, :], sel, None, ALU.mult).then_inc(*ve.done(f"row {h}"))

                row(0)
                row(1)
                dve.tensor_copy(wt[:, :], at(dw, i, 64, 32, 32)).then_inc(*ve.done("taps"))
                dve.tensor_copy(ue[:, PADU:], channel(uk[:, :, PADU:], i, 1, 0)).then_inc(*ve.done("u"))
                dve.wait_ge(*te.at("cb", i))
                dve.tensor_tensor(cbm[:, :, :], chunks(wbank(3)), mU[:, :].unsqueeze(1).to_broadcast([P, NCH, P]),
                                  ALU.mult).then_inc(*ve.done("cb"))
                for q, dst, name in ((2, xw, "x w"), (0, xd, "x dt")):
                    for h in range(2):
                        dve.wait_ge(*te.at("x tokens", i))
                        c = gcol[:, q, 2 * h:2 * h + 2, csc].unsqueeze(3).to_broadcast([P, 2, HG, 64])
                        dve.tensor_tensor(dst[:, 2 * h:2 * h + 2, :].rearrange("p c (h v) -> p c h v", h=HG),
                                          wbank(h).rearrange("p (c h v) -> p c h v", c=2, h=HG), c, ALU.mult)\
                           .then_inc(*ve.done(f"{name} {h}"))
                dve.wait_ge(*ve.at("u", i))
                dve.wait_ge(*te.at("state 0", i))
                dve.tensor_copy(HS[:, 0, :], wbank(2)[:, 0:2 * P]).then_inc(*ve.done("state 0"))
                for c in (1, 2):
                    dve.wait_ge(*ve.at(f"state {c - 1}", i))
                    e = ecl[:, csc, c:c + 1].rearrange("p h a -> p (h a)").unsqueeze(2).to_broadcast([P, HG, 64])
                    dve.tensor_tensor(HS[:, c, :].rearrange("p (h v) -> p h v", h=HG),
                                      HS[:, c - 1, :].rearrange("p (h v) -> p h v", h=HG), e, ALU.mult)\
                       .then_inc(*ve.done(f"decayed {c}"))
                    dve.wait_ge(*ve.at(f"decayed {c}", i))
                    dve.wait_ge(*te.at(f"state {c}", i))
                    dve.tensor_tensor(HS[:, c, :], HS[:, c, :], wbank(2 + c % 2)[:, 0:2 * P], ALU.add)\
                       .then_inc(*ve.done(f"state {c}"))
                taps(dve, ve, i, ue, 0, 4)
                for h in range(HG):
                    dve.wait_ge(*ae.at(f"exp cs {h}", i))
                    dve.tensor_tensor(ecs[:, h % 2, :], ecs[:, h % 2, :], stg[:, 3, :], ALU.mult)\
                       .then_inc(*ve.done(f"C exp cs {h}"))
                    dve.wait_ge(*ae.at(f"exp d {h}", i))
                    dve.tensor_tensor(Dd[:, h % 2, :], Dd[:, h % 2, :],
                                      cbm[:, :, :].rearrange("p c n -> p (c n)"), ALU.mult).then_inc(*ve.done(f"M {h}"))
                    if h < 2:
                        row(h + 2)
                    evac(h)
                    if h < HG - 1:
                        taps(dve, ve, i, ue, 4 + 5 * h, 9 + 5 * h)
                for d in range(2):
                    dve.wait_ge(*te.at("y 3", i))
                    w = at(dskip, i, 2, d)
                    dve.scalar_tensor_tensor(out=yf[:, d, :], in0=stg[:, d, :], scalar=w, in1=wbank(2 + d),
                                             op0=ALU.mult, op1=ALU.add).then_inc(*ve.done(f"y skip {d}"))
                    dve.wait_ge(*ve.at(f"y skip {d}", i))
                    dve.wait_ge(*ap_.at("silu z", i))
                    dve.tensor_tensor(yf[:, d, :], yf[:, d, :], gp[:, d, :], ALU.mult).then_inc(*ve.done(f"y z {d}"))
                taps(dve, ve, i, ue, 19, 27)
                for d in range(2):
                    dve.wait_ge(*ae.at("1/rms y", i))
                    dve.scalar_tensor_tensor(out=yf[:, d, :], in0=yf[:, d, :], scalar=at(snw, i, 2, d), in1=Rt[:, :],
                                             op0=ALU.mult, op1=ALU.mult).then_inc(*ve.done(f"y {d}"))
                for d in range(2):
                    dve.wait_ge(*ve.at(f"y {d}", i))
                    dve.tensor_copy(yh[:, d, :], yf[:, d, :]).then_inc(*ve.done(f"y hi {d}"))
                for d in range(2):
                    dve.wait_ge(*ve.at(f"y hi {d}", i))
                    dve.tensor_tensor(yl[:, d, :], yf[:, d, :], yh[:, d, :].bitcast(F32), ALU.subtract)\
                       .then_inc(*ve.done(f"y lo {d}"))
                taps(dve, ve, i, ue, 27, TAPS, 1)
                evac(4)
                evac(5)

            def out_tensor(pe, s, i, j, waits):
                for m in range(KD):
                    product(pe, s, i, j + m // 4, m % 4, yh, yl, waits)

            def adds_of(dve, s, i, j):
                def add(m):
                    a = (j + m // 4, m % 4)
                    dve.wait_ge(*tile_done(s, i, *a))
                    dve.tensor_tensor(xT[:, m, :], tile(s, *a), xT[:, m, :], ALU.add).then_inc(*taken(s, *a))
                return add

            def ln_tensor_mean(pe):
                pe.wait_ge(*ae.at("ln y", GROUPS - 1))
                pe.wait_ge(*ve.at(f"tap {TAPS - 1}", GROUPS - 1))
                for k in range(KD):
                    last = pe.matmul(wbank(0), ones, conv31[:, k, :], start=k == 0, stop=k == KD - 1)
                last.then_inc(*tl.done("mean"))

            def ln_tensor_var(pe):
                for k in range(KD):
                    pe.wait_ge(*al.at(f"square {k}"))
                    pe.matmul(wbank(1), ones, sq[:, k % 2, :], start=k == 0, stop=k == KD - 1)\
                      .then_inc(*tl.done(f"sum {k}"))

            def ln_vector(dve):
                dve.wait_ge(*al.at("mean"))
                for k in range(KD):
                    dve.tensor_tensor(conv31[:, k, :], conv31[:, k, :], acc[:, :], ALU.subtract)\
                       .then_inc(*vl.done(f"centered {k}"))

            def ln_scalar(act):
                act.wait_ge(*tl.at("mean"))
                act.activation(acc[:, :], wbank(0), ACT.Copy, scale=1.0 / D).then_inc(*al.done("mean"))
                for k in range(KD):
                    if k == 2:
                        for j in (0, 1):
                            hi_after(act, last_sec, 0, j, True)
                    if k >= 2:
                        act.wait_ge(*tl.at(f"sum {k - 2}"))
                    act.wait_ge(*vl.at(f"centered {k}"))
                    act.activation(sq[:, k % 2, :], conv31[:, k, :], ACT.Square).then_inc(*al.done(f"square {k}"))
                act.wait_ge(*tl.at(f"sum {KD - 1}"))
                act.activation(Rt[:, :], wbank(1), ACT.Ln, scale=1.0 / D, bias=bias[:, 3:4]).then_inc(*al.done("ln"))
                act.wait_ge(*al.at("ln"))
                act.activation(Rt[:, :], Rt[:, :], ACT.Exp, scale=-0.5).then_inc(*al.done("1/std"))

            def out_vector(dve, i, buf, add=lambda m: None):
                vz.turn()
                for x in range(2):
                    dve.tensor_tensor(stg[:, x, :], channel(conv31[:, :, :], i, 2, x), Rt[:, :], ALU.mult)\
                       .then_inc(*vz.done(f"normed {x}"))
                add(0)
                add(1)
                for x in range(2):
                    dve.wait_ge(*az.at(f"silu {x}", i))
                    dve.tensor_tensor(yf[:, x, :], stg[:, x, :], channel(zs[:, :, :], i, 2, x), ALU.mult)\
                       .then_inc(*vz.done(f"y {x}"))
                add(2)
                add(3)
                for x in range(2):
                    dve.wait_ge(*az.at(f"y hi {x}", i))
                    dve.tensor_tensor(ols[buf][:, x, :], yf[:, x, :], ohs[buf][:, x, :].bitcast(F32), ALU.subtract)\
                       .then_inc(*vz.done(f"y lo {x}"))
                for m in range(4, KD):
                    add(m)

            def out_scalar(act, i, buf):
                az.turn()
                for x in range(2):
                    act.wait_ge(*vz.at(f"normed {x}", i))
                    act.activation(stg[:, x, :], stg[:, x, :], ACT.Silu, scale=at(lnw, i, 2, x), bias=at(lnb, i, 2, x))\
                       .then_inc(*az.done(f"silu {x}"))
                for x in range(2):
                    act.wait_ge(*vz.at(f"y {x}", i))
                    act.activation(ohs[buf][:, x, :], yf[:, x, :], ACT.Copy).then_inc(*az.done(f"y hi {x}"))

            def out_tensor_b(pe, i, j, h, buf):
                for m in range(KD):
                    product(pe, out_sec, i, j + m // 4, m % 4, ohs[buf], ols[buf],
                            [vz.at(f"y lo {k}", h) for k in range(2)])

            def tensor(pe):
                nv["first product"](pe, dt_sec, 0, 0)
                rest = in_pieces(pe, first_sec, 0)
                for _ in range(3):
                    next(rest)
                for k in range(KD):
                    nv["second sum"](pe, k)
                for _ in rest:
                    pass
                dt_tensor(pe)

                def glu_turn(i, last):
                    for j in range(6):
                        product(pe, glu_sec, i, j, 0, xh, xl)
                loop(pe, GROUPS, glu_turn)

                def turn(i, last):
                    rest = in_pieces(pe, sec, i)
                    work_tensor(pe, i, lambda: next(rest, None))
                    for _ in rest:
                        pass
                    out_tensor(pe, sec, i, 6, [ve.at(f"y lo {k}", i) for k in range(2)])
                loop(pe, GROUPS - 1, turn)
                work_tensor(pe, GROUPS - 1, lambda: None)
                ln_tensor_mean(pe)
                out_tensor(pe, last_sec, 0, 0, [ve.at(f"y lo {k}", GROUPS - 1) for k in range(2)])
                ln_tensor_var(pe)

                def out_turn(i, last):
                    for b in range(2):
                        out_tensor_b(pe, i, 2 * b, 2 * i + b, b)
                loop(pe, 2, out_turn)

            def scalar(act):
                hi_after(act, dt_sec, 0, 0, True)
                dt_scalar(act)
                for j in range(3, 6):
                    hi_after(act, first_sec, 0, j, True)
                prep_scalar(act, first_sec, 0, 0)
                loop(act, GROUPS, lambda i, last: glu_scalar(act, i, last))

                def turn(i, last):
                    work_scalar(act, i, lambda j: hi_after(act, sec, i, j, last))
                    prep_scalar(act, sec, i, i + 1)
                    for j in (6, 7):
                        hi_after(act, sec, i, j, last)
                loop(act, GROUPS - 1, turn)
                work_scalar(act, GROUPS - 1, lambda j: None)
                ln_scalar(act)
                out_scalar(act, 0, 0)

                def out_turn(i, last):
                    out_scalar(act, 2 * i + 1, 1)
                    for j in (0, 1):
                        hi_after(act, out_sec, i, j, last)
                    if not last:
                        out_scalar(act, 2 * i + 2, 0)
                    for j in (2, 3):
                        hi_after(act, out_sec, i, j, last)
                loop(act, 2, out_turn)

            def vector(dve):
                dt_take(dve)
                for t in range(3):
                    evac(dve, first_sec, 0, t)
                dt_vector(dve)
                evac(dve, first_sec, 0, 3)

                def take_z(m):
                    if m in (0, 4):
                        evac(dve, first_sec, 0, 4 + m // 4)
                prep_vector(dve, first_sec, 0, 0, take_z)
                loop(dve, GROUPS, lambda i, last: glu_vector(dve, i))

                def turn(i, last):
                    work_vector(dve, i, lambda t: evac(dve, sec, i, t))
                    prep_vector(dve, sec, i, i + 1, adds_of(dve, sec, i, 6))
                loop(dve, GROUPS - 1, turn)
                work_vector(dve, GROUPS - 1, lambda t: None)
                ln_vector(dve)
                for j in (0, 1):
                    add_to_x(dve, last_sec, 0, j, range(4 * j, 4 * j + 4))
                dve.wait_ge(*al.at("1/std"))
                out_vector(dve, 0, 0)

                def out_turn(i, last):
                    out_vector(dve, 2 * i + 1, 1, lambda m: add_tile(dve, out_sec, i, m // 4, m % 4, m))
                    if last:
                        for j in (2, 3):
                            add_to_x(dve, out_sec, i, j, range(4 * j - 8, 4 * j - 4))
                    else:
                        out_vector(dve, 2 * i + 2, 0, lambda m: add_tile(dve, out_sec, i, 2 + m // 4, m % 4, m))
                loop(dve, 2, out_turn)

            def tables(act):
                act.wait_ge(*x_ready_before)
                act.dma_start(mU[:, :], T["gdn_masks"][:, 0:P]).then_inc(mask_in, 16)

            def sync(sp):
                for s in sections:
                    load_slots(s)(sp)

            def gpsimd(pool):
                for s in sections:
                    split_slots(s)(pool)

            x_ready.append(tile_taken(out_sec, 1, 3, 3))
            me = {"sync": sync, "gpsimd": gpsimd, "scalar": scalar, "tensor": tensor, "vector": vector,
                  "steps": {"scalar": [ab, ag, ap_, ae, al, az], "tensor": [tb, te, tl],
                            "vector": [vbs, vg, vp, ve, vl, vz]}}
            return merge({"scalar": tables}, nv, me)

        def gdn_layer(n, l):
            nv = norm(n, param("norm_g1"))
            gate_sec, first_sec, sec, last_sec = f"gdn_ba{n}", f"gdn_first{n}", f"gdn{n}", f"gdn_last{n}"
            H, DK = 8, 128
            DV = 256
            pre = sb("pre", [P, 4, 3 + SEQ])
            gp = sb("gp", [P, 2, SEQ])
            gs = sb("gs", [P, 2, SEQ])
            stg = sb("stg", [P, 4, SEQ])
            qn, kn, vs = stg[:, 0, :], stg[:, 1, :], stg[:, 2:4, :]
            rqk = sb("rqk", [P, 2, SEQ])
            kbe = sb("kbe", [P, NCH, P])
            kdec = sb("kdec", [P, NCH, P])
            vb = sb("vb", [P, NCH, DV])
            d1 = sb("d1", [P, NCH, P])
            d2 = sb("d2", [P, NCH, P])
            eg = sb("eg", [P, SEQ])
            egl = sb("egl", [P, NCH])
            N = sb("N", [P, NCH, P])
            A = sb("A", [P, NCH, P])
            U = sb("U", [P, NCH, P])
            NA = sb("NA", [P, 2, NCH, P])
            NB = sb("NB", [P, 2, NCH, P])
            yh = sb("gyh", [P, 2, SEQ], F32R)
            yl = sb("gyl", [P, 2, SEQ], F32R)
            Q = sb("Q", [P, SEQ])
            Gm = sb("Gm", [8, SEQ])
            gcol = sb("gcol", [P, 4, H, NCH])
            dmax, dmin = d2, d1
            Y, Dinv = d1, d2
            nwT = NB[:, 0, :, :]
            vn = NB[:, 1, :, :].rearrange("p c n -> p (c n)").rearrange("p (b v) -> p b v", b=2)
            S = NA[:, 0, :, :].rearrange("p c n -> p (c n)").rearrange("p (b v) -> p b v", b=2)
            yf = vb[:, :, :].rearrange("p c v -> p (c v)").rearrange("p (d s) -> p d s", d=2)
            osq = NA[:, :, :, :].rearrange("p a c n -> p a (c n)")
            ro = U[:, :, :].rearrange("p c n -> p (c n)")
            tmp = [pre[:, x, 0:SEQ] for x in range(4)] + [gp[:, 0, :], gp[:, 1, :]]
            conv = param("gdn_conv")
            ng = param("gdn_norm_g")
            dtb, alog = param("gdn_dt_bias"), param("gdn_a_log")
            onesrow = sb("g_onesrow", [P, SEQ])
            masks = sb("g_masks", [P, 6, P])
            maskU, nstrict, bd16, mT = masks[:, 0, :], masks[:, 1, :], masks[:, 2, :], \
                [masks[:, 3 + s, :] for s in range(3)]
            masks_in = sem("gdn_masks_in")
            ab, tb, vbs = steps(f"gdn_gate{n}", "scalar", "tensor", "vector")
            ap_, tp, vp = steps(f"gdn_prep{n}", "scalar", "tensor", "vector")
            ae, te, ve = steps(sec, "scalar", "tensor", "vector")
            x_ready_before = x_ready[-1]

            def chunks(ap):
                return ap.rearrange("p (c n) -> p c n", c=NCH)

            def over(ap):
                return ap.unsqueeze(1).to_broadcast([P, NCH, P])

            def each(q, i, width=P):
                c = gcol[:, q, ds(i, 1), :] if not isinstance(i, int) else gcol[:, q, i:i + 1, :]
                return c.rearrange("p a c -> p (a c)").unsqueeze(2).to_broadcast([P, NCH, width])

            def colv(ap, i, per, k):
                return ap[:, ds(i * per + k, 1)] if not isinstance(i, int) else ap[:, i * per + k:i * per + k + 1]

            b8, a8 = slice(0, 8), slice(32, 40)

            def gate_vector(dve):
                dve.wait_ge(*tile_done(gate_sec, 0, 0, 0))
                dve.tensor_tensor(tmp[0], tile(gate_sec, 0, 0), R[:, :], ALU.mult).then_inc(*taken(gate_sec, 0, 0))
                dve.memset(onesrow[:, :], 1.0).then_inc(*vbs.done("ones"))
                dve.memset(Q[:, :], 0.0).then_inc(*vbs.done("Q zero"))
                dve.wait_ge(*tile_taken(gate_sec, 0, 0, 0))
                dve.tensor_scalar(tmp[1][a8], tmp[0][a8], dtb[a8], None, ALU.add).then_inc(*vbs.done("z"))
                dve.wait_ge(*ab.at("exp b"))
                dve.tensor_scalar(tmp[2][b8], tmp[2][b8], 1.0, None, ALU.add).then_inc(*vbs.done("1+exp"))
                dve.wait_ge(*vbs.at("1+exp"))
                dve.reciprocal(Q[b8, :], tmp[2][b8]).then_inc(*vbs.done("beta"))
                dve.wait_ge(*ab.at("exp z"))
                dve.tensor_scalar(tmp[3][a8], tmp[2][a8], 1.0, None, ALU.add).then_inc(*vbs.done("u"))
                dve.wait_ge(*vbs.at("u"))
                dve.tensor_scalar(tmp[4][a8], tmp[3][a8], -1.0, None, ALU.add).then_inc(*vbs.done("u-1"))
                dve.wait_ge(*vbs.at("u-1"))
                dve.tensor_scalar(tmp[5][a8], tmp[4][a8], 0.0, None, ALU.is_equal).then_inc(*vbs.done("is 0"))
                dve.wait_ge(*vbs.at("is 0"))
                dve.tensor_tensor(tmp[4][a8], tmp[4][a8], tmp[5][a8], ALU.add).then_inc(*vbs.done("den"))
                dve.wait_ge(*vbs.at("den"))
                dve.reciprocal(tmp[4][a8], tmp[4][a8]).then_inc(*vbs.done("1/den"))
                dve.wait_ge(*ab.at("ln u"))
                dve.wait_ge(*vbs.at("1/den"))
                dve.tensor_tensor(tmp[3][a8], tmp[3][a8], tmp[4][a8], ALU.mult).then_inc(*vbs.done("ln/den"))
                dve.wait_ge(*vbs.at("ln/den"))
                dve.tensor_tensor(tmp[3][a8], tmp[3][a8], tmp[5][a8], ALU.add).then_inc(*vbs.done("ratio"))
                dve.wait_ge(*vbs.at("ratio"))
                dve.tensor_tensor(tmp[3][a8], tmp[3][a8], tmp[2][a8], ALU.mult).then_inc(*vbs.done("log1p"))
                dve.wait_ge(*vbs.at("log1p"))
                dve.scalar_tensor_tensor(out=tmp[3][a8], in0=tmp[1][a8], scalar=0.0, in1=tmp[3][a8], op0=ALU.max,
                                         op1=ALU.add).then_inc(*vbs.done("softplus"))
                dve.wait_ge(*vbs.at("softplus"))
                dve.wait_ge(*ab.at("exp a"))
                dve.tensor_scalar(tmp[3][a8], tmp[3][a8], egl[a8, 0:1], -1.0, ALU.mult, ALU.mult)\
                   .then_inc(*vbs.done("g"))
                dve.wait_ge(*vbs.at("g"))
                for c in range(NCH):
                    s = slice(c * P, (c + 1) * P)
                    dve.tensor_tensor_scan(Q[a8, s], onesrow[a8, s], tmp[3][a8, s], 0.0, ALU.mult, ALU.add)\
                       .then_inc(*vbs.done(f"cumsum {c}"))
                for c in range(NCH):
                    s = slice(c * P, (c + 1) * P)
                    dve.wait_ge(*vbs.at(f"cumsum {c}"))
                    dve.tensor_scalar(tmp[4][a8, s], Q[a8, s], Q[a8, c * P + P - 1:(c + 1) * P], None, ALU.subtract)\
                       .then_inc(*vbs.done(f"g-last {c}"))
                dve.wait_ge(*ab.at("exp g"))
                dve.tensor_tensor(Q[64:72, :], Q[b8, :], tmp[1][b8], ALU.mult).then_inc(*vbs.done("beta exp g"))
                dve.wait_ge(*tb.at("columns"))
                dve.tensor_copy(gcol[:, :, :, :],
                                wbank(0).rearrange("p (c q h) -> p q h c", c=NCH, q=4)[:, :, 0:H, :])\
                   .then_inc(*vbs.done("columns"))
                dve.memset(pre[:, :, 0:3], 0.0).then_inc(*vbs.done("pads"))
                dve.wait_ge(*vbs.at("pads"))
                dve.wait_ge(masks_in, 16)

            def gate_scalar(act):
                hi_after(act, gate_sec, 0, 0, True)
                act.wait_ge(*vbs.at("z"))
                act.activation(tmp[2][a8], tmp[1][a8], ACT.Abs).then_inc(*ab.done("abs z"))
                act.activation(tmp[2][b8], tmp[0][b8], ACT.Exp, scale=-1.0).then_inc(*ab.done("exp b"))
                act.wait_ge(*ab.at("abs z"))
                act.activation(tmp[2][a8], tmp[2][a8], ACT.Exp, scale=-1.0).then_inc(*ab.done("exp z"))
                act.activation(egl[a8, 0:1], alog[a8], ACT.Exp).then_inc(*ab.done("exp a"))
                act.wait_ge(*vbs.at("u-1"))
                act.activation(tmp[3][a8], tmp[3][a8], ACT.Ln).then_inc(*ab.done("ln u"))
                for j in range(3):
                    hi_after(act, first_sec, 0, j, True)
                act.wait_ge(*vbs.at("g-last 3"))
                act.activation(tmp[1][b8], Q[a8, :], ACT.Exp).then_inc(*ab.done("exp g"))
                act.activation(Q[96:104, :], tmp[4][a8], ACT.Exp, scale=-1.0).then_inc(*ab.done("exp last-g"))

            def gate_tensor(pe):
                pe.wait_ge(*vbs.at("beta exp g"))
                pe.wait_ge(*ab.at("exp last-g"))
                for c in range(NCH):
                    last = pe.transpose(wbank(0)[:, c * P:(c + 1) * P], Q[:, c * P:(c + 1) * P], ident)
                last.then_inc(*tb.done("columns"))

            def evacuate(dve, s, i, t, h):
                j, m = t, 0
                dve.wait_ge(*tile_done(s, i, j, m))
                if t == 0:
                    dve.wait_ge(*ap_.at("silu gate", h, 1))
                dst = pre[:, t, 3:] if t < 4 else gp[:, t - 4, :]
                dve.tensor_tensor(dst, tile(s, j, m), R[:, :], ALU.mult).then_inc(*taken(s, j, m))

            def tap_pieces(dve, s, i, h):
                vp.turn()
                for x in range(4):
                    for tap in range(4):
                        w = colv(conv, h, 16, x * 4 + tap)
                        if tap == 0:
                            dve.wait_ge(*tile_taken(s, i, x, 0))
                            dve.wait_ge(*ve.at("q exp g", h, 1))
                            dve.tensor_scalar(stg[:, x, :], pre[:, x, 0:SEQ], w, None, ALU.mult)\
                               .then_inc(*vp.done(f"tap {tap} {x}"))
                        else:
                            dve.wait_ge(*vp.at(f"tap {tap - 1} {x}", h))
                            dve.scalar_tensor_tensor(out=stg[:, x, :], in0=pre[:, x, tap:tap + SEQ], scalar=w,
                                                     in1=stg[:, x, :], op0=ALU.mult, op1=ALU.add)\
                               .then_inc(*vp.done(f"tap {tap} {x}"))
                        yield

            def normalize(dve, h):
                dve.tensor_scalar(Gm[:, :], Q[a8, :], ident[a8, ds(h + 32, 1)] if not isinstance(h, int) else
                                  ident[a8, 32 + h:33 + h], None, ALU.mult).then_inc(*vp.done("G masked"))
                for x, name in ((1, "k"), (0, "q")):
                    dve.wait_ge(*ap_.at(f"1/norm {name}", h))
                    dve.tensor_tensor(stg[:, x, :], stg[:, x, :], rqk[:, x, :], ALU.mult)\
                       .then_inc(*vp.done(f"{name} normed"))

            def silu_scalar(act, h):
                ap_.turn()
                act.wait_ge(*te.at("v tokens", h, 1))
                for x in (0, 1, 2, 3):
                    act.wait_ge(*vp.at(f"tap 3 {x}", h))
                    act.activation(stg[:, x, :], stg[:, x, :], ACT.Silu).then_inc(*ap_.done(f"silu {x}"))
                for x in (1, 0):
                    act.wait_ge(*ap_.at(f"silu {x}", h))
                    act.activation(sq[:, x, :], stg[:, x, :], ACT.Square).then_inc(*ap_.done(f"square {x}"))

            def norm_scalar(act, h):
                act.wait_ge(*ve.at("y gated 1", h, 1))
                act.wait_ge(*gate_taken(h))
                act.activation(gs[:, :, :], gp[:, :, :], ACT.Silu).then_inc(*ap_.done("silu gate"))
                for x, name in ((1, "k"), (0, "q")):
                    s = DK if name == "q" else 1.0
                    act.wait_ge(*tp.at(f"sum {x}", h))
                    act.activation(rqk[:, x, :], wbank(x), ACT.Ln, scale=float(s), bias=bias[:, 1 - x:2 - x])\
                       .then_inc(*ap_.done(f"ln {name}"))
                for x, name in ((1, "k"), (0, "q")):
                    act.wait_ge(*ap_.at(f"ln {name}", h))
                    act.activation(rqk[:, x, :], rqk[:, x, :], ACT.Exp, scale=-0.5)\
                       .then_inc(*ap_.done(f"1/norm {name}"))

            def gate_taken(h):
                if isinstance(h, int) and h == 0:
                    return tile_taken(first_sec, 0, 5, 0)
                return tile_taken(sec, h - 1, 5, 0)

            def prep_tensor(pe, h):
                tp.turn()
                pe.wait_ge(*ve.at("y gated 1", h, 1))
                for x in (1, 0):
                    pe.wait_ge(*ap_.at(f"square {x}", h))
                    pe.matmul(wbank(x), ones, sq[:, x, :], start=True, stop=True).then_inc(*tp.done(f"sum {x}"))

            def work_tensor(pe, i, more):
                te.turn()

                def four(b, left, right, name, start=True, stop=True):
                    for c in range(NCH):
                        last = pe.matmul(wbank(b)[:, c * P:(c + 1) * P], left[:, c, :], right[:, c, :],
                                         start=True, stop=True)
                    last.then_inc(*te.done(name))

                def four_transposes(b, src, name):
                    for c in range(NCH):
                        last = pe.transpose(wbank(b)[:, c * P:(c + 1) * P], src[:, c, :], ident)
                    last.then_inc(*te.done(name))

                knc, qnc = chunks(kn), chunks(qn)
                pe.wait_ge(*vp.at("G masked", i))
                pe.matmul(wbank(3), ones[0:8, :], Gm[:, :], start=True, stop=True).then_inc(*te.done("G row"))
                pe.wait_ge(*vp.at("k normed", i))
                four_transposes(0, knc, "k tokens")
                pe.wait_ge(*ap_.at("silu 3", i))
                for c in range(NCH):
                    for d in range(2):
                        at = (c % 2) * DV + d * P
                        last = pe.transpose(wbank(1 + c // 2)[:, at:at + P], vs[:, d, c * P:(c + 1) * P], ident)
                last.then_inc(*te.done("v tokens"))
                more()
                more()
                pe.wait_ge(*ve.at("k dec", i))
                four(0, knc, knc, "kk")
                pe.wait_ge(*ve.at("v beta 1", i))
                pe.wait_ge(*vp.at("q normed", i))
                four(1, knc, qnc, "kq")
                more()
                pe.wait_ge(*ve.at("N", i))
                four_transposes(2, N, "N transposed")
                more()
                pe.wait_ge(*ve.at("U1", i))
                Nt = NB[:, 0, :, :]
                four(0, Nt, N, "N2")
                pe.wait_ge(*ve.at("A", i))
                four(1, N, Nt, "N2 transposed")
                more()
                pe.wait_ge(*ve.at("N2", i))
                four(2, NA[:, 0], U, "U2")
                pe.wait_ge(*ve.at("N2 transposed", i))
                four(0, NA[:, 1], NA[:, 0], "N4")
                four(1, NA[:, 0], NA[:, 1], "N4 transposed")
                more()
                pe.wait_ge(*ae.at("N4", i))
                pe.wait_ge(*ve.at("U2", i))
                four(2, NB[:, 0], U, "U4")
                pe.wait_ge(*ve.at("N4 transposed", i))
                four(0, NB[:, 1], NB[:, 0], "N8")
                more()
                pe.wait_ge(*ae.at("N8", i))
                pe.wait_ge(*ve.at("U4", i))
                four(1, NA[:, 0], U, "U8")
                more()
                for s in range(3):
                    pe.wait_ge(*ve.at("U8" if s == 0 else f"U join {s - 1}", i))
                    four(0, N, U, f"join {s}")
                    four_transposes(2, U, f"U transposed {s}")
                    more()
                    pe.wait_ge(*ve.at(f"Y {s}", i))
                    pe.wait_ge(*ae.at(f"U transposed {s}", i))
                    four(1, Dinv, Y, f"joined {s}")
                    more()
                pe.wait_ge(*ve.at("U join 2", i))
                four(0, kbe, U, "w")
                for c in range(NCH):
                    if c >= 1:
                        pe.wait_ge(*ve.at(f"state {c - 1}", i))
                        pe.wait_ge(*ae.at("-w", i))
                    pe.matmul(wbank(1)[:, 0:DV], U[:, c, :], vb[:, c, :], start=True, stop=c == 0)\
                      .then_inc(*te.done(f"v new {c} a"))
                    if c:
                        pe.matmul(wbank(1)[:, 0:DV], nwT[:, c, :], S[:, (c - 1) % 2, :], start=False, stop=True)\
                          .then_inc(*te.done(f"v new {c}"))
                        for d in range(2):
                            pe.matmul(wbank(2 + d)[:, c * P:(c + 1) * P], S[:, (c - 1) % 2, d * P:(d + 1) * P],
                                      chunks(eg[:, :])[:, c, :], start=True, stop=False)
                        more(1)
                        pe.wait_ge(*ve.at(f"v new {c}", i))
                        for d in range(2):
                            last = pe.matmul(wbank(2 + d)[:, c * P:(c + 1) * P], vn[:, c % 2, d * P:(d + 1) * P],
                                             A[:, c, :], start=False, stop=True)
                    else:
                        more(1)
                        pe.wait_ge(*ve.at(f"v new {c}", i))
                        for d in range(2):
                            last = pe.matmul(wbank(2 + d)[:, c * P:(c + 1) * P], vn[:, c % 2, d * P:(d + 1) * P],
                                             A[:, c, :], start=True, stop=True)
                    last.then_inc(*te.done(f"o {c}"))
                    if c < NCH - 1:
                        if c == 0:
                            pe.wait_ge(*ae.at("-w", i))
                        pe.matmul(wbank(0)[:, 0:DV], kdec[:, c, :], vn[:, c % 2, :], start=True, stop=True)\
                          .then_inc(*te.done(f"state {c}"))
                    more(1)
                for d in range(2):
                    pe.wait_ge(*ae.at(f"o square {d}", i))
                    pe.matmul(wbank(1), ones, osq[:, d, :], start=d == 0, stop=d == 1).then_inc(*te.done(f"o sum {d}"))

            def work_scalar(act, i, between):
                ae.turn()
                act.wait_ge(*te.at("G row", i))
                act.activation(eg[:, :], wbank(3), ACT.Exp).then_inc(*ae.done("exp G"))
                act.wait_ge(*ve.at("d min", i))
                act.activation(dmin[:, :, :], dmin[:, :, :], ACT.Exp).then_inc(*ae.done("E1"))
                act.wait_ge(*ve.at("d max", i))
                act.activation(dmax[:, :, :], dmax[:, :, :], ACT.Exp, scale=-1.0).then_inc(*ae.done("E2"))
                between(0)
                act.wait_ge(*te.at("N4", i))
                act.activation(NB[:, 0, :, :], chunks(wbank(0)), ACT.Copy).then_inc(*ae.done("N4"))
                act.wait_ge(*te.at("N8", i))
                act.activation(NA[:, 0, :, :], chunks(wbank(0)), ACT.Copy).then_inc(*ae.done("N8"))
                for s in range(3):
                    act.wait_ge(*te.at(f"U transposed {s}", i))
                    act.activation(Dinv[:, :, :], chunks(wbank(2)), ACT.Copy).then_inc(*ae.done(f"U transposed {s}"))
                    if s != 1:
                        between(1 if s == 0 else 2)
                act.wait_ge(*te.at("w", i))
                act.activation(nwT, chunks(wbank(0)), ACT.Copy, scale=-1.0).then_inc(*ae.done("-w"))
                between(3)
                act.wait_ge(*te.at("o 3", i))
                for d in range(2):
                    act.activation(osq[:, d, :], wbank(2 + d), ACT.Square).then_inc(*ae.done(f"o square {d}"))
                act.wait_ge(*te.at("o sum 1", i))
                act.activation(ro, wbank(1), ACT.Ln, scale=1.0 / DV, bias=bias[:, 0:1]).then_inc(*ae.done("ln o"))
                act.wait_ge(*ae.at("ln o", i))
                act.activation(ro, ro, ACT.Exp, scale=-0.5).then_inc(*ae.done("1/rms o"))

            def work_vector(dve, i, evac, fill):
                ve.turn()
                dve.wait_ge(*te.at("k tokens", i))
                dve.tensor_tensor(kbe[:, :, :], chunks(wbank(0)), each(2, i), ALU.mult).then_inc(*ve.done("k beta"))
                dve.tensor_tensor(kdec[:, :, :], chunks(wbank(0)), each(3, i), ALU.mult).then_inc(*ve.done("k dec"))
                dve.wait_ge(*ae.at("exp G", i))
                dve.tensor_tensor(d1[:, :, :], chunks(wbank(3)), each(1, i), ALU.subtract).then_inc(*ve.done("d"))
                dve.wait_ge(*ve.at("d", i))
                dve.tensor_scalar(d2[:, :, :], d1[:, :, :], 0.0, None, ALU.max).then_inc(*ve.done("d max"))
                dve.wait_ge(*ve.at("d max", i))
                dve.tensor_scalar(d1[:, :, :], d1[:, :, :], 0.0, None, ALU.min).then_inc(*ve.done("d min"))
                dve.wait_ge(*te.at("v tokens", i))
                for h in range(2):
                    c = gcol[:, 0, ds(i, 1), 2 * h:2 * h + 2] if not isinstance(i, int) else \
                        gcol[:, 0, i:i + 1, 2 * h:2 * h + 2]
                    dve.tensor_tensor(vb[:, 2 * h:2 * h + 2, :], wbank(1 + h).rearrange("p (c v) -> p c v", c=2),
                                      c.rearrange("p a c -> p (a c)").unsqueeze(2).to_broadcast([P, 2, DV]),
                                      ALU.mult).then_inc(*ve.done(f"v beta {h}"))
                dve.wait_ge(*ae.at("E2", i))
                dve.tensor_tensor(d2[:, :, :], d2[:, :, :], over(nstrict), ALU.mult).then_inc(*ve.done("E2 masked"))
                dve.tensor_tensor(d1[:, :, :], d1[:, :, :], over(maskU), ALU.mult).then_inc(*ve.done("E1 masked"))
                dve.wait_ge(*ve.at("E2 masked", i))
                dve.tensor_tensor(d2[:, :, :], d2[:, :, :], each(0, i), ALU.mult).then_inc(*ve.done("E2 beta"))
                dve.wait_ge(*te.at("kk", i))
                dve.wait_ge(*ve.at("E2 beta", i))
                dve.tensor_tensor(N[:, :, :], chunks(wbank(0)), d2[:, :, :], ALU.mult).then_inc(*ve.done("N"))
                dve.wait_ge(*te.at("kq", i))
                dve.tensor_tensor(A[:, :, :], chunks(wbank(1)), d1[:, :, :], ALU.mult).then_inc(*ve.done("A"))
                dve.wait_ge(*ae.at("exp G", i))
                dve.tensor_copy(egl[:, :], eg[:, P - 1::P]).then_inc(*ve.done("exp G last"))
                dve.wait_ge(*te.at("N transposed", i))
                dve.tensor_tensor(NB[:, 0, :, :], chunks(wbank(2)), over(bd16), ALU.mult).then_inc(*ve.done("Nt"))
                dve.wait_ge(*ve.at("Nt", i))
                dve.tensor_tensor(U[:, :, :], NB[:, 0, :, :], over(ident), ALU.add).then_inc(*ve.done("U1"))
                dve.tensor_tensor(eg[:, :], qn, eg[:, :], ALU.mult).then_inc(*ve.done("q exp g"))
                dve.wait_ge(*te.at("N2", i))
                dve.tensor_tensor(NA[:, 0, :, :], chunks(wbank(0)), over(bd16), ALU.mult).then_inc(*ve.done("N2"))
                dve.wait_ge(*te.at("N2 transposed", i))
                dve.tensor_tensor(NA[:, 1, :, :], chunks(wbank(1)), over(bd16), ALU.mult)\
                   .then_inc(*ve.done("N2 transposed"))
                evac(0)
                dve.wait_ge(*te.at("U2", i))
                dve.wait_ge(*ve.at("N2 transposed", i))
                dve.tensor_tensor(U[:, :, :], U[:, :, :], chunks(wbank(2)), ALU.add).then_inc(*ve.done("U2"))
                fill()
                dve.wait_ge(*te.at("N4 transposed", i))
                dve.tensor_copy(NB[:, 1, :, :], chunks(wbank(1))).then_inc(*ve.done("N4 transposed"))
                fill()
                dve.wait_ge(*te.at("U4", i))
                dve.tensor_tensor(U[:, :, :], U[:, :, :], chunks(wbank(2)), ALU.add).then_inc(*ve.done("U4"))
                fill()
                dve.wait_ge(*te.at("U8", i))
                dve.wait_ge(*ve.at("U4", i))
                dve.tensor_tensor(U[:, :, :], U[:, :, :], chunks(wbank(1)), ALU.add).then_inc(*ve.done("U8"))
                fill()
                for s in range(3):
                    dve.wait_ge(*te.at(f"join {s}", i))
                    dve.tensor_tensor(Y[:, :, :], chunks(wbank(0)), over(mT[s]), ALU.mult).then_inc(*ve.done(f"Y {s}"))
                    if s == 1:
                        fill()
                    else:
                        evac(1 if s == 0 else 2)
                    dve.wait_ge(*te.at(f"joined {s}", i))
                    dve.tensor_tensor(U[:, :, :], U[:, :, :], chunks(wbank(1)), ALU.add)\
                       .then_inc(*ve.done(f"U join {s}"))
                    fill()
                for c in range(NCH):
                    dve.wait_ge(*te.at(f"v new {c}" if c else "v new 0 a", i))
                    dve.tensor_copy(vn[:, c % 2, :], wbank(1)[:, 0:DV]).then_inc(*ve.done(f"v new {c}"))
                    if c < 2:
                        fill()
                    if c < NCH - 1:
                        dve.wait_ge(*te.at(f"state {c}", i))
                        if c == 0:
                            dve.tensor_copy(S[:, 0, :], wbank(0)[:, 0:DV]).then_inc(*ve.done("state 0"))
                        else:
                            dve.wait_ge(*ve.at(f"state {c - 1}", i))
                            dve.scalar_tensor_tensor(out=S[:, c % 2, :], in0=S[:, (c - 1) % 2, :],
                                                     scalar=egl[:, c:c + 1], in1=wbank(0)[:, 0:DV],
                                                     op0=ALU.mult, op1=ALU.add).then_inc(*ve.done(f"state {c}"))
                        if c < 2:
                            fill()
                    if c == 2:
                        evac(3)
                dve.wait_ge(*te.at("o 3", i))
                dve.wait_ge(*ap_.at("silu gate", i))
                for d in range(2):
                    dve.wait_ge(*ae.at(f"o square {d}", i))
                    dve.scalar_tensor_tensor(out=yf[:, d, :], in0=wbank(2 + d), scalar=ng[:, d:d + 1],
                                             in1=gs[:, d, :], op0=ALU.mult, op1=ALU.mult)\
                       .then_inc(*ve.done(f"y gated {d}"))
                for _ in range(4):
                    fill()
                dve.wait_ge(*ae.at("1/rms o", i))
                for d in range(2):
                    dve.wait_ge(*ve.at(f"y gated {d}", i))
                    dve.tensor_tensor(yf[:, d, :], yf[:, d, :], ro, ALU.mult).then_inc(*ve.done(f"y {d}"))
                for d in range(2):
                    dve.wait_ge(*ve.at(f"y {d}", i))
                    dve.tensor_copy(yh[:, d, :], yf[:, d, :]).then_inc(*ve.done(f"y hi {d}"))
                for d in range(2):
                    dve.wait_ge(*ve.at(f"y hi {d}", i))
                    dve.tensor_tensor(yl[:, d, :], yf[:, d, :], yh[:, d, :].bitcast(F32), ALU.subtract)\
                       .then_inc(*ve.done(f"y lo {d}"))

            def pieces(pe, s, i):
                for t in range(6):
                    for k in range(KD):
                        product(pe, s, i, t, 0, xh, xl, None, k, k + 1)
                        yield

            def out_tensor(pe, s, i, h, j):
                for m in range(KD):
                    product(pe, s, i, j + m // 4, m % 4, yh, yl, [ve.at(f"y lo {k}", h) for k in range(2)])

            def adds_of(dve, s, i, j):
                def add(m):
                    at = (j + m // 4, m % 4)
                    dve.wait_ge(*tile_done(s, i, *at))
                    dve.tensor_tensor(xT[:, m, :], tile(s, *at), xT[:, m, :], ALU.add).then_inc(*taken(s, *at))
                return add

            def tensor(pe):
                nv["first product"](pe, gate_sec, 0, 0)
                rest = pieces(pe, first_sec, 0)
                for _ in range((BANKS - 1) * KD):
                    next(rest)
                gate_tensor(pe)
                for _ in rest:
                    pass
                prep_tensor(pe, 0)

                def turn(i, last):
                    rest = pieces(pe, sec, i)
                    work_tensor(pe, i, lambda n=2: [next(rest, None) for _ in range(n)])
                    for _ in rest:
                        pass
                    prep_tensor(pe, i + 1)
                    out_tensor(pe, sec, i, i, 6)
                loop(pe, H - 1, turn)
                work_tensor(pe, H - 1, lambda n=2: None)
                out_tensor(pe, last_sec, 0, H - 1, 0)

            def scalar(act):
                gate_scalar(act)
                for j in range(3, 6):
                    if j == 4:
                        silu_scalar(act, 0)
                    hi_after(act, first_sec, 0, j, True)
                norm_scalar(act, 0)

                def turn(i, last):
                    work_scalar(act, i, lambda k: hi_after(act, sec, i, k, last))
                    silu_scalar(act, i + 1)
                    for j in (4, 5):
                        hi_after(act, sec, i, j, last)
                    norm_scalar(act, i + 1)
                    for j in (6, 7):
                        hi_after(act, sec, i, j, last)
                loop(act, H - 1, turn)
                work_scalar(act, H - 1, lambda k: None)
                for j in (0, 1):
                    hi_after(act, last_sec, 0, j, True)

            def vector(dve):
                gate_vector(dve)
                for t in range(4):
                    evacuate(dve, first_sec, 0, t, 0)
                for x, _ in enumerate(tap_pieces(dve, first_sec, 0, 0)):
                    if x == 5:
                        evacuate(dve, first_sec, 0, 4, 0)
                evacuate(dve, first_sec, 0, 5, 0)
                normalize(dve, 0)

                def turn(i, last):
                    conv_of_next = tap_pieces(dve, sec, i, i + 1)
                    work_vector(dve, i, lambda t: evacuate(dve, sec, i, t, i + 1), lambda: next(conv_of_next, None))
                    for _ in conv_of_next:
                        pass
                    for t in (4, 5):
                        evacuate(dve, sec, i, t, i + 1)
                    add = adds_of(dve, sec, i, 6)
                    for m in range(4):
                        add(m)
                    normalize(dve, i + 1)
                    for m in range(4, 8):
                        add(m)
                loop(dve, H - 1, turn)
                work_vector(dve, H - 1, lambda t: None, lambda: None)
                for j in (0, 1):
                    add_to_x(dve, last_sec, 0, j, range(4 * j, 4 * j + 4))

            def tables(act):
                act.wait_ge(*x_ready_before)
                act.dma_start(masks[:, :, :], T["gdn_masks"].rearrange("p (k n) -> p k n", k=6)).then_inc(masks_in, 16)

            def sync(sp):
                for s in (gate_sec, first_sec, sec, last_sec):
                    load_slots(s)(sp)

            def gpsimd(pool):
                for s in (gate_sec, first_sec, sec, last_sec):
                    split_slots(s)(pool)

            x_ready.append(tile_taken(last_sec, 0, 1, 3))
            me = {"sync": sync, "gpsimd": gpsimd, "scalar": scalar, "tensor": tensor, "vector": vector,
                  "steps": {"scalar": [ab, ap_, ae], "tensor": [tb, tp, te], "vector": [vbs, vp, ve]}}
            return merge({"scalar": tables}, nv, me)

        def rotary_tables(dve, act, st, sa, which, pos_i, cosT, sinT, tmp, inv, engine):
            a, k, m = tmp
            if engine == "vector":
                dve.tensor_copy(a, pos_i).then_inc(*st.done("pos"))
                dve.wait_ge(*st.at("pos"))
                dve.tensor_scalar(a, a, inv, None, ALU.mult).then_inc(*st.done("angle"))
                dve.wait_ge(*st.at("angle"))
                dve.tensor_scalar(k, a, 1.0 / (2 * math.pi), ROUND, ALU.mult, ALU.add).then_inc(*st.done("turns a"))
                dve.wait_ge(*st.at("turns a"))
                dve.tensor_scalar(k, k, -ROUND, None, ALU.add).then_inc(*st.done("turns"))
                dve.wait_ge(*st.at("turns"))
                for x, part in enumerate(TWO_PI):
                    dve.scalar_tensor_tensor(out=a, in0=k, scalar=-part, in1=a, op0=ALU.mult, op1=ALU.add)\
                       .then_inc(*st.done(f"less {x}"))
                    dve.wait_ge(*st.at(f"less {x}"))
                dve.tensor_scalar(a, a, PI_BELOW, -PI_BELOW, ALU.min, ALU.max).then_inc(*st.done("r"))
            else:
                act.wait_ge(*st.at("r"))
                act.activation(m, a, ACT.Abs).then_inc(*sa.done("|r|"))
                act.activation(sinT, a, ACT.Sin).then_inc(*sa.done("sin"))
                act.wait_ge(*sa.at("|r|"))
                act.activation(cosT, m, ACT.Sin, scale=-1.0, bias=bias[:, 2:3]).then_inc(*sa.done("cos"))

        def mla_layer(n, l):
            nv = norm(n, param("norm_g2"))
            c_sec, first_sec, sec, last_sec = f"mla_c{n}", f"mla_first{n}", f"mla{n}", f"mla_last{n}"
            PAIRS, CQ, CKV = 8, 6, 4
            SCALE = 192 ** -0.5
            qh = sb("cqh", [P, CQ, SEQ], F32R)
            ql = sb("cql", [P, CQ, SEQ], F32R)
            kh = sb("ckvh", [P, CKV, SEQ], F32R)
            kl = sb("ckvl", [P, CKV, SEQ], F32R)
            cosT = sb("cosT", [P, SEQ])
            sinT = sb("sinT", [P, SEQ])
            kr = sb("kr", [P, SEQ])
            mk = sb("mk", [P, 2, P])
            rot = mk[:, 0, :]
            maskb = sb("maskb", [P, 2, P], BF16)
            identb, causal = maskb[:, 0, :], maskb[:, 1, :]
            mxs = sb("mxs", [P, 8])
            nmx = sb("nmx", [P, 8])
            rs = sb("rs", [P, 8])
            ri = sb("ri", [P, 8])
            work = sb("mwork", [P, 20 * SEQ])

            def part(at, k):
                return work[:, at * SEQ:(at + k) * SEQ].rearrange("p (k s) -> p k s", s=SEQ)
            qn, kn, qrz, vT = part(0, 2), part(2, 2), part(4, 2), part(6, 2)
            gs, vt = part(8, 2), part(10, 2)
            vt = vt.rearrange("p k (c v) -> p (k c) v", v=2 * P)
            prob = work[:, 12 * SEQ:17 * SEQ].rearrange("p (h n) -> p h n", h=2)
            pT = work[:, 17 * SEQ:17 * SEQ + 1280]
            c = part(0, CQ + CKV)
            pos_i = part(12, 1)[:, 0, :].bitcast(I32)
            tmp = [part(13, 1)[:, 0, :], part(14, 1)[:, 0, :], part(15, 1)[:, 0, :]]
            krx = part(16, 1)[:, 0, :]
            rc = [part(17, 1)[:, 0, :], part(18, 1)[:, 0, :]]
            yh = sb("myh", [P, 2, SEQ], F32R)
            yl = sb("myl", [P, 2, SEQ], F32R)
            xr, xt = sq[:, 0, :], sq[:, 1, :]
            pos_in = sem("mla_pos_in")
            gq, gkv = param("mla_q_norm_g"), param("mla_kv_norm_g")
            ab, tb, vbs = steps(f"mla_c{n}", "scalar", "tensor", "vector")
            ap_, tp, vp = steps(f"mla_prep{n}", "scalar", "tensor", "vector")
            ae, te, ve = steps(sec, "scalar", "tensor", "vector")
            x_ready_before = x_ready[-1]
            TILES = [(0, 0), (0, 1), (1, 0), (1, 1), (2, 0), (3, 0), (4, 0), (5, 0), (6, 0)]
            off_q = [sum(range(t + 1)) * P for t in range(NCH)]
            off_k = [sum(NCH - u for u in range(t)) * P for t in range(NCH)]

            def c_slot(t):
                return t if t < CKV else t + 1

            def c_vector(dve):
                dve.wait_ge(pos_in, 32)
                dve.tensor_copy(identb, ident).then_inc(*vbs.done("identity"))
                dve.tensor_copy(causal, mk[:, 1, :]).then_inc(*vbs.done("mask"))
                rotary_tables(dve, None, vbs, ab, "vector", pos_i, cosT[:, :], sinT[:, :], tmp, param("mla_inv"),
                              "vector")

                def take(t):
                    dve.wait_ge(*tile_done(c_sec, 0, c_slot(t), 0))
                    dve.tensor_tensor(c[:, t, :], tile(c_sec, c_slot(t), 0), R[:, :], ALU.mult)\
                       .then_inc(*taken(c_sec, c_slot(t), 0))

                def operand(t):
                    q = t >= CKV
                    hi, lo = (qh[:, t - CKV, :], ql[:, t - CKV, :]) if q else (kh[:, t, :], kl[:, t, :])
                    g = gq[:, t - CKV:t - CKV + 1] if q else gkv[:, t:t + 1]
                    dve.scalar_tensor_tensor(out=c[:, t, :], in0=c[:, t, :], scalar=g, in1=rc[q],
                                             op0=ALU.mult, op1=ALU.mult).then_inc(*vbs.done(f"c {t}"))
                    dve.wait_ge(*vbs.at(f"c {t}"))
                    dve.tensor_copy(hi, c[:, t, :]).then_inc(*vbs.done(f"c hi {t}"))
                    dve.wait_ge(*vbs.at(f"c hi {t}"))
                    dve.tensor_tensor(lo, c[:, t, :], hi.bitcast(F32), ALU.subtract).then_inc(*vbs.done(f"c lo {t}"))

                for t in range(CKV):
                    take(t)
                dve.wait_ge(*tile_done(c_sec, 0, CKV, 0))
                dve.tensor_tensor(krx, tile(c_sec, CKV, 0), R[:, :], ALU.mult).then_inc(*taken(c_sec, CKV, 0))
                dve.wait_ge(*ab.at("1/rms kv"))
                for t in range(CKV):
                    take(CKV + t)
                    operand(t)
                dve.wait_ge(*tile_taken(c_sec, 0, CKV, 0))
                dve.wait_ge(*ab.at("cos"))
                dve.tensor_tensor(kr[:, :], krx, cosT[:, :], ALU.mult).then_inc(*vbs.done("k cos"))
                dve.wait_ge(*vbs.at("k cos"))
                dve.wait_ge(*tb.at("k rotated"))
                dve.tensor_tensor(krx, wbank(2), sinT[:, :], ALU.mult).then_inc(*vbs.done("k sin"))
                dve.wait_ge(*vbs.at("k sin"))
                dve.tensor_tensor(kr[:, :], kr[:, :], krx, ALU.add).then_inc(*vbs.done("k rope"))
                for t in range(2 * CKV, CQ + CKV):
                    take(t)
                dve.wait_ge(*ab.at("1/rms q"))
                for t in range(CKV, CQ + CKV):
                    operand(t)
                dve.wait_ge(*vbs.at(f"c lo {CQ + CKV - 1}"))
                dve.memset(qrz[:, :, :], 0.0).then_inc(*vbs.done("q rope 0"))
                dve.wait_ge(*vbs.at("q rope 0"))

            def c_scalar(act):
                rotary_tables(None, act, vbs, ab, "scalar", pos_i, cosT[:, :], sinT[:, :], tmp, None, "scalar")
                for j in range(CKV + 1 + CQ):
                    hi_after(act, c_sec, 0, j, True)
                    if j == CKV:
                        continue
                    t = j if j < CKV else j - 1
                    if t >= 2:
                        act.wait_ge(*tb.at(f"sum {t - 2}"))
                    act.wait_ge(*tile_taken(c_sec, 0, j, 0))
                    act.activation(sq[:, t % 2, :], c[:, t, :], ACT.Square).then_inc(*ab.done(f"square {t}"))
                    if t in (CKV - 1, CKV + CQ - 1):
                        q = t >= CKV
                        act.wait_ge(*tb.at(f"sum {t}"))
                        act.activation(Rt[:, :], wbank(int(q)), ACT.Ln, scale=1.0 / ((CQ if q else CKV) * P),
                                       bias=bias[:, 0:1]).then_inc(*ab.done(f"ln {t}"))
                        act.wait_ge(*ab.at(f"ln {t}"))
                        act.activation(rc[q], Rt[:, :], ACT.Exp, scale=-0.5)\
                           .then_inc(*ab.done("1/rms q" if q else "1/rms kv"))

            def c_tensor(pe):
                def total(t):
                    q = t >= CKV
                    pe.wait_ge(*ab.at(f"square {t}"))
                    pe.matmul(wbank(int(q)), ones, sq[:, t % 2, :], start=t in (0, CKV),
                              stop=t in (CKV - 1, CKV + CQ - 1))\
                      .then_inc(*tb.done(f"sum {t}"))
                for j in range(CKV + 1 + CQ):
                    if j == 0:
                        nv["first product"](pe, c_sec, 0, 0)
                    else:
                        product(pe, c_sec, 0, j, 0, xh, xl)
                    if 1 <= j <= CKV:
                        total(j - 1)
                    elif j > CKV + 1:
                        total(j - 2)
                    if j == CKV + 2:
                        pe.wait_ge(*tile_taken(c_sec, 0, CKV, 0))
                        pe.matmul(wbank(2), rot, krx, start=True, stop=True).then_inc(*tb.done("k rotated"))
                total(CKV + CQ - 1)

            def in_pieces(pe, s, i, waits=False):
                for t, (j, m) in enumerate(TILES):
                    nk = W.sec[s]["items"][j][0]
                    hi, lo = (kh, kl) if j < 2 else (qh, ql) if j < 5 else (xh, xl)
                    w = None
                    if waits and j < 5:
                        w = [vbs.at(f"c lo {k + (0 if j < 2 else CKV)}") for k in range(nk)]
                    for k in range(0, nk, 2):
                        product(pe, s, i, j, m, hi, lo, w, k, k + 2)
                        yield

            def evac_scalar(act, s, i, t):
                j, m = TILES[t]
                act.wait_ge(*tile_done(s, i, j, m))
                dst = [vT[:, 0, :], vT[:, 1, :], kn[:, 0, :], kn[:, 1, :], qn[:, 0, :], qn[:, 1, :], xr][t]
                act.activation(dst, tile(s, j, m), ACT.Copy).then_inc(*taken(s, j, m))

            def evac_gate(dve, s, i, x):
                j, m = TILES[7 + x]
                dve.wait_ge(*tile_done(s, i, j, m))
                dve.tensor_tensor(gs[:, x, :], tile(s, j, m), R[:, :], ALU.mult).then_inc(*taken(s, j, m))

            def prep_tensor(pe, s, i, h):
                tp.turn()
                pe.wait_ge(*tile_taken(s, i, *TILES[6]))
                pe.wait_ge(*ve.at("y 1", h, 1))
                pe.matmul(wbank(2), rot, xr, start=True, stop=True).then_inc(*tp.done("rotated"))

            def prep_vector(dve, s, i, h):
                vp.turn()
                dve.wait_ge(*tile_taken(s, i, *TILES[6]))
                dve.tensor_tensor(xt, xr, cosT[:, :], ALU.mult).then_inc(*vp.done("cos"))
                dve.wait_ge(*tp.at("rotated", h))
                dve.tensor_tensor(Rt[:, :], wbank(2), sinT[:, :], ALU.mult).then_inc(*vp.done("sin"))
                dve.wait_ge(*vp.at("sin", h))
                for x in range(2):
                    r = slice(64 * x, 64 * x + 64)
                    dve.tensor_tensor(qrz[r, x, :], xt[r, :], Rt[r, :], ALU.add).then_inc(*vp.done(f"q rope {x}"))

            def prep_scalar(act, s, i, h):
                ap_.turn()
                act.wait_ge(*tile_taken(s, i, *TILES[7]))
                act.wait_ge(*tile_taken(s, i, *TILES[8]))
                act.activation(gs[:, :, :], gs[:, :, :], ACT.Silu).then_inc(*ap_.done("silu"))

            def work_tensor(pe, s, i, h, more):
                te.turn()
                pe.wait_ge(*vp.at("q rope 1", h))
                for cc in range(NCH):
                    for d in range(2):
                        at = (cc % 2) * 2 * P + d * P
                        last = pe.transpose(wbank(cc // 2)[:, at:at + P], vT[:, d, cc * P:(cc + 1) * P], ident)
                last.then_inc(*te.done("v tokens"))
                for x in range(2 * NCH):
                    hd, t = x // NCH, x % NCH
                    b, w = x % 4, (t + 1) * P
                    if x < 2:
                        pe.wait_ge(*ve.at(f"v {x}", i))
                    elif x >= NCH:
                        pe.wait_ge(*ae.at(f"exp {x - NCH}", i))
                    q = slice(t * P, (t + 1) * P)
                    pe.matmul(wbank(b)[:, 0:w], qn[:, hd, q], kn[:, hd, 0:w], start=True, stop=False)
                    pe.matmul(wbank(b)[:, 0:w], qrz[:, hd, q], kr[:, 0:w], start=False, stop=False)
                    pe.matmul(wbank(b)[:, t * P:w], identb, causal, start=False, stop=True)\
                      .then_inc(*te.done(f"scores {x}"))
                    more()
                for hd in range(2):
                    for t in range(NCH):
                        b = t % 3
                        if t == 3:
                            more()
                            pe.wait_ge(*ve.at(f"p transposed {hd} 0", i))
                        elif hd:
                            pe.wait_ge(*ve.at("p transposed 0 3", i))
                        elif t == 0:
                            pe.wait_ge(*ae.at("exp 7", i))
                        for u in range(t, NCH):
                            if t == 0 and hd == 0:
                                pe.wait_ge(*ve.at(f"p {hd * NCH + u}", i))
                            a = off_q[u] + t * P
                            last = pe.transpose(wbank(b)[:, (u - t) * P:(u - t + 1) * P],
                                                prob[:, hd, a:a + P], ident)
                        last.then_inc(*te.done(f"p transposed {hd} {t}"))
                    more()
                    for t in range(NCH):
                        pe.wait_ge(*ve.at(f"p transposed {hd} {t}", i))
                        last = pe.matmul(wbank(3)[:, t * P:], vt[:, t, hd * P:(hd + 1) * P],
                                         pT[:, off_k[t]:off_k[t] + (NCH - t) * P], start=t == 0, stop=t == NCH - 1)
                    last.then_inc(*te.done(f"o {hd}"))
                    more()

            def work_scalar(act, i, evac, after):
                ae.turn()
                for x in range(2 * NCH):
                    hd, t = x // NCH, x % NCH
                    w = (t + 1) * P
                    act.wait_ge(*ve.at(f"max {x}", i))
                    act.activation(prob[:, hd, off_q[t]:off_q[t] + w], wbank(x % 4)[:, 0:w], ACT.Exp, scale=SCALE,
                                   bias=nmx[:, x:x + 1], accum_out=rs[:, x:x + 1]).then_inc(*ae.done(f"exp {x}"))
                    if x == NCH - 1:
                        evac(0)
                        evac(1)
                        after(0)
                for t in range(2, 4):
                    evac(t)
                after(1)
                for t in (4, 5, 6):
                    evac(t)
                    after(t - 2)

            def work_vector(dve, i, evac):
                ve.turn()
                dve.wait_ge(*te.at("v tokens", i))
                for x in range(2):
                    dve.tensor_copy(vt[:, 2 * x:2 * x + 2, :], wbank(x).rearrange("p (c v) -> p c v", c=2))\
                       .then_inc(*ve.done(f"v {x}"))

                def normalize(x):
                    hd, t = x // NCH, x % NCH
                    s = slice(off_q[t], off_q[t] + (t + 1) * P)
                    dve.wait_ge(*ae.at(f"exp {x}", i))
                    dve.reciprocal(ri[:, x:x + 1], rs[:, x:x + 1]).then_inc(*ve.done(f"1/sum {x}"))
                    dve.wait_ge(*ve.at(f"1/sum {x}", i))
                    dve.tensor_scalar(prob[:, hd, s], prob[:, hd, s], ri[:, x:x + 1], None, ALU.mult)\
                       .then_inc(*ve.done(f"p {x}"))
                for x in range(2 * NCH):
                    w = (x % NCH + 1) * P
                    dve.wait_ge(*te.at(f"scores {x}", i))
                    dve.reduce_max(mxs[:, x:x + 1], wbank(x % 4)[:, 0:w], AX.X).then_inc(*ve.done(f"max raw {x}"))
                    dve.wait_ge(*ve.at(f"max raw {x}", i))
                    dve.tensor_scalar(nmx[:, x:x + 1], mxs[:, x:x + 1], -SCALE, None, ALU.mult)\
                       .then_inc(*ve.done(f"max {x}"))
                    if x:
                        normalize(x - 1)
                normalize(2 * NCH - 1)
                for hd in range(2):
                    for t in range(NCH):
                        w = (NCH - t) * P
                        dve.wait_ge(*te.at(f"p transposed {hd} {t}", i))
                        dve.tensor_copy(pT[:, off_k[t]:off_k[t] + w], wbank(t % 3)[:, 0:w])\
                           .then_inc(*ve.done(f"p transposed {hd} {t}"))
                    dve.wait_ge(*te.at(f"o {hd}", i))
                    if hd == 0:
                        dve.wait_ge(*ap_.at("silu", i))
                    dve.tensor_tensor(prob[:, hd, 0:SEQ], wbank(3), gs[:, hd, :], ALU.mult)\
                       .then_inc(*ve.done(f"y {hd}"))
                    dve.wait_ge(*ve.at(f"y {hd}", i))
                    dve.tensor_copy(yh[:, hd, :], prob[:, hd, 0:SEQ]).then_inc(*ve.done(f"y hi {hd}"))
                    dve.wait_ge(*ve.at(f"y hi {hd}", i))
                    dve.tensor_tensor(yl[:, hd, :], prob[:, hd, 0:SEQ], yh[:, hd, :].bitcast(F32), ALU.subtract)\
                       .then_inc(*ve.done(f"y lo {hd}"))
                evac(0)
                evac(1)

            def out_tensor(pe, s, i, h, j):
                for m in range(KD):
                    product(pe, s, i, j + m // 4, m % 4, yh, yl, [ve.at(f"y lo {k}", h) for k in range(2)])

            def tensor(pe):
                c_tensor(pe)
                for _ in in_pieces(pe, first_sec, 0, True):
                    pass
                prep_tensor(pe, first_sec, 0, 0)

                def turn(i, last):
                    rest = in_pieces(pe, sec, i)
                    work_tensor(pe, sec, i, i, lambda: next(rest, None))
                    for _ in rest:
                        pass
                    prep_tensor(pe, sec, i, i + 1)
                    out_tensor(pe, sec, i, i, 7)
                loop(pe, PAIRS - 1, turn)
                work_tensor(pe, None, PAIRS - 1, PAIRS - 1, lambda: None)
                out_tensor(pe, last_sec, 0, PAIRS - 1, 0)

            def scalar(act):
                c_scalar(act)
                act.wait_ge(*vbs.at("q rope 0"))
                for t in range(7):
                    evac_scalar(act, first_sec, 0, t)
                    if TILES[t][1] == W.sec[first_sec]["items"][TILES[t][0]][1] - 1:
                        hi_after(act, first_sec, 0, TILES[t][0], True)
                for j in (5, 6):
                    hi_after(act, first_sec, 0, j, True)
                prep_scalar(act, first_sec, 0, 0)

                def turn(i, last):
                    work_scalar(act, i, lambda t: evac_scalar(act, sec, i, t),
                                lambda j: hi_after(act, sec, i, j, last))
                    for j in (5, 6):
                        hi_after(act, sec, i, j, last)
                    prep_scalar(act, sec, i, i + 1)
                    for j in (7, 8):
                        hi_after(act, sec, i, j, last)
                loop(act, PAIRS - 1, turn)
                work_scalar(act, PAIRS - 1, lambda t: None, lambda j: None)
                for j in (0, 1):
                    hi_after(act, last_sec, 0, j, True)

            def vector(dve):
                c_vector(dve)
                for x in range(2):
                    evac_gate(dve, first_sec, 0, x)
                prep_vector(dve, first_sec, 0, 0)

                def turn(i, last):
                    work_vector(dve, i, lambda x: evac_gate(dve, sec, i, x))
                    prep_vector(dve, sec, i, i + 1)
                    for j in (7, 8):
                        add_to_x(dve, sec, i, j, range(4 * (j - 7), 4 * (j - 7) + 4))
                loop(dve, PAIRS - 1, turn)
                work_vector(dve, PAIRS - 1, lambda x: None)
                for j in (0, 1):
                    add_to_x(dve, last_sec, 0, j, range(4 * j, 4 * j + 4))

            def tables(act):
                act.wait_ge(*x_ready_before)
                act.dma_start(pos_i, T["positions"].to_broadcast([P, SEQ])).then_inc(pos_in, 16)
                act.dma_start(mk[:, :, :], T["mla_masks"].rearrange("p (k n) -> p k n", k=2)).then_inc(pos_in, 16)

            def sync(sp):
                for s in (c_sec, first_sec, sec, last_sec):
                    load_slots(s)(sp)

            def gpsimd(pool):
                for s in (c_sec, first_sec, sec, last_sec):
                    split_slots(s)(pool)

            x_ready.append(tile_taken(last_sec, 0, 1, 3))
            me = {"sync": sync, "gpsimd": gpsimd, "scalar": scalar, "tensor": tensor, "vector": vector,
                  "steps": {"scalar": [ab, ap_, ae], "tensor": [tb, tp, te], "vector": [vbs, vp, ve]}}
            return merge({"scalar": tables}, nv, me)

        def odd_layer(n, l):
            nv = norm(n, param("c_norm_w"))
            first_sec, sec, last_sec = f"odd_first{n}", f"odd{n}", f"odd_last{n}"
            PAIRS = 4
            SCALE = 64 ** -0.5
            LAM0 = 0.8 - 0.6 * math.exp(-0.3 * 1)
            cosT = sb("o_cosT", [P, SEQ])
            sinT = sb("o_sinT", [P, SEQ])
            mk = sb("o_mk", [P, 3, P])
            rot, halves = mk[:, 0, :], mk[:, 2, :]
            maskb = sb("o_maskb", [P, 2, P], BF16)
            identb, allowed = maskb[:, 0, :], maskb[:, 1, :]
            mxs, nmx, rs, ri = (sb(f"o_{name}", [P, 16]) for name in ("mxs", "nmx", "rs", "ri"))
            lam = sb("o_lam", [P, 8])
            xq = sb("o_xq", [P, 4, SEQ])
            rr = sb("o_rr", [P, 4, SEQ])
            qz = sb("o_qz", [P, 2, 2, SEQ])
            kn = sb("o_kn", [P, 2, SEQ])
            vT = sb("o_vT", [P, 2, SEQ])
            vt = sb("o_vt", [P, NCH, 2 * P])
            gs = sb("o_gs", [P, 2, SEQ])
            prob = sb("o_prob", [P, 2, 1280])
            p1 = sb("o_p1", [P, 2, SEQ])
            pT = sb("o_pT", [P, 1280])
            yf = sb("o_yf", [P, 2, SEQ])
            yh = sb("o_yh", [P, 2, SEQ], F32R)
            yl = sb("o_yl", [P, 2, SEQ], F32R)
            pos_i = pT[:, 0:SEQ].bitcast(I32)
            tmp = [rr[:, 0, :], rr[:, 1, :], rr[:, 2, :]]
            pos_in = sem("odd_pos_in")
            wq, wk, subln = param("c_q_norm_w"), param("c_k_norm_w"), param("c_subln_w")
            lams = param("c_lams")
            ab, tb, vbs = steps(f"odd_tables{n}", "scalar", "tensor", "vector")
            ap_, tp, vp = steps(f"odd_prep{n}", "scalar", "tensor", "vector")
            ae, te, ve = steps(sec, "scalar", "tensor", "vector")
            x_ready_before = x_ready[-1]
            off_q = [sum(range(t + 1)) * P for t in range(NCH)]
            off_k = [sum(NCH - u for u in range(t)) * P for t in range(NCH)]
            X = [(hd, t, m) for hd in range(2) for t in range(NCH) for m in range(2)]

            def tables_vector(dve):
                dve.memset(qz[:, :, :, :], 0.0).then_inc(*vbs.done("q 0"))
                dve.wait_ge(pos_in, 32)
                dve.tensor_copy(identb, ident).then_inc(*vbs.done("identity"))
                dve.tensor_copy(allowed, mk[:, 1, :]).then_inc(*vbs.done("mask"))
                rotary_tables(dve, None, vbs, ab, "vector", pos_i, cosT[:, :], sinT[:, :], tmp, param("odd_inv"),
                              "vector")
                dve.tensor_tensor(lam[0:64, 0:2], lams[0:64, 0:2], lams[0:64, 2:4], ALU.mult)\
                   .then_inc(*vbs.done("lq lk"))
                dve.tensor_scalar(lam[:, 4:5], subln, 1.0 - LAM0, None, ALU.mult).then_inc(*vbs.done("subln"))
                dve.wait_ge(*ab.at("exp"))
                dve.tensor_tensor(lam[:, 5:6], lam[:, 3:4], lam[:, 2:3], ALU.subtract).then_inc(*vbs.done("diff"))
                dve.wait_ge(*vbs.at("diff"))
                dve.tensor_scalar(lam[:, 6:7], lam[:, 5:6], -LAM0, None, ALU.add).then_inc(*vbs.done("-lam"))
                dve.wait_ge(*vbs.at("-lam"))
                dve.wait_ge(*ab.at("cos"))

            def tables_scalar(act):
                rotary_tables(None, act, vbs, ab, "scalar", pos_i, cosT[:, :], sinT[:, :], tmp, None, "scalar")
                act.wait_ge(*tb.at("lam"))
                act.activation(lam[:, 2:4], wbank(1)[:, 0:2], ACT.Exp).then_inc(*ab.done("exp"))

            def tables_tensor(pe):
                pe.wait_ge(*vbs.at("lq lk"))
                pe.matmul(wbank(1)[:, 0:2], ones[0:64, :], lam[0:64, 0:2], start=True, stop=True)\
                  .then_inc(*tb.done("lam"))

            def in_pieces(pe, s, i, first, end):
                for t in range(first, end):
                    for k in range(0, KD, 2):
                        product(pe, s, i, t, 0, xh, xl, None, k, k + 2)
                        yield

            def slot_of(s, t):
                return 9 if s == sec and t == 7 else t

            def evac(dve, s, i, t):
                j = slot_of(s, t)
                dve.wait_ge(*tile_done(s, i, j, 0))
                dst = [vT[:, 0, :], vT[:, 1, :]] + [xq[:, x, :] for x in range(4)] + [gs[:, 0, :], gs[:, 1, :]]
                dve.tensor_tensor(dst[t], tile(s, j, 0), R[:, :], ALU.mult).then_inc(*taken(s, j, 0))

            def prep_tensor_a(pe, h):
                tp.turn()
                pe.wait_ge(*ve.at("y gated 1", h, 1))
                for x in range(4):
                    pe.wait_ge(*ap_.at(f"square {x}", h))
                    pe.matmul(wbank(x), halves, rr[:, x, :], start=True, stop=True).then_inc(*tp.done(f"sum {x}"))

            def prep_tensor_b(pe, h):
                for x in range(4):
                    pe.wait_ge(*vp.at(f"normed {x}", h))
                    pe.matmul(wbank(x), rot, xq[:, x, :], start=True, stop=True).then_inc(*tp.done(f"rotated {x}"))

            def prep_scalar(act, s, i, h):
                ap_.turn()
                for x in range(4):
                    act.wait_ge(*tile_taken(s, i, 2 + x, 0))
                    if x == 0:
                        act.wait_ge(*vp.at("rope 3", h, 1))
                    act.activation(rr[:, x, :], xq[:, x, :], ACT.Square).then_inc(*ap_.done(f"square {x}"))
                for x in range(4):
                    act.wait_ge(*tp.at(f"sum {x}", h))
                    act.activation(rr[:, x, :], wbank(x), ACT.Ln, scale=1.0 / 64, bias=bias[:, 0:1])\
                       .then_inc(*ap_.done(f"ln {x}"))
                for x in range(4):
                    act.wait_ge(*ap_.at(f"ln {x}", h))
                    act.activation(rr[:, x, :], rr[:, x, :], ACT.Exp, scale=-0.5).then_inc(*ap_.done(f"1/rms {x}"))

            def silu_scalar(act, s, i, h):
                for x in range(2):
                    act.wait_ge(*tile_taken(s, i, slot_of(s, 6 + x), 0))
                act.activation(gs[:, :, :], gs[:, :, :], ACT.Silu).then_inc(*ap_.done("silu"))

            def prep_vector_a(dve, h):
                vp.turn()
                for x in range(4):
                    dve.wait_ge(*ap_.at(f"1/rms {x}", h))
                    dve.scalar_tensor_tensor(out=xq[:, x, :], in0=xq[:, x, :], scalar=(wk, wq)[x // 2],
                                             in1=rr[:, x, :], op0=ALU.mult, op1=ALU.mult)\
                       .then_inc(*vp.done(f"normed {x}"))

            def prep_vector_b(dve, h, between=None):
                for x in range(4):
                    if x == 0:
                        dve.wait_ge(*vp.at("normed 3", h))
                    dve.tensor_tensor(rr[:, x, :], xq[:, x, :], cosT[:, :], ALU.mult).then_inc(*vp.done(f"cos {x}"))
                    dve.wait_ge(*tp.at(f"rotated {x}", h))
                    dve.wait_ge(*vp.at(f"cos {x}", h))
                    dve.tensor_tensor(xq[:, x, :], wbank(x), sinT[:, :], ALU.mult).then_inc(*vp.done(f"sin {x}"))
                    dve.wait_ge(*vp.at(f"sin {x}", h))
                    if x < 2:
                        last = dve.tensor_tensor(kn[:, x, :], rr[:, x, :], xq[:, x, :], ALU.add)
                    else:
                        for m in range(2):
                            r = slice(64 * m, 64 * m + 64)
                            last = dve.tensor_tensor(qz[r, x - 2, m, :], rr[r, x, :], xq[r, x, :], ALU.add)
                            if m == 0:
                                last.then_inc(*vp.done(f"rope a {x}"))
                    last.then_inc(*vp.done(f"rope {x}"))
                    if between:
                        between(x)

            def work_tensor(pe, i, more):
                te.turn()
                pe.wait_ge(*vp.at("rope 3", i))
                for cc in range(NCH):
                    for d in range(2):
                        at = (cc % 2) * 2 * P + d * P
                        last = pe.transpose(wbank(cc // 2)[:, at:at + P], vT[:, d, cc * P:(cc + 1) * P], ident)
                last.then_inc(*te.done("v tokens"))
                for x, (hd, t, m) in enumerate(X):
                    b, w = x % 4, (t + 1) * P
                    if x < 2:
                        pe.wait_ge(*ve.at(f"v {x}", i))
                    elif x >= 4:
                        pe.wait_ge(*ae.at(f"exp {x - 4}", i))
                    pe.matmul(wbank(b)[:, 0:w], qz[:, hd, m, t * P:w], kn[:, hd, 0:w], start=True, stop=False)
                    pe.matmul(wbank(b)[:, t * P:w], identb, allowed, start=False, stop=True)\
                      .then_inc(*te.done(f"scores {x}"))
                    more()
                for hd in range(2):
                    for t in range(NCH):
                        b = t % 3
                        if t == 3:
                            more()
                            pe.wait_ge(*ve.at(f"p transposed {hd} 0", i))
                        elif hd:
                            pe.wait_ge(*ve.at("p transposed 0 3", i))
                            if t == 2:
                                pe.wait_ge(*ae.at("o ln 0", i))
                        elif t == 0:
                            pe.wait_ge(*ae.at("exp 15", i))
                        for u in range(t, NCH):
                            if t == 0 and hd == 0:
                                pe.wait_ge(*ve.at(f"p {2 * u + 1}", i))
                            a = off_q[u] + t * P
                            last = pe.transpose(wbank(b)[:, (u - t) * P:(u - t + 1) * P],
                                                prob[:, hd, a:a + P], ident)
                        last.then_inc(*te.done(f"p transposed {hd} {t}"))
                    more()
                    for t in range(NCH):
                        pe.wait_ge(*ve.at(f"p transposed {hd} {t}", i))
                        last = pe.matmul(wbank(3)[:, t * P:], vt[:, t, hd * P:(hd + 1) * P],
                                         pT[:, off_k[t]:off_k[t] + (NCH - t) * P], start=t == 0, stop=t == NCH - 1)
                    last.then_inc(*te.done(f"o {hd}"))
                    more()
                    pe.wait_ge(*ae.at(f"o square {hd}", i))
                    pe.matmul(wbank(2), ones, yf[:, hd, :], start=True, stop=True).then_inc(*te.done(f"o sum {hd}"))
                    more()

            def work_scalar(act, i, after):
                ae.turn()
                for x, (hd, t, m) in enumerate(X):
                    w = (t + 1) * P
                    dst = p1[:, t % 2, 0:w] if m else prob[:, hd, off_q[t]:off_q[t] + w]
                    act.wait_ge(*ve.at(f"max {x}", i))
                    act.activation(dst, wbank(x % 4)[:, 0:w], ACT.Exp, scale=SCALE,
                                   bias=nmx[:, x:x + 1], accum_out=rs[:, x:x + 1]).then_inc(*ae.done(f"exp {x}"))
                    if x in (5, 9, 13):
                        after((x - 5) // 4)
                after(3)
                for hd in range(2):
                    act.wait_ge(*te.at(f"o {hd}", i))
                    act.activation(yf[:, hd, :], wbank(3), ACT.Square).then_inc(*ae.done(f"o square {hd}"))
                    act.wait_ge(*te.at(f"o sum {hd}", i))
                    if hd:
                        act.wait_ge(*ve.at("y 0", i))
                    act.activation(ro, wbank(2), ACT.Ln, scale=1.0 / P, bias=bias[:, 0:1])\
                       .then_inc(*ae.done(f"o ln {hd}"))
                    act.wait_ge(*ae.at(f"o ln {hd}", i))
                    act.activation(ro, ro, ACT.Exp, scale=-0.5).then_inc(*ae.done(f"1/rms o {hd}"))
                for j in range(4, 7):
                    after(j)

            ro = sq[:, 0, :]

            def work_vector(dve, i, evac):
                ve.turn()
                dve.wait_ge(*te.at("v tokens", i))
                for x in range(2):
                    dve.tensor_copy(vt[:, 2 * x:2 * x + 2, :], wbank(x).rearrange("p (c v) -> p c v", c=2))\
                       .then_inc(*ve.done(f"v {x}"))

                def normalize(x):
                    hd, t, m = X[x]
                    w = (t + 1) * P
                    s = slice(off_q[t], off_q[t] + w)
                    dve.wait_ge(*ae.at(f"exp {x}", i))
                    dve.reciprocal(ri[:, x:x + 1], rs[:, x:x + 1]).then_inc(*ve.done(f"1/sum {x}"))
                    dve.wait_ge(*ve.at(f"1/sum {x}", i))
                    if m == 0:
                        dve.tensor_scalar(prob[:, hd, s], prob[:, hd, s], ri[:, x:x + 1], None, ALU.mult)\
                           .then_inc(*ve.done(f"p {x}"))
                    else:
                        dve.tensor_scalar(ri[:, x:x + 1], ri[:, x:x + 1], lam[:, 6:7], None, ALU.mult)\
                           .then_inc(*ve.done(f"lam/sum {x}"))
                        dve.wait_ge(*ve.at(f"lam/sum {x}", i))
                        dve.scalar_tensor_tensor(out=prob[:, hd, s], in0=p1[:, t % 2, 0:w], scalar=ri[:, x:x + 1],
                                                 in1=prob[:, hd, s], op0=ALU.mult, op1=ALU.add)\
                           .then_inc(*ve.done(f"p {x}"))
                for x, (hd, t, m) in enumerate(X):
                    w = (t + 1) * P
                    dve.wait_ge(*te.at(f"scores {x}", i))
                    dve.reduce_max(mxs[:, x:x + 1], wbank(x % 4)[:, 0:w], AX.X).then_inc(*ve.done(f"max raw {x}"))
                    dve.wait_ge(*ve.at(f"max raw {x}", i))
                    dve.tensor_scalar(nmx[:, x:x + 1], mxs[:, x:x + 1], -SCALE, None, ALU.mult)\
                       .then_inc(*ve.done(f"max {x}"))
                    if x:
                        normalize(x - 1)
                    if x % 4 == 3:
                        evac(x // 4)
                normalize(15)
                def finish(hd):
                    dve.wait_ge(*ve.at(f"y gated {hd}", i))
                    dve.wait_ge(*ae.at(f"1/rms o {hd}", i))
                    dve.tensor_tensor(yf[:, hd, :], yf[:, hd, :], ro, ALU.mult).then_inc(*ve.done(f"y {hd}"))
                    dve.wait_ge(*ve.at(f"y {hd}", i))
                    dve.tensor_copy(yh[:, hd, :], yf[:, hd, :]).then_inc(*ve.done(f"y hi {hd}"))
                    dve.wait_ge(*ve.at(f"y hi {hd}", i))
                    dve.tensor_tensor(yl[:, hd, :], yf[:, hd, :], yh[:, hd, :].bitcast(F32), ALU.subtract)\
                       .then_inc(*ve.done(f"y lo {hd}"))

                for hd in range(2):
                    for t in range(NCH):
                        w = (NCH - t) * P
                        dve.wait_ge(*te.at(f"p transposed {hd} {t}", i))
                        dve.tensor_copy(pT[:, off_k[t]:off_k[t] + w], wbank(t % 3)[:, 0:w])\
                           .then_inc(*ve.done(f"p transposed {hd} {t}"))
                    if hd == 0:
                        dve.wait_ge(*ap_.at("silu", i))
                    else:
                        finish(0)
                    dve.wait_ge(*te.at(f"o sum {hd}", i))
                    dve.scalar_tensor_tensor(out=yf[:, hd, :], in0=wbank(3), scalar=lam[:, 4:5], in1=gs[:, hd, :],
                                             op0=ALU.mult, op1=ALU.mult).then_inc(*ve.done(f"y gated {hd}"))
                finish(1)
                for t in range(4, 7):
                    evac(t)

            def out_half(pe, s, i, h, j):
                for m in range(4):
                    product(pe, s, i, j, m, yh, yl, [ve.at(f"y lo {k}", h) for k in range(2)])

            def tensor(pe):
                nv["first product"](pe, first_sec, 0, 0)
                product(pe, first_sec, 0, 1, 0, xh, xl)
                tables_tensor(pe)
                for _ in in_pieces(pe, first_sec, 0, 2, 8):
                    pass
                prep_tensor_a(pe, 0)
                prep_tensor_b(pe, 0)

                def turn(i, last):
                    rest = in_pieces(pe, sec, i, 0, 7)
                    work_tensor(pe, i, lambda: next(rest, None))
                    for _ in rest:
                        pass
                    prep_tensor_a(pe, i + 1)
                    out_half(pe, sec, i, i, 7)
                    prep_tensor_b(pe, i + 1)
                    out_half(pe, sec, i, i, 8)
                    product(pe, sec, i, 9, 0, xh, xl)
                loop(pe, PAIRS - 1, turn)
                work_tensor(pe, PAIRS - 1, lambda: None)
                for j in range(2):
                    out_half(pe, last_sec, 0, PAIRS - 1, j)

            def scalar(act):
                tables_scalar(act)
                for j in range(8):
                    hi_after(act, first_sec, 0, j, True)
                prep_scalar(act, first_sec, 0, 0)
                silu_scalar(act, first_sec, 0, 0)

                def turn(i, last):
                    work_scalar(act, i, lambda j: hi_after(act, sec, i, j, last))
                    prep_scalar(act, sec, i, i + 1)
                    for j in (7, 8):
                        hi_after(act, sec, i, j, last)
                    silu_scalar(act, sec, i, i + 1)
                    hi_after(act, sec, i, 9, last)
                loop(act, PAIRS - 1, turn)
                work_scalar(act, PAIRS - 1, lambda j: None)
                for j in (0, 1):
                    hi_after(act, last_sec, 0, j, True)

            def vector(dve):
                tables_vector(dve)
                for t in range(8):
                    evac(dve, first_sec, 0, t)
                prep_vector_a(dve, 0)
                prep_vector_b(dve, 0)

                def turn(i, last):
                    work_vector(dve, i, lambda t: evac(dve, sec, i, t))
                    prep_vector_a(dve, i + 1)
                    add_to_x(dve, sec, i, 7, range(0, 4))
                    prep_vector_b(dve, i + 1, lambda x: add_tile(dve, sec, i, 8, x, 4 + x))
                    evac(dve, sec, i, 7)
                loop(dve, PAIRS - 1, turn)
                work_vector(dve, PAIRS - 1, lambda t: None)
                for j in (0, 1):
                    add_to_x(dve, last_sec, 0, j, range(4 * j, 4 * j + 4))

            def tables(act):
                act.wait_ge(*x_ready_before)
                act.dma_start(pos_i, T["positions_2"].to_broadcast([P, SEQ])).then_inc(pos_in, 16)
                act.dma_start(mk[:, :, :], T["odd_masks"].rearrange("p (k n) -> p k n", k=3)).then_inc(pos_in, 16)

            def sync(sp):
                for s in (first_sec, sec, last_sec):
                    load_slots(s)(sp)

            def gpsimd(pool):
                for s in (first_sec, sec, last_sec):
                    split_slots(s)(pool)

            x_ready.append(tile_taken(last_sec, 0, 1, 3))
            me = {"sync": sync, "gpsimd": gpsimd, "scalar": scalar, "tensor": tensor, "vector": vector,
                  "steps": {"scalar": [ab, ap_, ae], "tensor": [tb, tp, te], "vector": [vbs, vp, ve]}}
            return merge({"scalar": tables}, nv, me)

        STAGE = {"load": load_x, "pool": pool_layer, "gdn": gdn_layer, "mla": mla_layer, "even": even_layer,
                 "odd": odd_layer, "store": store_x}
        stages = []
        small = []

        small.append((cst[:, :], T["consts"]))
        small.append((par[:, :], T["params"]))

        for n, (kind, j) in enumerate(plan):
            with ExitStack() as mine:
                area[0] = mine
                stages.append(STAGE[kind](n, j))
            area[0] = top

        def credit(eng, engine):
            for st in stages:
                for s in st.get("steps", {}).get(engine, []):
                    eng.sem_inc(s.sem, s.counts.get("per turn", 1))

        block = top.enter_context(nc.Block())

        @block.sync
        def _(sp):
            for dst, src in small:
                sp.dma_start(dst, src).then_inc(consts_in, 16)
            for st in stages:
                if "sync" in st:
                    st["sync"](sp)

        @block.gpsimd
        def _(pool):
            for q in range(RING):
                pool.sem_inc(lo_ready[q], 1)
            for k, value in enumerate(BIASES):
                pool.memset(bias[:, k:k + 1], value).then_inc(consts_in, 1)
            credit(pool, "gpsimd")
            for st in stages:
                if "gpsimd" in st:
                    st["gpsimd"](pool)

        @block.scalar
        def _(act):
            credit(act, "scalar")
            act.wait_ge(consts_in, 16 * len(small) + len(BIASES))
            for first in W.at_start:
                slot_hi(act, *first)
            for st in stages:
                if "scalar" in st:
                    st["scalar"](act)

        @block.vector
        def _(dve):
            for b in range(BANKS):
                dve.sem_inc(bank_taken[b], 1)
            credit(dve, "vector")
            dve.wait_ge(consts_in, 16 * len(small) + len(BIASES))
            for st in stages:
                if "vector" in st:
                    st["vector"](dve)

        @block.tensor
        def _(pe):
            for q in range(RING):
                pe.sem_inc(slot_used[q], 1)
            credit(pe, "tensor")
            pe.wait_ge(consts_in, 16 * len(small) + len(BIASES))
            for st in stages:
                if "tensor" in st:
                    st["tensor"](pe)


MLA_IN = [(4, 2)] * 2 + [(6, 1)] * 3 + [(8, 1)] * 2
SLOTS = {
    "pool": [("pool", 4, [(8, 1)] * 8 + [(4, 2)] * 6)],
    "gdn": [("gdn_ba", 1, [(8, 1)]), ("gdn_first", 1, [(8, 1)] * 6), ("gdn", 7, [(8, 1)] * 6 + [(2, 4)] * 2),
            ("gdn_last", 1, [(2, 4)] * 2)],
    "mla": [("mla_c", 1, [(8, 1)] * 11), ("mla_first", 1, MLA_IN), ("mla", 7, MLA_IN + [(2, 4)] * 2),
            ("mla_last", 1, [(2, 4)] * 2)],
    "even": [("ev_dt", 1, [(8, 1)]), ("ev_first", 1, [(8, 1)] * 6), ("ev_glu", 4, [(8, 1)] * 6),
             ("ev_ssd", 3, [(8, 1)] * 6 + [(2, 4)] * 2), ("ev_last", 1, [(2, 4)] * 2),
             ("ev_out", 2, [(2, 4)] * 4)],
    "odd": [("odd_first", 1, [(8, 1)] * 8), ("odd", 3, [(8, 1)] * 7 + [(2, 4)] * 2 + [(8, 1)]),
            ("odd_last", 1, [(2, 4)] * 2)],
}


def tiles(w, n=P):
    for c in range(0, w.shape[1], n):
        yield w[:, c:c + n]


def slot_sources(kind, l, A):
    if kind == "pool":
        w_in, w_grp, w_out = A["pool_w_in"][l], A["pool_w_grp"][l], A["pool_w_out"][l]
        for g in range(4):
            yield from tiles(w_in[:, g * 512:(g + 1) * 512])
            yield from tiles(w_in[:, 2048 + g * 512:2048 + (g + 1) * 512])
            yield from tiles(w_grp[g], 256)
            yield from tiles(w_out[g * 512:(g + 1) * 512], 256)
    if kind == "gdn":
        w, out = A["gdn_w_in"][l], A["gdn_w_out"][l]

        def head(h):
            yield w[:, h * 128:h * 128 + 128]
            yield w[:, 1024 + h * 128:1152 + h * 128]
            yield from tiles(w[:, 2048 + h * 256:2304 + h * 256])
            yield from tiles(w[:, 4096 + h * 256:4352 + h * 256])

        ba = np.zeros((D, P), np.float32)
        ba[:, 0:8], ba[:, 32:40] = w[:, 6144:6152], w[:, 6152:6160]
        yield ba
        yield from head(0)
        for h in range(7):
            yield from head(h + 1)
            yield from tiles(out[h * 256:(h + 1) * 256], 512)
        yield from tiles(out[7 * 256:], 512)
    if kind == "mla":
        w, uq, ukv, out = A["mla_w_in"][l], A["mla_w_uq"][l], A["mla_w_ukv"][l], A["mla_w_out"][l]

        def pair(t):
            a, b = 2 * t, 2 * t + 1
            for c in (128, 0):
                yield np.concatenate([ukv[:, h * 256 + c:h * 256 + c + 128] for h in (a, b)], axis=1)
            for h in (a, b):
                yield uq[:, h * 192:h * 192 + 128]
            yield np.concatenate([uq[:, h * 192 + 128:h * 192 + 192] for h in (a, b)], axis=1)
            yield from tiles(w[:, 1344 + t * 256:1344 + (t + 1) * 256])

        yield from tiles(w[:, 768:1280])
        yield np.concatenate([w[:, 1280:1344]] * 2, axis=1)
        yield from tiles(w[:, 0:768])
        yield from pair(0)
        for t in range(7):
            yield from pair(t + 1)
            yield from tiles(out[t * 256:(t + 1) * 256], 512)
        yield from tiles(out[7 * 256:], 512)
    if kind == "even":
        w, out = A["a_w_in_2"][l], A["a_w_out_2"][l]

        def group(g):
            yield from tiles(w[:, 1024 + g * 256:1024 + (g + 1) * 256])
            yield w[:, 2048 + g * 128:2048 + (g + 1) * 128]
            yield w[:, 2560 + g * 128:2560 + (g + 1) * 128]
            yield from tiles(w[:, g * 256:(g + 1) * 256])

        yield w[:, 3072:3200]
        yield from group(0)
        for t in range(4):
            for u in (2 * t, 2 * t + 1):
                yield w[:, 3088 + u * 128:3088 + (u + 1) * 128]
                yield w[:, 4112 + u * 128:4112 + (u + 1) * 128]
            yield from tiles(w[:, 5136 + t * 256:5136 + (t + 1) * 256])
        for g in range(4):
            if g < 3:
                yield from group(g + 1)
            yield from tiles(out[g * 256:(g + 1) * 256], 512)
        for g in range(4):
            yield from tiles(out[1024 + g * 256:1024 + (g + 1) * 256], 512)
    if kind == "odd":
        w, out = A["c_w_in_2"][l], A["c_w_out_2"][l]

        def heads(t):
            for c in (2048, 1024, 0, 3072):
                yield from tiles(w[:, c + t * 256:c + (t + 1) * 256])

        yield from heads(0)
        for t in range(3):
            *first, gate = heads(t + 1)
            yield from first
            yield from tiles(out[t * 256:(t + 1) * 256], 512)
            yield gate
        yield from tiles(out[3 * 256:], 512)


def lay_out_weights(layers, A):
    seen, slots = {}, []
    for kind in layers:
        l = seen[kind] = seen.get(kind, -1) + 1
        shapes = [s for _, iters, items in SLOTS.get(kind, []) for _ in range(iters) for s in items]
        parts = list(slot_sources(kind, l, A)) if shapes else []
        assert len(parts) == len(shapes)
        for (nk, nm), w in zip(shapes, parts):
            assert w.shape == (nk * P, nm * P), (kind, w.shape, nk, nm)
            slot = np.zeros((P, SLOT), np.float32)
            slot[:, :nk * nm * P] = w.reshape(nk, P, nm * P).transpose(1, 0, 2).reshape(P, -1)
            slots.append(slot)
    return np.stack(slots) if slots else np.zeros((1, P, SLOT), np.float32)


def columns(v):
    v = np.asarray(v, np.float32)
    lead = int(np.prod(v.shape[:-1]))
    return v.reshape(lead, -1, P).transpose(2, 0, 1).reshape(P, -1)


def small_parameters(A):
    out = {}
    for k in range(4):
        out[f"norm_g{k}"] = columns(A["norm_g"][k])
    for l in range(2):
        out[f"pool_scale{l}"] = columns(A["pool_scale"][l])
    out["final_g"] = columns(A["final_g"])
    taps = A["gdn_conv"][0].reshape(4, 32, P)
    out["gdn_conv"] = np.concatenate(
        [taps[:, t].T for h in range(8) for t in (h, 8 + h, 16 + 2 * h, 17 + 2 * h)], axis=1)
    out["gdn_norm_g"] = columns(A["gdn_norm_g"][0])
    out["mla_q_norm_g"] = columns(A["mla_q_norm_g"][0])
    out["mla_kv_norm_g"] = columns(A["mla_kv_norm_g"][0])
    r = np.arange(P)
    out["mla_inv"] = (10000.0 ** (-(r % 32) / 32.0)).astype(np.float32).reshape(P, 1)
    out["c_norm_w"] = columns(A["c_norm_w_2"][0])
    out["odd_inv"] = np.where(r % 64 < 16, 500000.0 ** (-2.0 * (r % 8) / 16.0), 0.0).astype(np.float32).reshape(P, 1)
    for name in ("c_q_norm_w", "c_k_norm_w"):
        out[name] = np.concatenate([A[name + "_2"][0]] * 2).reshape(P, 1)
    out["c_subln_w"] = columns(A["c_subln_w_2"][0])
    out["c_lams"] = np.zeros((P, 4), np.float32)
    for k, name in enumerate(("c_lq1_2", "c_lq2_2", "c_lk1_2", "c_lk2_2")):
        out["c_lams"][0:64, k] = A[name][0]
    out["a_norm_w"] = columns(A["a_norm_w_2"][0])
    for name in ("a_dt_bias", "a_a_log"):
        out[name] = np.zeros((P, 1), np.float32)
        out[name][0:16, 0] = A[name + "_2"][0]
    taps = np.concatenate([A["a_conv_w_2"][0], A["a_conv_b_2"][0][None]]).reshape(5, 16, P)
    out["a_conv"] = np.concatenate(
        [taps[:, t].T for g in range(4) for t in (2 * g, 2 * g + 1, 8 + g, 12 + g)], axis=1)
    taps = np.concatenate([A["a_dw_w_2"][0], A["a_dw_b_2"][0][None]]).reshape(32, KD, P)
    out["a_dw"] = np.concatenate([taps[:, t].T for t in range(KD)], axis=1)
    out["a_d_skip"] = columns(np.repeat(A["a_d_skip_2"][0], 64))
    for name in ("a_ssd_norm_w", "a_ln_w", "a_ln_b"):
        out[name] = columns(A[name + "_2"][0])
    for name in ("gdn_dt_bias", "gdn_a_log"):
        out[name] = np.zeros((P, 1), np.float32)
        out[name][32:40, 0] = A[name][0]
    return out


PARAMS = {}


def lay_out_parameters(A):
    at, parts = 0, small_parameters(A)
    for name, v in parts.items():
        PARAMS[name] = (at, at + v.shape[1])
        at += v.shape[1]
    PARAMS["end"] = (at, at)
    return np.concatenate(list(parts.values()), axis=1)


LAYERS = ("load", "pool", "gdn", "mla", "pool", "even", "odd", "store")
BIASES = (EPS, EPS * 128, math.pi / 2, 1e-5)
GDN_MASKS = ("upper", "-strict lower", "blocks 16", "join 16", "join 32", "join 64")


def constants():
    p, x = np.arange(P)[:, None], np.arange(P)[None, :]
    c = {"identity": p == x, "ones": p + x >= 0, "upper": x >= p, "-strict lower": -1.0 * (x < p),
         "blocks 16": p // 16 == x // 16}
    for s in (16, 32, 64):
        c[f"join {s}"] = (p // (2 * s) == x // (2 * s)) & (p // s % 2 == 0) & (x // s % 2 == 1)
    rot = np.zeros((P, P), np.float32)
    for m in range(P):
        if m % 64 < 32:
            rot[m + 32, m] = -1.0
        else:
            rot[m - 32, m] = 1.0
    orot = np.zeros((P, P), np.float32)
    for m in range(P):
        if m % 64 < 8:
            orot[m + 8, m] = -1.0
        elif m % 64 < 16:
            orot[m - 8, m] = 1.0
    t = np.arange(SEQ)
    rcnt = np.stack([1.0 / np.minimum(t + 1, w) for w in WINDOWS]).astype(np.float32)
    odd_masks = [orot, np.where((x >= 64) & (p < 64), NEG, 0.0), p // 64 == x // 64]
    return {"odd_masks": np.concatenate([m.astype(np.float32) for m in odd_masks], axis=1),
            "mla_masks": np.concatenate([rot, np.where(x > p, NEG, 0.0).astype(np.float32)], axis=1),
            "consts": np.concatenate([c[k].astype(np.float32) for k in ("identity", "ones")], axis=1),
            "gdn_masks": np.concatenate([c[k].astype(np.float32) for k in GDN_MASKS], axis=1),
            "rcnt": np.ascontiguousarray(np.broadcast_to(rcnt.reshape(1, -1), (P, 4 * SEQ)))}


def kernel(**inputs):
    from concourse import bacc, mybir
    from concourse.bass_utils import run_bass_kernel_spmd

    A = {name: np.asarray(a) for name, a in inputs.items()}
    arrays = {"x": A["x"], "positions": A["positions"], "positions_2": A["positions_2"],
              "weights": lay_out_weights(LAYERS, A), "params": lay_out_parameters(A), **constants()}
    arrays = {name: np.ascontiguousarray(a) for name, a in arrays.items()}
    counts = {}
    for _ in range(2):
        nc = bacc.Bacc("TRN2", target_bir_lowering=False, num_devices=1)
        T = {name: nc.dram_tensor(f"{name}_dram", a.shape, mybir.dt.from_np(a.dtype), kind="ExternalInput").ap()
             for name, a in arrays.items()}
        out = nc.dram_tensor("out_dram", (1, SEQ, D), mybir.dt.float32, kind="ExternalOutput").ap()
        program(nc, T, out, counts, LAYERS)
    r = run_bass_kernel_spmd(nc, [{f"{name}_dram": a for name, a in arrays.items()}], core_ids=[0])
    return r.results[0]["out_dram"]
```
